# Optimizing a Trainium2 kernel written in Bass

```python
import jax, jax.numpy as jnp
from jax import lax
import numpy as np

D_MODEL = 1024
BATCH = 1
SEQ = 256
DEPTH = 1
DEC_BATCH = 8
DEC_SEQ = 8
PAST_LEN = 2048
PAGE_SIZE = 128

GDN_HEADS = 8
GDN_DK = 128
GDN_DV = 128
GDN_QK = GDN_HEADS * GDN_DK
GDN_VW = GDN_HEADS * GDN_DV
QKV_W = 2 * GDN_QK + GDN_VW
GDN_CONV = 4
GDN_CHUNK = 64
SC_WIDTH = D_MODEL
SC_CONV = 3
N_EXPERTS = 32
TOP_K = 4
D_EXPERT = D_MODEL
SWIGLU_LIMIT = 7.0
SWIGLU_ALPHA = 1.702
MOE_BLOCK = 128
NORM_EPS = 1e-6
IN_SIZES = (QKV_W, GDN_VW, GDN_HEADS, GDN_HEADS, SC_WIDTH, SC_WIDTH, SC_WIDTH, D_MODEL, D_MODEL)
IN_WIDTH = 2 * GDN_QK + 2 * GDN_VW + 2 * GDN_HEADS + 3 * SC_WIDTH + 2 * D_MODEL

kernel_name = "hybrid_gdn_shortconv_moe_adaln_step"

def rms_norm(x, w):
    xf = x.astype(jnp.float32)
    y = xf * lax.rsqrt(jnp.mean(xf * xf, axis=-1, keepdims=True) + NORM_EPS)
    return (y * w.astype(jnp.float32)).astype(x.dtype)

def l2_norm(x):
    return x * lax.rsqrt(jnp.sum(x * x, axis=-1, keepdims=True) + 1e-6)

def causal_dwconv(x_ext, w):
    ch = w.shape[1]
    return lax.conv_general_dilated(x_ext, w[:, None, :].astype(x_ext.dtype), window_strides=(1,),
                                    padding='VALID', dimension_numbers=('NWC', 'WIO', 'NWC'),
                                    feature_group_count=ch)

def split_cols(a, sizes):
    out, off = [], 0
    for s in sizes:
        out.append(a[..., off:off + s])
        off += s
    return out

def gated_delta_chunked(q, k, v, beta, g, s0):
    Bn, T, H, DK = q.shape
    C = min(GDN_CHUNK, T)
    n = -(-T // C)
    pad = n * C - T
    if pad:
        pw = ((0, 0), (0, pad), (0, 0), (0, 0))
        q, k, v = jnp.pad(q, pw), jnp.pad(k, pw), jnp.pad(v, pw)
        beta, g = jnp.pad(beta, pw[:3]), jnp.pad(g, pw[:3])

    def to_chunks(a):
        a = a.reshape((Bn, n, C) + a.shape[2:])
        return jnp.moveaxis(a, (1, 3), (0, 2))

    qc, kc, vc = to_chunks(q), to_chunks(k), to_chunks(v)
    bc, gc = to_chunks(beta), to_chunks(g)
    dec = jnp.cumsum(gc, axis=-1)
    idx = jnp.arange(C)
    causal = idx[:, None] >= idx[None, :]
    strict = idx[:, None] > idx[None, :]
    decay_mat = jnp.exp(jnp.where(causal, dec[..., :, None] - dec[..., None, :], -jnp.inf))
    kk = jnp.einsum('nbhid,nbhjd->nbhij', kc, kc)
    a_mat = jnp.where(strict, bc[..., :, None] * kk * decay_mat, 0.0)
    lhs = a_mat + jnp.eye(C, dtype=jnp.float32)
    u_v = lax.linalg.triangular_solve(lhs, bc[..., None] * vc, left_side=True, lower=True,
                                      unit_diagonal=True)
    w_k = lax.linalg.triangular_solve(lhs, (bc * jnp.exp(dec))[..., None] * kc, left_side=True,
                                      lower=True, unit_diagonal=True)
    qk = jnp.einsum('nbhid,nbhjd->nbhij', qc, kc) * decay_mat
    q_dec = qc * jnp.exp(dec)[..., None]
    k_tail = kc * jnp.exp(dec[..., -1:] - dec)[..., None]
    chunk_decay = jnp.exp(dec[..., -1])

    def step(S, xs):
        uv, wk, qkm, qd, kt, cd = xs
        u = uv - jnp.einsum('bhcd,bhde->bhce', wk, S)
        o = jnp.einsum('bhcd,bhde->bhce', qd, S) + jnp.einsum('bhij,bhje->bhie', qkm, u)
        S = S * cd[..., None, None] + jnp.einsum('bhcd,bhce->bhde', kt, u)
        return S, o

    s_final, o = lax.scan(step, s0, (u_v, w_k, qk, q_dec, k_tail, chunk_decay))
    o = jnp.transpose(o, (1, 0, 3, 2, 4)).reshape(Bn, n * C, H, o.shape[-1])[:, :T]
    return o, s_final

def moe_ffn(xf, w_router, b_router, w_gate, b_gate, w_up, b_up, w_down, b_down):
    N, D = xf.shape
    logits = xf.astype(jnp.float32) @ w_router.astype(jnp.float32) + b_router.astype(jnp.float32)
    top_val, top_idx = lax.top_k(logits, TOP_K)
    top_w = jax.nn.softmax(top_val, axis=-1)
    M = N * TOP_K
    flat_e = top_idx.reshape(M).astype(jnp.int32)
    flat_tok = jnp.arange(M, dtype=jnp.int32) // TOP_K
    order = jnp.argsort(flat_e, stable=True)
    e_sorted, tok_sorted = flat_e[order], flat_tok[order]
    w_sorted = top_w.reshape(M)[order]
    counts = jnp.zeros((N_EXPERTS,), jnp.int32).at[flat_e].add(1)
    padded = (counts + MOE_BLOCK - 1) // MOE_BLOCK * MOE_BLOCK
    pad_end = jnp.cumsum(padded)
    pad_start = pad_end - padded
    start = jnp.cumsum(counts) - counts
    dest = pad_start[e_sorted] + jnp.arange(M, dtype=jnp.int32) - start[e_sorted]
    n_blocks = -(-M // MOE_BLOCK) + N_EXPERTS
    buf = jnp.zeros((n_blocks * MOE_BLOCK, D), xf.dtype).at[dest].set(xf[tok_sorted])
    block_e = jnp.minimum(jnp.searchsorted(pad_end, jnp.arange(n_blocks, dtype=jnp.int32) * MOE_BLOCK,
                                           side='right'), N_EXPERTS - 1).astype(jnp.int32)

    def expert_block(args):
        xb, e = args
        gate = xb @ w_gate[e] + b_gate[e]
        up = xb @ w_up[e] + b_up[e]
        gate = jnp.minimum(gate, SWIGLU_LIMIT)
        up = jnp.clip(up, -SWIGLU_LIMIT, SWIGLU_LIMIT)
        glu = gate * jax.nn.sigmoid(SWIGLU_ALPHA * gate)
        return ((up + 1.0) * glu) @ w_down[e] + b_down[e]

    out = lax.map(expert_block, (buf.reshape(n_blocks, MOE_BLOCK, D), block_e))
    rows = out.reshape(n_blocks * MOE_BLOCK, D)[dest]
    y = jnp.zeros((N, D), jnp.float32).at[tok_sorted].add(rows.astype(jnp.float32) * w_sorted[:, None])
    return y.astype(xf.dtype)

def hybrid_layer(x, c, conv_state, rec_state, sc_state, w_ada, b_ada, norm1_w, w_in, gdn_conv_w,
                 gdn_a_log, gdn_dt_bias, gdn_norm_w, w_branch_a, sc_conv_w, w_branch_b, w_out,
                 norm2_w, w_router, b_router, w_gate, b_gate, w_up, b_up, w_down, b_down):
    Bn, T, D = x.shape
    dt = x.dtype
    f32 = jnp.float32
    ada = (jax.nn.silu(c) @ w_ada + b_ada)[:, None, :]
    sh1, sc1, g1, sh2, sc2, g2 = jnp.split(ada, 6, axis=-1)
    h = rms_norm(x, norm1_w) * (1 + sc1) + sh1
    proj = h @ w_in
    qkv, z, b_lin, a_lin, sc_b, sc_c, sc_h, gate_a, gate_b = split_cols(proj, IN_SIZES)

    qkv_ext = jnp.concatenate([conv_state.astype(dt), qkv], axis=1)
    new_conv = qkv_ext[:, -(GDN_CONV - 1):]
    qkv_c = jax.nn.silu(causal_dwconv(qkv_ext, gdn_conv_w)).astype(f32)
    q = qkv_c[..., :GDN_QK].reshape(Bn, T, GDN_HEADS, GDN_DK)
    k = qkv_c[..., GDN_QK:2 * GDN_QK].reshape(Bn, T, GDN_HEADS, GDN_DK)
    v = qkv_c[..., 2 * GDN_QK:].reshape(Bn, T, GDN_HEADS, GDN_DV)
    q = l2_norm(q) * (GDN_DK ** -0.5)
    k = l2_norm(k)
    beta = jax.nn.sigmoid(b_lin.astype(f32))
    g = -jnp.exp(gdn_a_log.astype(f32)) * jax.nn.softplus(a_lin.astype(f32) + gdn_dt_bias.astype(f32))
    o, new_rec = gated_delta_chunked(q, k, v, beta, g, rec_state.astype(f32))
    o = o * lax.rsqrt(jnp.mean(o * o, axis=-1, keepdims=True) + NORM_EPS) * gdn_norm_w.astype(f32)
    o = o * jax.nn.silu(z.astype(f32).reshape(Bn, T, GDN_HEADS, GDN_DV))
    y_a = o.reshape(Bn, T, GDN_VW).astype(dt) @ w_branch_a

    pre = sc_c * sc_h
    pre_ext = jnp.concatenate([sc_state.astype(dt), pre], axis=1)
    new_sc = pre_ext[:, -(SC_CONV - 1):]
    y_b = (sc_b * causal_dwconv(pre_ext, sc_conv_w)) @ w_branch_b

    merged = jax.nn.sigmoid(gate_a) * y_a + jax.nn.sigmoid(gate_b) * y_b
    x = x + g1 * (merged @ w_out)

    h2 = rms_norm(x, norm2_w) * (1 + sc2) + sh2
    ffn = moe_ffn(h2.reshape(Bn * T, D), w_router, b_router, w_gate, b_gate, w_up, b_up, w_down, b_down)
    x = x + g2 * ffn.reshape(Bn, T, D)
    return x, new_conv.astype(conv_state.dtype), new_rec.astype(rec_state.dtype), new_sc.astype(sc_state.dtype)

def setup_inputs(seed: int = 0) -> dict:
    key = jax.random.key(seed)
    ks = jax.random.split(key, 40)
    f32 = jnp.float32

    def nrm(k, shape, scale):
        return jax.random.normal(k, shape, f32) * scale

    L, D, E, F = DEPTH, D_MODEL, N_EXPERTS, D_EXPERT
    dt0 = jnp.exp(jax.random.uniform(ks[11], (L, GDN_HEADS), f32, np.log(0.001), np.log(0.1)))
    return {
        'x_prompt': nrm(ks[0], (BATCH, SEQ, D), 1.0),
        'x_sample': nrm(ks[1], (DEC_BATCH, DEC_SEQ, D), 1.0),
        'c_prompt': nrm(ks[2], (BATCH, D), 1.0),
        'c_sample': nrm(ks[3], (DEC_BATCH, D), 1.0),
        'state_gdn_conv': nrm(ks[4], (L, DEC_BATCH, GDN_CONV - 1, QKV_W), 1.0),
        'state_gdn_rec': nrm(ks[5], (L, DEC_BATCH, GDN_HEADS, GDN_DK, GDN_DV), 0.1),
        'state_sc_conv': nrm(ks[6], (L, DEC_BATCH, SC_CONV - 1, SC_WIDTH), 1.0),
        'w_ada': nrm(ks[7], (L, D, 6 * D), D ** -0.5),
        'b_ada': nrm(ks[8], (L, 6 * D), 0.02),
        'norm1_w': 1.0 + nrm(ks[9], (L, D), 0.02),
        'w_in': nrm(ks[10], (L, D, IN_WIDTH), D ** -0.5),
        'gdn_conv_w': nrm(ks[12], (L, GDN_CONV, QKV_W), GDN_CONV ** -0.5),
        'gdn_a_log': jnp.log(jax.random.uniform(ks[13], (L, GDN_HEADS), f32, 1.0, 16.0)),
        'gdn_dt_bias': dt0 + jnp.log(-jnp.expm1(-dt0)),
        'gdn_norm_w': 1.0 + nrm(ks[14], (L, GDN_DV), 0.02),
        'w_branch_a': nrm(ks[15], (L, GDN_VW, D), GDN_VW ** -0.5),
        'sc_conv_w': nrm(ks[16], (L, SC_CONV, SC_WIDTH), SC_CONV ** -0.5),
        'w_branch_b': nrm(ks[17], (L, SC_WIDTH, D), SC_WIDTH ** -0.5),
        'w_out': nrm(ks[18], (L, D, D), D ** -0.5),
        'norm2_w': 1.0 + nrm(ks[19], (L, D), 0.02),
        'w_router': nrm(ks[20], (L, D, E), D ** -0.5),
        'b_router': nrm(ks[21], (L, E), 0.01),
        'w_gate': nrm(ks[22], (L, E, D, F), D ** -0.5),
        'b_gate': nrm(ks[23], (L, E, F), 0.02),
        'w_up': nrm(ks[24], (L, E, D, F), D ** -0.5),
        'b_up': nrm(ks[25], (L, E, F), 0.02),
        'w_down': nrm(ks[26], (L, E, F, D), F ** -0.5),
        'b_down': nrm(ks[27], (L, E, D), 0.02),
        'final_norm_w': 1.0 + nrm(ks[28], (D,), 0.02),
    }

def reference(x_prompt, x_sample, c_prompt, c_sample, state_gdn_conv, state_gdn_rec, state_sc_conv,
              w_ada, b_ada, norm1_w, w_in, gdn_conv_w, gdn_a_log, gdn_dt_bias, gdn_norm_w, w_branch_a,
              sc_conv_w, w_branch_b, w_out, norm2_w, w_router, b_router, w_gate, b_gate, w_up, b_up,
              w_down, b_down, final_norm_w):
    bp = x_prompt.shape[0]
    zero_conv = jnp.zeros((bp, GDN_CONV - 1, QKV_W), state_gdn_conv.dtype)
    zero_rec = jnp.zeros((bp, GDN_HEADS, GDN_DK, GDN_DV), state_gdn_rec.dtype)
    zero_sc = jnp.zeros((bp, SC_CONV - 1, SC_WIDTH), state_sc_conv.dtype)
    xp, xs = x_prompt, x_sample
    pc, pr, ps, sc_, sr, ss = [], [], [], [], [], []
    for l in range(DEPTH):
        lp = (w_ada[l], b_ada[l], norm1_w[l], w_in[l], gdn_conv_w[l], gdn_a_log[l], gdn_dt_bias[l],
              gdn_norm_w[l], w_branch_a[l], sc_conv_w[l], w_branch_b[l], w_out[l], norm2_w[l],
              w_router[l], b_router[l], w_gate[l], b_gate[l], w_up[l], b_up[l], w_down[l], b_down[l])
        xp, c1, r1, s1 = hybrid_layer(xp, c_prompt, zero_conv, zero_rec, zero_sc, *lp)
        xs, c2, r2, s2 = hybrid_layer(xs, c_sample, state_gdn_conv[l], state_gdn_rec[l], state_sc_conv[l], *lp)
        pc.append(c1); pr.append(r1); ps.append(s1)
        sc_.append(c2); sr.append(r2); ss.append(s2)
    y_prompt = rms_norm(xp, final_norm_w)
    y_sample = rms_norm(xs, final_norm_w)
    return (y_prompt, y_sample, jnp.stack(pc), jnp.stack(pr), jnp.stack(ps),
            jnp.stack(sc_), jnp.stack(sr), jnp.stack(ss))


_drawn_inputs = setup_inputs


def setup_inputs(seed=0):
    import zlib

    import numpy as np

    out = dict(_drawn_inputs(seed))
    spreads = {}
    factors = {'b_router': 5.297,
     'b_gate': 8.0,
     'b_up': 8.0,
     'b_down': 8.0,
     'final_norm_w': 7.631,
     'gdn_norm_w': 3.2}
    for name, (base, spread) in spreads.items():
        noise = np.random.default_rng([zlib.crc32(name.encode()), seed]).standard_normal(out[name].shape)
        drawn = base * np.exp(spread * noise) if base else spread * noise
        out[name] = __import__('jax').numpy.asarray(drawn.astype(out[name].dtype))
    for name, factor in factors.items():
        out[name] = (out[name] * factor).astype(out[name].dtype)
    return out
```

```python
from contextlib import ExitStack

import concourse.bass as bass
from concourse import mybir

F32 = mybir.dt.float32
I32 = mybir.dt.int32
ALU = mybir.AluOpType
ACT = mybir.ActivationFunctionType
AX = mybir.AxisListType

P = 128
D = 1024
NC = D // P
SEQ = 256
NS = 8
ST = 8
T = SEQ + NS * ST
H = 8
QKV = 3 * D
E = 32
TOPK = 4
NSEQ = 1 + NS
EPS = 1e-6
LIMIT = 7.0
ALPHA = 1.702
NTILE = 3
TILE = [(0, 128), (128, 128), (256, 64)]
KW = 4
EXT = SEQ + KW - 1
SEXT = ST + KW - 1
EW = EXT + NS * SEXT
SW = 3
PEXT = SEQ + SW - 1
PSEXT = ST + SW - 1
PW = PEXT + NS * PSEXT
TAILS = 3 * NSEQ
PTAILS = 2 * NSEQ
HALF = 512
RING = 6
RING1 = 4
C_AB, C_B, C_C, C_H, C_GA, C_GB = 4096, 4112, 5136, 6160, 7184, 8208
LEVELS = 7
SLEVELS = 3
CAP = 128
NARROW = 64

ADA1 = [("ada", n * HALF) for n in range(4)]
QKVS = [("in", c * HALF) for c in (2, 3, 0, 1, 4, 5)]
ZS = [("in", 3072), ("in", 3584)]
ADA2 = [("ada", n * HALF) for n in range(4, 12)]
HS = [("in", C_H), ("in", C_H + HALF)]
CS = [("in", C_C), ("in", C_C + HALF)]
BS = [("in", C_B), ("in", C_B + HALF)]
GBS = [("in", C_GB), ("in", C_GB + HALF)]
WBS = [("wb", 0), ("wb", HALF)]
GAS = [("in", C_GA), ("in", C_GA + HALF)]
WAS = [("wa", 0), ("wa", HALF)]
WOS = [("wo", 0), ("wo", HALF)]
SLOTS = ADA1 + QKVS + ZS + ADA2 + HS + CS + BS + GBS + WBS + GAS + WAS + WOS
S_QKV, S_Z = 4, 10
S_ADA2 = 12
S_H = 20
NSLOT1 = len(SLOTS)
assert NSLOT1 == 36 and NSLOT1 % RING1 == 0


class Order:

    def __init__(self, semaphore):
        self.semaphore, self.count = semaphore, 0

    def link(self, engine, instruction):
        self.count += 1
        instruction.then_inc(self.semaphore, 1)
        engine.wait_ge(self.semaphore, self.count)


def build(nc, t, stop=9, dbg=None):
    dbg = dbg or {}
    with ExitStack() as top:
        def sb(name, shape, stack=top, dt=F32):
            return stack.enter_context(nc.sbuf_tensor(name, shape, dt))

        sems = {}

        def sem(name):
            if name not in sems:
                sems[name] = top.enter_context(nc.semaphore(name))
            return sems[name]

        order = Order(sem("vector_order"))
        norm = [sem("norm_" + x) for x in ("square", "sum", "mean", "log", "rstd")]
        ring = sb("ring", [P, RING, NC, HALF])
        states = ring[:, RING1:RING].rearrange("p r c n -> p (r c n)").rearrange(
            "p (h s v) -> p h s v", h=H, s=NS)
        ident = sb("ident", [P, P])
        ones = sb("ones", [P, P])
        causal = sb("causal", [P, P])
        scausal = sb("scausal", [64, 64])
        sblock = sb("sblock", [64, NS])
        ssame = sb("ssame", [64, 64])
        vecs = sb("vecs", [P, 193])
        adaT = sb("adaT", [P, 48, NSEQ])
        biasT = sb("biasT", [P, 3, NC, E])
        work = sb("work", [P, 6 * 1024])
        gbuf = work[:].rearrange("p (k a n) -> p k a n", k=6, a=2)
        x2T = work[:, 0:NC * T].rearrange("p (c t) -> p c t", c=NC)
        rows_of = work[:, NC * T:NC * T + NTILE * D].rearrange("p (a d) -> p a d", a=NTILE)
        slot_full = [sem(f"slot_full{r}") for r in range(RING)]
        ada_t, raw_t, z_t, ada2_t, unit_t, st_out = (sem(x) for x in (
            "ada_t", "raw_t", "z_t", "ada2_t", "unit_t", "st_out"))

        n1w = vecs[:, 0:8]
        n2w = vecs[:, 8:16]
        nfw = vecs[:, 16:24]
        gnw = vecs[:, 24:25]
        convw = vecs[:, 25:121].rearrange("p (j c) -> p j c", j=KW)
        scw = vecs[:, 121:145].rearrange("p (j c) -> p j c", j=SW)
        bada = vecs[:, 145:193]
        A_SH1, A_SC1, A_G1, A_SH2, A_SC2, A_G2 = (adaT[:, 8 * n:8 * n + 8, :] for n in range(6))

        w_in = t["w_in"][0]
        dram = {"ada": t["w_ada"][0], "in": w_in, "wb": t["w_branch_b"][0], "wa": t["w_branch_a"][0],
                "wo": t["w_out"][0]}

        def slot_done(i):
            if i < S_QKV:
                return ada_t, i + 1
            if i < S_Z:
                return raw_t, 4 * (i - S_QKV + 1)
            if i < S_ADA2:
                return z_t, 4 * (i - S_Z + 1)
            if i < S_H:
                return ada2_t, i - S_ADA2 + 1
            return unit_t, 4 * (i - S_H + 1)

        def load_slot(sp, i):
            kind, n0 = SLOTS[i]
            r = i % RING1
            if i >= RING1:
                sp.wait_ge(*slot_done(i - RING1))
            src = dram[kind][:, n0:n0 + HALF].rearrange("(c p) n -> p c n", p=P)
            sp.dma_start(ring[:, r], src).then_inc(slot_full[r], 16)

        def load_expert_half(sp, e, j):
            name = ("w_gate", "w_up", "w_down")[j // 2]
            src = t[name][0, e, :, HALF * (j % 2):HALF * (j % 2) + HALF].rearrange("(c p) n -> p c n", p=P)
            sp.dma_start(ring[:, j], src).then_inc(slot_full[j], 16)

        def wait_slot(pe, i):
            pe.wait_ge(slot_full[i % RING1], 16 * (i // RING1 + 1))

        with ExitStack() as st12:
            hT = sb("hT", [P, NC, T], st12)
            cT = sb("cT", [P, NC, NSEQ], st12)
            gst = sb("gst", [P, 3 * NC, 3 * NS], st12)
            sst = sb("sst", [P, NC, 2 * NS], st12)
            with ExitStack() as st:
                ps = st.enter_context(nc.psum_tensor("ps_pro", [P, 8, 512], F32))
                xrow = sb("xrow", [P, NTILE, D], st)
                crow = sb("crow", [NSEQ, D], st)
                vrow1 = sb("vrow1", [121, P], st)
                vrow2 = sb("vrow2", [72, P], st)
                brow = sb("brow", [E, 3, D], st)
                gstrow = sb("gstrow", [3 * NS, QKV], st)
                sstrow = sb("sstrow", [2 * NS, D], st)
                xT = sb("xT", [P, NC, T], st)
                sq = sb("sq", [P, 2, T], st)
                rstd = sb("rstd", [P, T], st)
                gw = sb("gw", [P, NC, NSEQ], st)
                ld_c, ld_v, ld_x, ld_b, ld_s = (sem(f"ld_{n}") for n in "cvxbs")
                k_ones, k_ident, k_masks = sem("k_ones"), sem("k_ident"), sem("k_masks")
                silu_c, vec_t, vec_s, c_sb = sem("silu_c"), sem("vec_t"), sem("vec_s"), sem("c_sb")
                bias_t, bias_s, st_t, st_s = sem("bias_t"), sem("bias_s"), sem("st_t"), sem("st_s")
                x_t, x_s = sem("x_t"), sem("x_s")
                sq_s, sum_t, mean_s, log_s, rstd_s = norm
                block = st.enter_context(nc.Block())

                @block.sync
                def _(sp):
                    for i in range(6):
                        load_slot(sp, i)

                @block.gpsimd
                def _(pool):
                    nc.gpsimd.memset(ones[:], 1.0).then_inc(k_ones, 1)
                    nc.gpsimd.memset(ident[:], 0.0).then_inc(k_ones, 1)
                    nc.gpsimd.memset(causal[:], 1.0).then_inc(k_ones, 1)
                    nc.gpsimd.memset(sblock[:], 1.0).then_inc(k_ones, 1)
                    pool.wait_ge(k_ones, 4)
                    nc.gpsimd.affine_select(out=ident[:], in_=ident[:], compare_op=ALU.not_equal, fill=1.0,
                                            base=0, pattern=[[-1, P]], channel_multiplier=1).then_inc(k_ident, 1)
                    nc.gpsimd.affine_select(out=causal[:], in_=causal[:], compare_op=ALU.is_ge, fill=0.0,
                                            base=0, pattern=[[1, P]], channel_multiplier=-1).then_inc(k_masks, 1)
                    nc.gpsimd.affine_select(out=sblock[:], in_=sblock[:], compare_op=ALU.is_ge, fill=0.0,
                                            base=0, pattern=[[-ST, NS]], channel_multiplier=1).then_inc(k_masks, 1)
                    pool.wait_ge(k_masks, 2)
                    nc.gpsimd.affine_select(out=sblock[:], in_=sblock[:], compare_op=ALU.is_ge, fill=0.0,
                                            base=ST - 1, pattern=[[ST, NS]], channel_multiplier=-1).then_inc(k_masks, 1)
                    pool.wait_ge(k_masks, 3)
                    nc.gpsimd.tensor_copy(ssame[:].rearrange("p (s t) -> p s t", s=NS),
                                          sblock[:].unsqueeze(2).to_broadcast([64, NS, ST])).then_inc(k_masks, 1)
                    pool.wait_ge(k_masks, 4)
                    nc.gpsimd.tensor_tensor(scausal[:], ssame[:], causal[0:64, 0:64], ALU.mult).then_inc(k_masks, 1)

                @block.scalar
                def _(act):
                    act.dma_start(crow[0:1, :], t["c_prompt"]).then_inc(ld_c, 16)
                    act.dma_start(crow[1:NSEQ, :], t["c_sample"]).then_inc(ld_c, 16)
                    for tau in range(2):
                        act.dma_start(xrow[:, tau, :], t["x_prompt"][0, P * tau:P * tau + P, :]).then_inc(ld_x, 16)
                    act.dma_start(xrow[0:64, 2, :], t["x_sample"].rearrange("s t d -> (s t) d")).then_inc(ld_x, 16)
                    rows = lambda a: a.rearrange("a (c p) -> (a c) p", p=P)
                    act.dma_start(vrow1[0:8, :], rows(t["norm1_w"])).then_inc(ld_v, 16)
                    act.dma_start(vrow1[8:16, :], rows(t["norm2_w"])).then_inc(ld_v, 16)
                    act.dma_start(vrow1[16:24, :], t["final_norm_w"].rearrange("(c p) -> c p", p=P)).then_inc(ld_v, 16)
                    act.dma_start(vrow1[24:25, :], t["gdn_norm_w"]).then_inc(ld_v, 16)
                    act.dma_start(vrow1[25:121, :], rows(t["gdn_conv_w"][0])).then_inc(ld_v, 16)
                    act.dma_start(vrow2[0:24, :], rows(t["sc_conv_w"][0])).then_inc(ld_v, 16)
                    act.dma_start(vrow2[24:72, :], rows(t["b_ada"])).then_inc(ld_v, 16)
                    act.dma_start(gstrow[:], t["state_gdn_conv"][0].rearrange("s j c -> (s j) c")).then_inc(ld_s, 16)
                    act.dma_start(sstrow[:], t["state_sc_conv"][0].rearrange("s j c -> (s j) c")).then_inc(ld_s, 16)
                    for n, name in enumerate(("b_gate", "b_up", "b_down")):
                        act.dma_start(brow[:, n, :], t[name][0]).then_inc(ld_b, 16)
                    act.wait_ge(ld_c, 32)
                    nc.scalar.activation(crow[:], crow[:], ACT.Silu).then_inc(silu_c, 1)
                    for c in range(NC):
                        act.wait_ge(x_t, c + 1)
                        if c >= 2:
                            act.wait_ge(sum_t, c - 1)
                        nc.scalar.activation(xT[:, c, :], ps[:, 3 + c % 4, 0:T], ACT.Copy).then_inc(x_s, 1)
                        nc.scalar.activation(sq[:, c % 2, :], ps[:, 3 + c % 4, 0:T], ACT.Square).then_inc(sq_s, 1)
                    act.wait_ge(mean_s, 1)
                    nc.scalar.activation(rstd[:], rstd[:], ACT.Ln).then_inc(log_s, 1)
                    act.wait_ge(log_s, 1)
                    nc.scalar.activation(rstd[:], rstd[:], ACT.Exp, scale=-0.5).then_inc(rstd_s, 1)

                @block.tensor
                def _(pe):
                    pe.wait_ge(k_ident, 1)
                    pe.wait_ge(ld_v, 7 * 16)
                    nc.tensor.transpose(ps[:, 0, 0:121], vrow1[:], ident[0:121, 0:121])
                    nc.tensor.transpose(ps[:, 0, 121:193], vrow2[:], ident[0:72, 0:72]).then_inc(vec_t, 1)
                    pe.wait_ge(silu_c, 1)
                    for c in range(NC):
                        last = nc.tensor.transpose(ps[:, 0, 256 + NSEQ * c:256 + NSEQ * c + NSEQ],
                                                   crow[:, P * c:P * c + P], ident[0:NSEQ, 0:NSEQ])
                    last.then_inc(vec_t, 1)
                    pe.wait_ge(ld_x, 48)
                    pe.wait_ge(k_ones, 4)

                    def add_square(c):
                        pe.wait_ge(sq_s, c + 1)
                        nc.tensor.matmul(ps[:, 7, 0:T], ones[:], sq[:, c % 2, :], start=c == 0,
                                         stop=c == NC - 1).then_inc(sum_t, 1)

                    for c in range(NC):
                        if c >= 4:
                            pe.wait_ge(sq_s, c - 3)
                        for tau, (t0, n) in enumerate(TILE):
                            last = nc.tensor.transpose(ps[:, 3 + c % 4, t0:t0 + n], xrow[0:n, tau, P * c:P * c + P],
                                                       ident[0:n, 0:n])
                        last.then_inc(x_t, 1)
                        if c >= 1:
                            add_square(c - 1)
                    add_square(NC - 1)
                    pe.wait_ge(ld_b, 48)
                    for n in range(3):
                        for c in range(NC):
                            k = n * NC + c
                            last = nc.tensor.transpose(ps[:, 1 + k // 16, 32 * (k % 16):32 * (k % 16) + E],
                                                       brow[:, n, P * c:P * c + P], ident[0:E, 0:E])
                    last.then_inc(bias_t, 1)
                    pe.wait_ge(ld_s, 32)
                    pe.wait_ge(sq_s, NC)
                    for c in range(3 * NC):
                        nc.tensor.transpose(ps[:, 3 + c // 16, 24 * (c % 16):24 * (c % 16) + 24],
                                            gstrow[:, P * c:P * c + P], ident[0:24, 0:24])
                    for c in range(NC):
                        last = nc.tensor.transpose(ps[:, 4, 384 + 16 * c:400 + 16 * c], sstrow[:, P * c:P * c + P],
                                                   ident[0:16, 0:16])
                    last.then_inc(st_t, 1)
                    pe.wait_ge(c_sb, 1)
                    for i in range(4):
                        wait_slot(pe, i)
                        for j in range(4):
                            o = ps[:, 5, NSEQ * (4 * i + j):NSEQ * (4 * i + j) + NSEQ]
                            for k in range(NC):
                                last = nc.tensor.matmul(o, ring[:, i % RING1, k, P * j:P * j + P], cT[:, k, :],
                                                        start=k == 0, stop=k == NC - 1)
                        last.then_inc(ada_t, 1)

                @block.vector
                def _(dve):
                    def link(ins):
                        order.link(dve, ins)

                    dve.wait_ge(vec_t, 2)
                    nc.vector.tensor_copy(vecs[:], ps[:, 0, 0:193]).then_inc(vec_s, 1)
                    nc.vector.tensor_copy(cT[:].rearrange("p c s -> p (c s)"), ps[:, 0, 256:256 + NC * NSEQ]).then_inc(c_sb, 1)
                    dve.wait_ge(sum_t, NC)
                    nc.vector.tensor_scalar(rstd[:], ps[:, 7, 0:T], 1.0 / D, EPS, ALU.mult, ALU.add).then_inc(mean_s, 1)
                    dve.wait_ge(bias_t, 1)
                    b2 = biasT[:].rearrange("p n c e -> p (n c e)")
                    nc.vector.tensor_copy(b2[:, 0:512], ps[:, 1, :])
                    nc.vector.tensor_copy(b2[:, 512:768], ps[:, 2, 0:256]).then_inc(bias_s, 1)
                    dve.wait_ge(st_t, 1)
                    g2 = gst[:].rearrange("p c j -> p (c j)")
                    nc.vector.tensor_copy(g2[:, 0:384], ps[:, 3, 0:384])
                    nc.vector.tensor_copy(g2[:, 384:576], ps[:, 4, 0:192])
                    nc.vector.tensor_copy(sst[:].rearrange("p c j -> p (c j)"), ps[:, 4, 384:512]).then_inc(st_s, 1)
                    dve.wait_ge(rstd_s, 1)
                    dve.wait_ge(x_s, NC)
                    link(nc.vector.tensor_tensor(xT[:], xT[:], rstd[:].unsqueeze(1).to_broadcast([P, NC, T]), ALU.mult))
                    dve.wait_ge(ada_t, 4)
                    dve.wait_ge(vec_s, 1)
                    link(nc.vector.tensor_tensor(adaT[:, 0:16, :], ps[:, 5, 0:16 * NSEQ].rearrange("p (c s) -> p c s", s=NSEQ),
                                                 bada[:, 0:16].unsqueeze(2).to_broadcast([P, 16, NSEQ]), ALU.add))
                    link(nc.vector.tensor_scalar(gw[:], A_SC1, 1.0, None, ALU.add))
                    link(nc.vector.tensor_tensor(gw[:], gw[:], n1w.unsqueeze(2).to_broadcast([P, NC, NSEQ]), ALU.mult))
                    for c in range(NC):
                        nc.vector.tensor_scalar(hT[:, c, 0:SEQ], xT[:, c, 0:SEQ], gw[:, c, 0:1], A_SH1[:, c, 0:1],
                                                ALU.mult, ALU.add)
                    for c in range(NC):
                        link(nc.vector.tensor_tensor(
                            hT[:, c, SEQ:T].rearrange("p (s t) -> p s t", s=NS),
                            xT[:, c, SEQ:T].rearrange("p (s t) -> p s t", s=NS),
                            gw[:, c, 1:NSEQ].unsqueeze(2).to_broadcast([P, NS, ST]), ALU.mult))
                        nc.vector.tensor_tensor(
                            hT[:, c, SEQ:T].rearrange("p (s t) -> p s t", s=NS),
                            hT[:, c, SEQ:T].rearrange("p (s t) -> p s t", s=NS),
                            A_SH1[:, c, 1:NSEQ].unsqueeze(2).to_broadcast([P, NS, ST]), ALU.add)

            for name, ap in (("hT", hT), ("gst", gst), ("sst", sst), ("biasT", biasT), ("ada1", adaT[:, 0:16, :])):
                if name in dbg:
                    dump(nc, sem("dbg_" + name), dbg[name], ap[:] if name != "ada1" else ap)
            if stop <= 1:
                return

            z_and_o = ExitStack()
            with z_and_o:
                oT = sb("oT", [P, H, T], z_and_o)
                zT = sb("zT", [P, H, T], z_and_o)
                tails = sb("tails", [P, 3 * NC, TAILS], z_and_o)
                with ExitStack() as st:
                    mixer(nc, t, st, sb, sem, ring, states, ident, ones, causal, scausal, sblock, ssame, convw,
                          bada, adaT, hT, cT, gst, oT, zT, tails, gbuf, order, load_slot, wait_slot)
                for name, ap in (("oT", oT), ("zT", zT), ("tails", tails), ("adaT", adaT)):
                    if name in dbg:
                        dump(nc, sem("dbg_" + name), dbg[name], ap[:])
                if stop <= 2:
                    return
                with ExitStack() as st:
                    branches(nc, t, st, sb, sem, ring, ident, scw, gnw, sst, adaT, hT, oT, zT, tails, x2T, rows_of, order,
                             load_slot, wait_slot, load_expert_half)
                if "x2T" in dbg:
                    dump(nc, sem("dbg_x2T"), dbg["x2T"], x2T)
            if stop <= 3:
                return
        experts(nc, t, top, sb, sem, ring, ident, ones, causal, vecs, adaT, biasT, x2T, rows_of, order, norm,
                slot_full, load_expert_half, dbg, stop)



def head_block(buf, tau, h):
    if tau < 2:
        return buf[:, h // 4, P * (h % 4):P * (h % 4) + P]
    return buf[0:64, 0, 64 * h:64 * h + 64]


def head_values(buf, tau, h):
    n = TILE[tau][1]
    return buf[0:n, h // 4, P * (h % 4):P * (h % 4) + P]


def groups(tau):
    return [(0, 2 * tau, range(0, 4), P), (1, 2 * tau + 1, range(4, 8), P)] if tau < 2 else [(0, 4, range(H), 64)]


def levels(tau):
    return LEVELS if tau < 2 else SLEVELS


def level_no(tau, lev, g):
    return 2 * LEVELS * tau + (2 * lev + g if tau < 2 else lev)


def wide_no(tau, lev, g):
    return 2 * (LEVELS - 1) * tau + (2 * (lev - 1) + g if tau < 2 else lev - 1)


GDN_STEPS = [(tau, kind, lev) for tau in range(NTILE) for kind, lev in
             [("tok", 0), ("rows", 0)] + [("level", x) for x in range(levels(tau))] +
             [("state", 0), ("value", 0), ("out", 0), ("turn", 0)]]


def mixer(nc, t, st, sb, sem, ring, states, ident, ones, causal, scausal, sblock, ssame, convw, bada, adaT, hT, cT, gst,
          oT, zT, tails, gbuf, order, load_slot, wait_slot):
    ps = st.enter_context(nc.psum_tensor("ps_mix", [P, 8, 512], F32))
    qkT = sb("qkT", [P, 2, H, T], st)
    ktok = sb("ktok", [P, 2, 512], st)
    vtok = sb("vtok", [P, 2, 512], st)
    nb, mb, tb, xb, wb, qb = (gbuf[:, i] for i in range(6))
    rowsum = gbuf[:, 0:5].rearrange("p a b c -> p (a b c)").rearrange("p (m t) -> p m t", t=T)
    cbuf = sb("cbuf", [P, 2 * EW + 2 * (EW - KW + 1)], st)
    ext = cbuf[:, 0:2 * EW].rearrange("p (a n) -> p a n", a=2)
    acc = cbuf[:, 2 * EW:].rearrange("p (a n) -> p a n", a=2)
    sqb = sb("sqb", [P, 2, T], st)
    S = cbuf[:, 0:1024].rearrange("p (a n) -> p a n", a=2)
    masks = sb("masks", [P, LEVELS, P], st)
    wab = sb("wab", [P, NC, 16], st)
    par = sb("par", [P, 2, H], st)
    ab = sb("ab", [P, NTILE, 16], st)
    earg = sb("earg", [P, NTILE, 16], st)
    beta = sb("beta", [P, NTILE, H], st)
    g = sb("g", [P, NTILE, H], st)
    pos = sb("pos_part", [P, NTILE, H], st)
    dec = sb("dec", [P, NTILE, 3, H], st)
    edec = sb("edec", [P, NTILE, 3, H], st)
    bdec = sb("bdec", [P, NTILE, H], st)
    gm = sb("gm", [64, H, NS], st)
    cds = sb("cds", [P, H, NS], st)
    oss = sb("oss", [P, 2, 4], st)

    (ld_w, ld_st, halo0, halo_s, raw_t, raw_s, tail_s, conv_s, silu_s, sq_s2, ss_t, ss_s, lnn_s, rs_s, nrm_s,
     mask0, mask_s) = (sem(x) for x in (
         "ld_w", "ld_st", "halo0", "halo_s", "raw_t", "raw_s", "tail_s", "conv_s", "qkv_silu_s", "qkv_sq_s", "ss_t",
         "ss_s", "lnn_s", "rs_s", "nrm_s", "mask0", "mask_s"))
    ab_t, ab_arg, ab_exp, ab_ln, g_s, dec_t, dec_s, edec_s, bdec_s = (sem(x) for x in (
        "ab_t", "ab_arg", "ab_exp", "ab_ln", "g_s", "dec_t", "dec_s", "edec_s", "bdec_s"))
    (tok_t, ktok_s, vtok_s, src_s, rows_t, darg_s, dexp_s, n_s, masked, w_t, w_s, tx_t, tx_s, ks_t, kq_t, kq_s, r_s,
     u_t, u_s, o_t, s_t, S_s, oln_s, orr_s, o_s, turn_t, turn_s) = (sem(x) for x in (
         "tok_t", "ktok_s", "vtok_s", "src_s", "rows_t", "darg_s", "dexp_s", "n_s", "masked", "w_t", "w_s", "tx_t",
         "tx_s", "ks_t", "kq_t", "kq_s", "r_s", "u_t", "u_s", "o_t", "s_t", "S_s", "oln_s", "orr_s", "o_s", "turn_t",
         "turn_s"))
    z_t, z_s, ada2_t, ada_s2, um_s, su_t, scaled_s, so_s, st_out = (sem(x) for x in (
        "z_t", "z_s", "ada2_t", "ada_s2", "um_s", "su_t", "scaled_s", "so_s", "st_out"))

    def chan(q):
        return (8 + q, q - 8, q)[q // 8]

    def dest(q):
        return (qkT[:, 1, q % 8], qkT[:, 0, q % 8], oT[:, q % 8])[q // 8]

    fills = [[] for _ in GDN_STEPS]
    units = [("z", m) for m in range(8)] + [("ada", m) for m in range(32)]
    for n, u in enumerate(units):
        fills[n * len(GDN_STEPS) // len(units)].append(u)

    block = st.enter_context(nc.Block())

    @block.sync
    def _(sp):
        for h in range(H):
            sp.dma_start(states[:, h], t["state_gdn_rec"][0, :, h].rearrange("s k v -> k s v")).then_inc(ld_st, 16)
        for i in range(6, 20):
            load_slot(sp, i)
        sp.wait_ge(S_s, 4)
        sp.dma_start(t["rec_prompt"][0, 0].rearrange("h k v -> k h v"),
                     S[:].rearrange("p a n -> p (a n)").rearrange("p (h v) -> p h v", h=H)).then_inc(st_out, 16)
        for h in range(H):
            sp.wait_ge(so_s, h + 1)
            sp.dma_start(t["rec_sample"][0, :, h].rearrange("s k v -> k s v"), states[:, h]).then_inc(st_out, 16)
        for i in range(20, 24):
            load_slot(sp, i)
        sp.wait_ge(st_out, 16 * (1 + H))

    @block.gpsimd
    def _(pool):
        nc.gpsimd.memset(ext[:, :, 0:KW - 1], 0.0).then_inc(halo0, 1)
        nc.gpsimd.memset(masks[:], 0.0).then_inc(mask0, 1)
        pool.wait_ge(mask0, 1)
        k = 0
        for lev in range(LEVELS):
            b = 1 << lev
            v = masks[:, lev].rearrange("p (m z r) -> p m z r", z=2, r=b)[:, :, 1, :]
            nc.gpsimd.memset(v, 1.0).then_inc(mask_s, 1)
            k += 1
            pool.wait_ge(mask_s, k)
            nc.gpsimd.affine_select(out=v, in_=v, compare_op=ALU.is_ge, fill=0.0, base=0,
                                    pattern=[[-2 * b, P // (2 * b)], [0, b]], channel_multiplier=1).then_inc(mask_s, 1)
            k += 1
            pool.wait_ge(mask_s, k)
            nc.gpsimd.affine_select(out=v, in_=v, compare_op=ALU.is_ge, fill=0.0, base=b - 1,
                                    pattern=[[2 * b, P // (2 * b)], [0, b]], channel_multiplier=-1).then_inc(mask_s, 1)
            k += 1
        pool.wait_ge(mask_s, k)
        for q in range(24):
            if q >= 2:
                pool.wait_ge(conv_s, q - 1)
            e = ext[:, q % 2, EXT:EW].rearrange("p (s j) -> p s j", s=NS)
            nc.gpsimd.tensor_copy(e[:, :, 0:KW - 1], gst[:, chan(q)].rearrange("p (s j) -> p s j", s=NS)).then_inc(halo_s, 1)
            pool.wait_ge(raw_s, q + 1)
            nc.gpsimd.tensor_copy(tails[:, chan(q), 0:3], ext[:, q % 2, EXT - 3:EXT])
            nc.gpsimd.tensor_copy(tails[:, chan(q), 3:TAILS].rearrange("p (s j) -> p s j", s=NS),
                                  e[:, :, SEXT - 3:SEXT]).then_inc(tail_s, 1)
        for tau, kind, lev in GDN_STEPS:
            if kind == "level":
                for gr, gi, heads, w in groups(tau):
                    n = TILE[tau][1]
                    pool.wait_ge(n_s, gi + 1)
                    if lev == 1:
                        pool.wait_ge(tx_s, level_no(tau, 0, gr) + 1)
                    if lev >= 2:
                        pool.wait_ge(w_t, level_no(tau, lev - 1, gr) + 1)
                    nc.gpsimd.tensor_tensor(
                        mb[0:n, gr, :].rearrange("p (h i) -> p h i", i=w),
                        nb[0:n, gr, :].rearrange("p (h i) -> p h i", i=w),
                        masks[0:n, lev, 0:w].unsqueeze(1).to_broadcast([n, 512 // w, w]), ALU.mult).then_inc(masked, 1)
            if (tau, kind) == (2, "state"):
                pool.wait_ge(kq_t, 2)
                pool.wait_ge(edec_s, 2)
                for h in range(H):
                    nc.gpsimd.tensor_tensor(states[:, h], states[:, h],
                                            cds[:, h, :].unsqueeze(2).to_broadcast([P, NS, P]), ALU.mult).then_inc(scaled_s, 1)

    @block.scalar
    def _(act):
        act.dma_start(wab[:], t["w_in"][0][:, C_AB:C_AB + 16].rearrange("(c p) n -> p c n", p=P)).then_inc(ld_w, 16)
        act.dma_start(par[:, 0, :], t["gdn_a_log"].to_broadcast([P, H])).then_inc(ld_w, 16)
        act.dma_start(par[:, 1, :], t["gdn_dt_bias"].to_broadcast([P, H])).then_inc(ld_w, 16)

        def silu(q):
            act.wait_ge(conv_s, q + 1)
            a = acc[:, q % 2]
            nc.scalar.activation(dest(q)[:, 0:SEQ], a[:, 0:SEQ], ACT.Silu)
            nc.scalar.activation(dest(q)[:, SEQ:T].rearrange("p (s t) -> p s t", s=NS), sample_cols(a),
                                 ACT.Silu).then_inc(silu_s, 1)
            if q < 16:
                act.wait_ge(silu_s, q + 1)
                if q >= 2:
                    act.wait_ge(ss_t, q - 1)
                nc.scalar.activation(sqb[:, q % 2, :], dest(q), ACT.Square).then_inc(sq_s2, 1)

        for q in range(24):
            act.wait_ge(raw_t, q + 1)
            if q >= 2:
                act.wait_ge(conv_s, q - 1)
                act.wait_ge(tail_s, q - 1)
            nc.scalar.activation(ext[:, q % 2, KW - 1:EXT], ps[:, q % 2, 0:SEQ], ACT.Copy)
            nc.scalar.activation(ext[:, q % 2, EXT:EW].rearrange("p (s j) -> p s j", s=NS)[:, :, KW - 1:SEXT],
                                 ps[:, q % 2, SEQ:T].rearrange("p (s t) -> p s t", s=NS), ACT.Copy).then_inc(raw_s, 1)
            if q >= 1:
                silu(q - 1)
            if q == 18:
                act.wait_ge(ss_s, 16)
                for i in range(2):
                    nc.scalar.activation(rowsum[:, 8 * i:8 * i + 8], rowsum[:, 8 * i:8 * i + 8], ACT.Ln).then_inc(lnn_s, 1)
                for i in range(2):
                    act.wait_ge(lnn_s, i + 1)
                    nc.scalar.activation(rowsum[:, 8 * i:8 * i + 8], rowsum[:, 8 * i:8 * i + 8], ACT.Exp,
                                         scale=-0.5).then_inc(rs_s, 1)
                act.wait_ge(ab_arg, 1)
                nc.scalar.activation(earg[:], earg[:], ACT.Exp)
                nc.scalar.activation(par[:, 0, :], par[:, 0, :], ACT.Exp).then_inc(ab_exp, 1)
                act.wait_ge(ab_exp, 1)
                nc.scalar.activation(ab[:, :, 0:8], earg[:, :, 8:16], ACT.Ln, bias=1.0).then_inc(ab_ln, 1)
        silu(23)
        act.wait_ge(dec_s, 1)
        nc.scalar.activation(edec[:], dec[:], ACT.Exp).then_inc(edec_s, 1)
        nc.scalar.activation(cds[:], ps[:, 7, 128:192].rearrange("p (h s) -> p h s", h=H), ACT.Exp).then_inc(edec_s, 1)

        for n_step, (tau, kind, lev) in enumerate(GDN_STEPS):
            t0, n = TILE[tau]
            if kind == "tok":
                act.wait_ge(tok_t, tau + 1)
                for gr in range(2):
                    nc.scalar.activation(vtok[0:n, gr, :], ps[0:n, 4 + gr, :], ACT.Copy).then_inc(vtok_s, 1)
            if kind == "rows":
                for gr, gi, heads, w in groups(tau):
                    act.wait_ge(darg_s, gi + 1)
                    nc.scalar.activation(tb[0:n, gr, :], xb[0:n, gr, :], ACT.Exp).then_inc(dexp_s, 1)
            if kind == "level" and lev >= 1:
                for gr, gi, heads, w in groups(tau):
                    act.wait_ge(w_t, level_no(tau, lev, gr) + 1)
                    nc.scalar.activation(wb[0:n, gr, :], ps[0:n, 2 + gr, :], ACT.Copy).then_inc(w_s, 1)
            if (tau, kind) == (2, "state"):
                for gr in range(2):
                    act.wait_ge(kq_t, gr + 1)
                    nc.scalar.activation(wb[:, gr, :], ps[:, 2 + gr, :], ACT.Copy).then_inc(kq_s, 1)
            if kind == "value":
                for gr in range(2):
                    act.wait_ge(u_t, 2 * tau + gr + 1)
                    nc.scalar.activation(mb[0:n, gr, :], ps[0:n, u_bank(tau) + gr, :], ACT.Copy).then_inc(u_s, 1)
            if kind == "out":
                for gr in range(2):
                    i = 2 * tau + gr
                    act.wait_ge(oln_s, i + 1)
                    nc.scalar.activation(oss[0:n, gr, :], oss[0:n, gr, :], ACT.Ln).then_inc(orr_s, 1)
                    act.wait_ge(orr_s, 2 * i + 1)
                    nc.scalar.activation(oss[0:n, gr, :], oss[0:n, gr, :], ACT.Exp, scale=-0.5).then_inc(orr_s, 1)
            if kind == "turn":
                for gr in range(2):
                    act.wait_ge(turn_t, 2 * tau + gr + 1)
                    nc.scalar.activation(oT[:, 4 * gr:4 * gr + 4, t0:t0 + n],
                                         ps[:, 6 + gr, 0:4 * n].rearrange("p (h t) -> p h t", h=4), ACT.Copy).then_inc(turn_s, 1)
            for what, m in fills[n_step]:
                if what == "z":
                    act.wait_ge(z_t, m + 1)
                    nc.scalar.activation(zT[:, m], ps[:, 0, 0:T], ACT.Copy).then_inc(z_s, 1)

    @block.tensor
    def _(pe):
        def sums(m):
            pe.wait_ge(sq_s2, m + 1)
            if m >= 2:
                pe.wait_ge(ss_s, m - 1)
            nc.tensor.matmul(ps[:, 2 + m % 2, 0:T], ones[:], sqb[:, m % 2, :], start=True, stop=True).then_inc(ss_t, 1)

        def chunk(i, j, out, rhs):
            for k in range(NC):
                last = nc.tensor.matmul(out, ring[:, i % RING1, k, P * j:P * j + P], rhs[:, k, :],
                                        start=k == 0, stop=k == NC - 1)
            return last

        pe.wait_ge(ld_w, 48)
        for tau, (t0, n) in enumerate(TILE):
            for k in range(NC):
                last = nc.tensor.matmul(ps[0:n, 6, 16 * tau:16 * tau + 16], hT[:, k, t0:t0 + n], wab[:, k, :],
                                        start=k == 0, stop=k == NC - 1)
        last.then_inc(ab_t, 1)
        for q in range(24):
            i, j = S_QKV + q // 4, q % 4
            if j == 0:
                wait_slot(pe, i)
            if q >= 2:
                pe.wait_ge(raw_s, q - 1)
            chunk(i, j, ps[:, q % 2, 0:T], hT).then_inc(raw_t, 1)
            if 3 <= q < 19:
                sums(q - 3)
            if q == 22:
                pe.wait_ge(g_s, 1)
                for tau, (t0, n) in enumerate(TILE):
                    o = ps[0:n, 7, 16 * tau:16 * tau + 16]
                    nc.tensor.matmul(o[:, 0:8], (scausal if tau == 2 else causal)[:], g[0:n, tau, :], start=True, stop=True)
                    nc.tensor.matmul(o[:, 8:16], (ssame if tau == 2 else ones)[:], g[0:n, tau, :], start=True, stop=True)
                nc.tensor.matmul(ps[:, 7, 128:192], ones[0:64, :], gm[:].rearrange("p h s -> p (h s)"),
                                 start=True, stop=True).then_inc(dec_t, 1)

        def tok(tau):
            t0, n = TILE[tau]
            if tau == 0:
                pe.wait_ge(nrm_s, 1)
                pe.wait_ge(silu_s, 24)
            else:
                pe.wait_ge(turn_s, 2 * tau)
                pe.wait_ge(S_s, 2 * tau)
            for src, bank in ((qkT[:, 1], 2), (oT, 4)):
                for h in range(H):
                    last = nc.tensor.transpose(ps[0:n, bank + h // 4, P * (h % 4):P * (h % 4) + P], src[:, h, t0:t0 + n],
                                               ident[:])
            last.then_inc(tok_t, 1)

        def rows(tau):
            t0, n = TILE[tau]
            for gr, gi, heads, w in groups(tau):
                pe.wait_ge(src_s, gi + 1)
                if gr == 0:
                    pe.wait_ge(ktok_s, tau + 1)
                    pe.wait_ge(vtok_s, 2 * tau + 2)
                    pe.wait_ge(nrm_s, 2)
                else:
                    pe.wait_ge(n_s, gi)
                nc.tensor.matmul(ps[0:n, 6, :], ones[0:n, 0:n], nb[0:n, gr, :], start=True, stop=True)
                nc.tensor.matmul(ps[0:n, 7, :], ones[0:n, 0:n], wb[0:n, gr, :], start=True, stop=True)
                for x, h in enumerate(heads):
                    nc.tensor.matmul(ps[0:n, 2 + 2 * gr, w * x:w * x + w], qkT[:, 1, h, t0:t0 + n],
                                     qkT[:, 1, h, t0:t0 + n], start=True, stop=True)
                for x, h in enumerate(heads):
                    last = nc.tensor.matmul(ps[0:n, 3 + 2 * gr, w * x:w * x + w], qkT[:, 1, h, t0:t0 + n],
                                            qkT[:, 0, h, t0:t0 + n], start=True, stop=True)
                last.then_inc(rows_t, 1)

        def level(tau, lev):
            n = TILE[tau][1]
            for gr, gi, heads, w in groups(tau):
                pe.wait_ge(masked, level_no(tau, lev, gr) + 1)
                if lev == 0:
                    pe.wait_ge(n_s, 2 * tau + len(groups(tau)))
                else:
                    pe.wait_ge(tx_s, level_no(tau, lev - 1, gr) + 1)
                for x, h in enumerate(heads):
                    rhs = ident[0:w, 0:w] if lev == 0 else head_block(tb, tau, h)
                    last = nc.tensor.matmul(ps[0:n, 2 + gr, w * x:w * x + w], head_block(mb, tau, h), rhs,
                                            start=True, stop=True)
                last.then_inc(w_t, 1)
            if lev == 0:
                return
            for gr, gi, heads, w in groups(tau):
                pe.wait_ge(w_s, wide_no(tau, lev, gr) + 1)
                if lev < levels(tau) - 1:
                    for x, h in enumerate(heads):
                        nc.tensor.matmul(ps[0:n, 4 + gr, w * x:w * x + w], head_block(xb, tau, h), head_block(wb, tau, h),
                                         start=True, stop=True)
                for x, h in enumerate(heads):
                    last = nc.tensor.matmul(ps[0:n, 6 + gr, w * x:w * x + w], head_block(wb, tau, h),
                                            head_block(xb, tau, h), start=True, stop=True)
                last.then_inc(tx_t, 1)

        def state(tau):
            t0, n = TILE[tau]
            pe.wait_ge(tx_s, level_no(tau, levels(tau) - 1, len(groups(tau)) - 1) + 1)
            if tau == 1:
                pe.wait_ge(S_s, 2)
                for gr in range(2):
                    for kq, bank in ((1, 2), (0, 4)):
                        for h in range(4 * gr, 4 * gr + 4):
                            last = nc.tensor.matmul(ps[:, bank + gr, P * (h % 4):P * (h % 4) + P], qkT[:, kq, h, t0:t0 + n],
                                                    head_values(S, 0, h), start=True, stop=True)
                    last.then_inc(ks_t, 1)
            if tau == 2:
                pe.wait_ge(ld_st, 16 * H)
                for h in range(H):
                    o = ps[:, 2 + h // 4, P * (h % 4):P * (h % 4) + P].rearrange("p (k t) -> p k t", k=2)
                    for s in range(NS):
                        last = nc.tensor.matmul(o[:, :, ST * s:ST * s + ST], states[:, h, s, :],
                                                qkT[:, :, h, SEQ + ST * s:SEQ + ST * s + ST], start=True, stop=True)
                    if h % 4 == 3:
                        last.then_inc(kq_t, 1)
                pe.wait_ge(kq_s, 2)
                for gr in range(2):
                    for kq, bank in ((1, 4), (0, 6)):
                        for x in range(4):
                            last = nc.tensor.transpose(ps[0:64, bank + gr, P * x:P * x + P],
                                                       wb[:, gr, P * x + 64 * kq:P * x + 64 * kq + 64], ident[:])
                    last.then_inc(ks_t, 1)

        def value(tau):
            n = TILE[tau][1]
            for gr in range(2):
                pe.wait_ge(r_s, 2 * tau + gr + 1)
                for h in range(4 * gr, 4 * gr + 4):
                    last = nc.tensor.matmul(head_values(ps[:, u_bank(tau):u_bank(tau) + 2], tau, h), head_block(xb, tau, h),
                                            head_values(nb, tau, h), start=True, stop=True)
                last.then_inc(u_t, 1)

        def out(tau):
            n = TILE[tau][1]
            for gr in range(2):
                pe.wait_ge(u_s, 2 * tau + gr + 1)
                for h in range(4 * gr, 4 * gr + 4):
                    last = nc.tensor.matmul(head_values(ps[:, o_bank(tau):o_bank(tau) + 2], tau, h), head_block(qb, tau, h),
                                            head_values(mb, tau, h), start=True, stop=True)
                last.then_inc(o_t, 1)
                if tau < 2:
                    for h in range(4 * gr, 4 * gr + 4):
                        last = nc.tensor.matmul(ps[:, 4 + gr, P * (h % 4):P * (h % 4) + P], head_values(ktok, tau, h),
                                                head_values(mb, tau, h), start=True, stop=True)
                    last.then_inc(s_t, 1)
            if tau == 2:
                for h in range(H):
                    pe.wait_ge(um_s, h + 1)
                    bank = 2 + 2 * (h % 2)
                    if h >= 2:
                        pe.wait_ge(so_s, h - 1)
                    elif h == 1:
                        pe.wait_ge(o_s, 6)
                    um = (xb, qb)[h % 2]
                    for x in range(2):
                        last = nc.tensor.matmul(ps[:, bank + x, :], head_values(ktok, tau, h), um[0:64, x, :],
                                                start=True, stop=True)
                    last.then_inc(su_t, 1)

        def turn(tau):
            n = TILE[tau][1]
            for gr in range(2):
                pe.wait_ge(o_s, 2 * tau + gr + 1)
                for h in range(4 * gr, 4 * gr + 4):
                    last = nc.tensor.transpose(ps[:, 6 + gr, n * (h % 4):n * (h % 4) + n], head_values(wb, tau, h),
                                               ident[0:n, 0:n])
                last.then_inc(turn_t, 1)

        for n_step, (tau, kind, lev) in enumerate(GDN_STEPS):
            {"tok": tok, "rows": rows, "state": state, "value": value, "out": out, "turn": turn}.get(
                kind, lambda tau: level(tau, lev))(tau)
            for what, m in fills[n_step]:
                if what == "z":
                    i, j = S_Z + m // 4, m % 4
                    if j == 0:
                        wait_slot(pe, i)
                    if m >= 1:
                        pe.wait_ge(z_s, m)
                    else:
                        pe.wait_ge(raw_s, 24)
                    chunk(i, j, ps[:, 0, 0:T], hT).then_inc(z_t, 1)
                else:
                    i, j = S_ADA2 + m // 4, m % 4
                    if j == 0:
                        wait_slot(pe, i)
                    last = chunk(i, j, ps[:, 1, NSEQ * m:NSEQ * m + NSEQ], cT)
                    if j == 3:
                        last.then_inc(ada2_t, 1)

    @block.vector
    def _(dve):
        def link(ins):
            order.link(dve, ins)

        def wide(ap, n, w=P):
            return ap.rearrange("p (h i) -> p h i", i=w)

        def conv(q):
            dve.wait_ge(raw_s, q + 1)
            dve.wait_ge(halo_s, q + 1)
            if q >= 2:
                dve.wait_ge(silu_s, q - 1)
            a, e, c = acc[:, q % 2, :], ext[:, q % 2, :], chan(q)
            m = EW - KW + 1
            link(nc.vector.tensor_scalar(a, e[:, 0:m], convw[:, 0, c:c + 1], None, ALU.mult))
            for j in range(1, KW):
                ins = nc.vector.scalar_tensor_tensor(out=a, in0=e[:, j:j + m], scalar=convw[:, j, c:c + 1], in1=a,
                                                     op0=ALU.mult, op1=ALU.add)
                if j < KW - 1:
                    link(ins)
                else:
                    ins.then_inc(conv_s, 1)

        def sum_out(m):
            dve.wait_ge(ss_t, m + 1)
            s = 1.0 if m < 8 else float(P)
            nc.vector.tensor_scalar(rowsum[:, m], ps[:, 2 + m % 2, 0:T], s, s * 1e-6, ALU.mult, ALU.add).then_inc(ss_s, 1)

        dve.wait_ge(halo0, 1)
        link(nc.vector.memset(ab[:], 0.0))
        dve.wait_ge(ab_t, 1)
        nc.vector.tensor_copy(ab[:, 0:2, :], ps[:, 6, 0:32].rearrange("p (a b) -> p a b", b=16))
        link(nc.vector.tensor_copy(ab[0:64, 2, :], ps[0:64, 6, 32:48]))
        dve.wait_ge(ld_w, 48)
        link(nc.vector.tensor_tensor(ab[:, :, 8:16], ab[:, :, 8:16], par[:, 1:2, :].to_broadcast([P, NTILE, H]), ALU.add))
        nc.vector.tensor_scalar(earg[:, :, 0:8], ab[:, :, 0:8], -1.0, None, ALU.mult)
        nc.vector.tensor_scalar(pos[:], ab[:, :, 8:16], 0.0, None, ALU.max)
        link(nc.vector.scalar_tensor_tensor(out=earg[:, :, 8:16], in0=ab[:, :, 8:16], scalar=-1.0, in1=ab[:, :, 8:16],
                                            op0=ALU.mult, op1=ALU.max))
        nc.vector.tensor_scalar(earg[:, :, 8:16], earg[:, :, 8:16], -1.0, None, ALU.mult).then_inc(ab_arg, 1)
        for q in range(24):
            conv(q)
            if 3 <= q < 19:
                sum_out(q - 3)
            if q == 20:
                for i in range(2):
                    dve.wait_ge(rs_s, i + 1)
                    x = qkT[:, 1 - i].rearrange("p h t -> p (h t)")
                    r = rowsum[:, 8 * i:8 * i + 8].rearrange("p h t -> p (h t)")
                    nc.vector.tensor_tensor(x, x, r, ALU.mult).then_inc(nrm_s, 1)
                dve.wait_ge(ab_ln, 1)
                link(nc.vector.tensor_scalar(earg[:, :, 0:8], earg[:, :, 0:8], 1.0, None, ALU.add))
                nc.vector.reciprocal(beta[:], earg[:, :, 0:8])
                link(nc.vector.tensor_tensor(g[:], pos[:], ab[:, :, 0:8], ALU.add))
                link(nc.vector.scalar_tensor_tensor(out=g[:], in0=g[:], scalar=-1.0,
                                                    in1=par[:, 0:1, :].to_broadcast([P, NTILE, H]), op0=ALU.mult, op1=ALU.mult))
                nc.vector.tensor_tensor(gm[:], g[0:64, 2, :].unsqueeze(2).to_broadcast([64, H, NS]),
                                        sblock[:].unsqueeze(1).to_broadcast([64, H, NS]), ALU.mult).then_inc(g_s, 1)
        link(nc.vector.memset(dec[:], 0.0))
        dve.wait_ge(dec_t, 1)
        for tau, (t0, n) in enumerate(TILE):
            nc.vector.tensor_copy(dec[0:n, tau, 0, :], ps[0:n, 7, 16 * tau:16 * tau + 8])
            link(nc.vector.tensor_copy(dec[0:n, tau, 2, :], ps[0:n, 7, 16 * tau + 8:16 * tau + 16]))
        nc.vector.tensor_tensor(dec[:, :, 1, :], dec[:, :, 2, :], dec[:, :, 0, :], ALU.subtract).then_inc(dec_s, 1)
        dve.wait_ge(edec_s, 1)
        link(nc.vector.tensor_tensor(bdec[:], beta[:], edec[:, :, 0, :], ALU.mult))

        for n_step, (tau, kind, lev) in enumerate(GDN_STEPS):
            t0, n = TILE[tau]
            causes = scausal if tau == 2 else causal
            if kind == "tok":
                if tau:
                    dve.wait_ge(turn_t, 2 * tau)
                for gr, gi, heads, w in groups(tau):
                    k = len(heads)
                    h0 = heads[0]
                    nc.vector.tensor_tensor(wide(nb[0:n, gr, :], n, w), causes[0:n, 0:w].unsqueeze(1).to_broadcast([n, k, w]),
                                            g[0:n, tau, h0:h0 + k].unsqueeze(2).to_broadcast([n, k, w]), ALU.mult)
                    nc.vector.tensor_tensor(wide(wb[0:n, gr, :], n, w), ident[0:n, 0:w].unsqueeze(1).to_broadcast([n, k, w]),
                                            beta[0:n, tau, h0:h0 + k].unsqueeze(2).to_broadcast([n, k, w]),
                                            ALU.mult).then_inc(src_s, 1)
                dve.wait_ge(tok_t, tau + 1)
                for gr in range(2):
                    ins = nc.vector.tensor_tensor(wide(ktok[0:n, gr, :], n), wide(ps[0:n, 2 + gr, :], n),
                                                  edec[0:n, tau, 1, 4 * gr:4 * gr + 4].unsqueeze(2).to_broadcast([n, 4, P]),
                                                  ALU.mult)
                ins.then_inc(ktok_s, 1)
            if kind == "rows":
                for gr, gi, heads, w in groups(tau):
                    k = len(heads)
                    h0 = heads[0]
                    dve.wait_ge(rows_t, gi + 1)
                    link(nc.vector.tensor_tensor(wide(xb[0:n, gr, :], n, w), wide(ps[0:n, 6, :], n, w),
                                                 dec[0:n, tau, 0, h0:h0 + k].unsqueeze(2).to_broadcast([n, k, w]), ALU.subtract))
                    nc.vector.tensor_scalar(xb[0:n, gr, :], xb[0:n, gr, :], 0.0, None, ALU.min).then_inc(darg_s, 1)
                    dve.wait_ge(dexp_s, gi + 1)
                    link(nc.vector.tensor_tensor(wide(tb[0:n, gr, :], n, w), wide(tb[0:n, gr, :], n, w),
                                                 causes[0:n, 0:w].unsqueeze(1).to_broadcast([n, k, w]), ALU.mult))
                    nc.vector.tensor_tensor(qb[0:n, gr, :], ps[0:n, 3 + 2 * gr, :], tb[0:n, gr, :], ALU.mult)
                    link(nc.vector.tensor_tensor(nb[0:n, gr, :], ps[0:n, 2 + 2 * gr, :], tb[0:n, gr, :], ALU.mult))
                    nc.vector.tensor_tensor(nb[0:n, gr, :], nb[0:n, gr, :], ps[0:n, 7, :], ALU.mult).then_inc(n_s, 1)
            if kind == "level":
                for gr, gi, heads, w in groups(tau):
                    k = len(heads)
                    if lev == 0:
                        eye = ident[0:n, 0:w].unsqueeze(1).to_broadcast([n, k, w])
                        dve.wait_ge(masked, level_no(tau, 0, gr) + 1)
                        nc.vector.tensor_tensor(wide(xb[0:n, gr, :], n, w), eye, wide(mb[0:n, gr, :], n, w), ALU.subtract)
                        dve.wait_ge(w_t, level_no(tau, 0, gr) + 1)
                        nc.vector.tensor_tensor(wide(tb[0:n, gr, :], n, w), eye, wide(ps[0:n, 2 + gr, :], n, w),
                                                ALU.subtract).then_inc(tx_s, 1)
                    else:
                        dve.wait_ge(tx_t, wide_no(tau, lev, gr) + 1)
                        dve.wait_ge(tx_s, level_no(tau, lev - 1, gr) + 1)
                        if lev < levels(tau) - 1:
                            nc.vector.tensor_tensor(tb[0:n, gr, :], tb[0:n, gr, :], ps[0:n, 4 + gr, :], ALU.subtract)
                        nc.vector.tensor_tensor(xb[0:n, gr, :], xb[0:n, gr, :], ps[0:n, 6 + gr, :],
                                                ALU.subtract).then_inc(tx_s, 1)
            if kind == "state":
                kb, qbank = (2, 4) if tau == 1 else (4, 6)
                for gr in range(2):
                    bc = lambda a: a[0:n, 4 * gr:4 * gr + 4].unsqueeze(2).to_broadcast([n, 4, P])
                    if gr == 0:
                        dve.wait_ge(vtok_s, 2 * tau + 2)
                    ins = nc.vector.tensor_tensor(wide(nb[0:n, gr, :], n), wide(vtok[0:n, gr, :], n), bc(beta[:, tau, :]),
                                                  ALU.mult)
                    if tau == 0:
                        ins.then_inc(r_s, 1)
                        continue
                    link(ins)
                    dve.wait_ge(ks_t, 2 * (tau - 1) + (gr + 1 if tau == 1 else 2))
                    nc.vector.tensor_tensor(wide(tb[0:n, gr, :], n), wide(ps[0:n, qbank + gr, :], n), bc(edec[:, tau, 0, :]),
                                            ALU.mult)
                    link(nc.vector.tensor_tensor(wide(wb[0:n, gr, :], n), wide(ps[0:n, kb + gr, :], n), bc(bdec[:, tau, :]),
                                                 ALU.mult))
                    nc.vector.tensor_tensor(nb[0:n, gr, :], nb[0:n, gr, :], wb[0:n, gr, :], ALU.subtract).then_inc(r_s, 1)
            if kind == "out":
                for gr in range(2):
                    i = 2 * tau + gr
                    dve.wait_ge(o_t, i + 1)
                    if tau == 0:
                        link(nc.vector.tensor_copy(wb[0:n, gr, :], ps[0:n, o_bank(tau) + gr, :]))
                    else:
                        link(nc.vector.tensor_tensor(wb[0:n, gr, :], ps[0:n, o_bank(tau) + gr, :], tb[0:n, gr, :], ALU.add))
                    link(nc.vector.tensor_tensor(nb[0:n, gr, :], wb[0:n, gr, :], wb[0:n, gr, :], ALU.mult))
                    link(nc.vector.tensor_reduce(oss[0:n, gr, :], wide(nb[0:n, gr, :], n), AX.X, ALU.add))
                    nc.vector.tensor_scalar(oss[0:n, gr, :], oss[0:n, gr, :], 1.0 / P, EPS, ALU.mult, ALU.add).then_inc(oln_s, 1)
                    if tau == 1:
                        sv = wide(S[:, gr, :], P)
                        link(nc.vector.tensor_tensor(sv, sv, edec[:, tau, 2, 4 * gr:4 * gr + 4].unsqueeze(2).to_broadcast([P, 4, P]),
                                                     ALU.mult))
                    if tau < 2:
                        dve.wait_ge(s_t, i + 1)
                    if tau == 0:
                        nc.vector.tensor_copy(S[:, gr, :], ps[:, 4 + gr, :]).then_inc(S_s, 1)
                    if tau == 1:
                        nc.vector.tensor_tensor(S[:, gr, :], S[:, gr, :], ps[:, 4 + gr, :], ALU.add).then_inc(S_s, 1)
                for gr in range(2):
                    i = 2 * tau + gr
                    dve.wait_ge(orr_s, 2 * i + 2)
                    nc.vector.tensor_tensor(wide(wb[0:n, gr, :], n), wide(wb[0:n, gr, :], n),
                                            oss[0:n, gr, :].unsqueeze(2).to_broadcast([n, 4, P]), ALU.mult).then_inc(o_s, 1)
                if tau == 2:
                    def spread(h):
                        if h >= 2:
                            dve.wait_ge(su_t, h - 1)
                        um = (xb, qb)[h % 2][0:64].rearrange("p a n -> p (a n)").rearrange("p (s v) -> p s v", s=NS)
                        nc.vector.tensor_tensor(um, head_values(mb, 2, h).unsqueeze(1).to_broadcast([64, NS, P]),
                                                sblock[:].unsqueeze(2).to_broadcast([64, NS, P]), ALU.mult).then_inc(um_s, 1)
                    dve.wait_ge(u_s, 6)
                    spread(0)
                    spread(1)
                    for h in range(H):
                        dve.wait_ge(su_t, h + 1)
                        dve.wait_ge(scaled_s, h + 1)
                        for x in range(2):
                            sv = states[:, h, 4 * x:4 * x + 4, :].rearrange("p s v -> p (s v)")
                            ins = nc.vector.tensor_tensor(sv, sv, ps[:, 2 + 2 * (h % 2) + x, :], ALU.add)
                        ins.then_inc(so_s, 1)
                        if h + 2 < H:
                            spread(h + 2)
        dve.wait_ge(ada2_t, 8)
        nc.vector.tensor_tensor(adaT[:, 16:48, :], ps[:, 1, 0:32 * NSEQ].rearrange("p (c s) -> p c s", s=NSEQ),
                                bada[:, 16:48].unsqueeze(2).to_broadcast([P, 32, NSEQ]), ALU.add).then_inc(ada_s2, 1)


def u_bank(tau):
    return 6 if tau < 2 else 2


def o_bank(tau):
    return 2 if tau < 2 else 4


def sample_cols(a):
    return a[:, EXT - KW + 1:EXT - KW + 1 + NS * SEXT].rearrange("p (s j) -> p s j", s=NS)[:, :, KW - 1:SEXT]


UNITS = [(kind, c) for kind in ("h", "c", "b", "gb", "wb", "ga", "wa", "wo") for c in range(NC)]
BY_ACT = ("h", "gb", "ga")


def taken(n):
    mine = UNITS[n][0] in BY_ACT
    return mine, sum((kind in BY_ACT) == mine for kind, _ in UNITS[:n + 1])


def branches(nc, t, st, sb, sem, ring, ident, scw, gnw, sst, adaT, hT, oT, zT, tails, x2T, xrow, order, load_slot,
             wait_slot, load_expert_half):
    ps = st.enter_context(nc.psum_tensor("ps_br", [P, 8, 512], F32))
    hb = sb("hb", [P, NC, T], st)
    gb = sb("gb", [P, NC, T], st)
    trow = sb("trow", [P, QKV], st)
    ga = trow[:, 0:NC * T].rearrange("p (c t) -> p c t", c=NC)
    ext = sb("ext2", [P, 2, PW], st)
    acc = sb("acc2", [P, 2, PW], st)
    gtmp = sb("gtmp", [P, 2, NS * ST], st)
    ptails = sb("ptails", [P, NC, PTAILS], st)
    prow = sb("prow", [PTAILS, D], st)
    unit_t, act_s, dve_s, x_ld, x_t, x_s, tr_t, tr_s, pt_t, pt_s, z_silu, o_s, halo0, halo, pre_s, ptail, out_d = (
        sem("br_" + x) if x != "unit_t" else sem(x) for x in (
            "unit_t", "act_s", "dve_s", "x_ld", "x_t", "x_s", "tr_t", "tr_s", "pt_t", "pt_s", "z_silu", "o_s", "halo0",
            "halo", "pre_s", "ptail", "out_d"))
    st_out = sem("st_out")
    SH, SC1, G1 = adaT[:, 0:8, :], adaT[:, 8:16, :], adaT[:, 16:24, :]

    def wait_taken(eng, n):
        mine, k = taken(n)
        eng.wait_ge(act_s if mine else dve_s, k)

    def seq_view(a):
        return a.rearrange("p (s t) -> p s t", s=NS)

    block = st.enter_context(nc.Block())

    @block.sync
    def _(sp):
        for i in range(24, NSLOT1):
            load_slot(sp, i)
            if i == 28:
                sp.wait_ge(tr_s, 6)
                sp.dma_start(t["conv_prompt"][0, 0], trow[0:3, :]).then_inc(out_d, 16)
                sp.dma_start(t["conv_sample"][0].rearrange("s j c -> (s j) c"), trow[3:TAILS, :]).then_inc(out_d, 16)
                sp.wait_ge(pt_s, 2)
                sp.dma_start(t["sc_prompt"][0, 0], prow[0:2, :]).then_inc(out_d, 16)
                sp.dma_start(t["sc_sample"][0].rearrange("s j c -> (s j) c"), prow[2:PTAILS, :]).then_inc(out_d, 16)
        load_expert_half(sp, 0, 4)
        load_expert_half(sp, 0, 5)
        for j in range(RING1):
            sp.wait_ge(unit_t, 4 * (NSLOT1 - RING1 + j - S_H + 1))
            load_expert_half(sp, 0, j)
        sp.wait_ge(out_d, 64)

    @block.gpsimd
    def _(pool):
        nc.gpsimd.memset(ext[:, :, 0:SW - 1], 0.0).then_inc(halo0, 1)
        for c in range(NC):
            if c >= 2:
                pool.wait_ge(dve_s, c - 1)
            e = seq_view(ext[:, c % 2, PEXT:PW])
            nc.gpsimd.tensor_copy(e[:, :, 0:SW - 1], seq_view(sst[:, c])).then_inc(halo, 1)
            pool.wait_ge(pre_s, c + 1)
            nc.gpsimd.tensor_copy(ptails[:, c, 0:2], ext[:, c % 2, PEXT - 2:PEXT])
            nc.gpsimd.tensor_copy(seq_view(ptails[:, c, 2:PTAILS]), e[:, :, PSEXT - 2:PSEXT]).then_inc(ptail, 1)

    @block.scalar
    def _(act):
        for tau in range(2):
            act.dma_start(xrow[:, tau, :], t["x_prompt"][0, P * tau:P * tau + P, :]).then_inc(x_ld, 16)
        act.dma_start(xrow[0:64, 2, :], t["x_sample"].rearrange("s t d -> (s t) d")).then_inc(x_ld, 16)
        nc.scalar.activation(zT[:], zT[:], ACT.Silu).then_inc(z_silu, 1)
        for c in range(NC):
            act.wait_ge(x_t, c + 1)
            nc.scalar.activation(x2T[:, c, :], ps[:, 2 + c % 4, 0:T], ACT.Copy).then_inc(x_s, 1)

        def take(kinds):
            for n, (kind, c) in enumerate(UNITS):
                if kind in kinds:
                    act.wait_ge(unit_t, n + 1)
                    dst = {"h": hb, "gb": gb, "ga": ga}[kind]
                    nc.scalar.activation(dst[:, c, :], ps[:, n % 2, 0:T], ACT.Copy if kind == "h" else ACT.Sigmoid).then_inc(act_s, 1)

        take(("h",))
        act.wait_ge(tr_t, 1)
        for i in range(6):
            nc.scalar.activation(trow[0:TAILS, HALF * i:HALF * i + HALF], ps[0:TAILS, 2 + i, :], ACT.Copy).then_inc(tr_s, 1)
        act.wait_ge(pt_t, 1)
        for i in range(2):
            nc.scalar.activation(prow[:, HALF * i:HALF * i + HALF], ps[0:PTAILS, 2 + i, :], ACT.Copy).then_inc(pt_s, 1)
        take(("gb",))
        act.wait_ge(out_d, 64)
        take(("ga",))

    @block.tensor
    def _(pe):
        pe.wait_ge(x_ld, 48)
        for c in range(NC):
            if c >= 4:
                pe.wait_ge(x_s, c - 3)
            for tau, (t0, n) in enumerate(TILE):
                last = nc.tensor.transpose(ps[:, 2 + c % 4, t0:t0 + n], xrow[0:n, tau, P * c:P * c + P], ident[0:n, 0:n])
            last.then_inc(x_t, 1)
        for n, (kind, c) in enumerate(UNITS):
            if (kind, c) == ("c", 0):
                pe.wait_ge(x_s, NC)
                for k in range(3 * NC):
                    last = nc.tensor.transpose(ps[0:TAILS, 2 + k // 4, P * (k % 4):P * (k % 4) + P], tails[:, k, :], ident[:])
                last.then_inc(tr_t, 1)
            if (kind, c) == ("b", 2):
                pe.wait_ge(ptail, NC)
                pe.wait_ge(tr_s, 6)
                for k in range(NC):
                    last = nc.tensor.transpose(ps[0:PTAILS, 2 + k // 4, P * (k % 4):P * (k % 4) + P], ptails[:, k, :], ident[:])
                last.then_inc(pt_t, 1)
            i, j = S_H + n // 4, n % 4
            if j == 0:
                wait_slot(pe, i)
            if n >= 2:
                wait_taken(pe, n - 2)
            if (kind, c) in (("wb", 0), ("wo", 0)):
                wait_taken(pe, n - 1 if kind == "wo" else n - NC - 1)
            if (kind, c) == ("wa", 0):
                pe.wait_ge(o_s, 1)
            rhs = {"wb": hb, "wa": oT, "wo": ga}.get(kind, hT)
            for k in range(NC):
                last = nc.tensor.matmul(ps[:, n % 2, 0:T], ring[:, i % RING1, k, P * j:P * j + P], rhs[:, k, :],
                                        start=k == 0, stop=k == NC - 1)
            last.then_inc(unit_t, 1)

    @block.vector
    def _(dve):
        def link(ins):
            order.link(dve, ins)

        dve.wait_ge(z_silu, 1)
        dve.wait_ge(halo0, 1)
        nc.vector.scalar_tensor_tensor(out=oT[:].rearrange("p h t -> p (h t)"), in0=oT[:].rearrange("p h t -> p (h t)"),
                                       scalar=gnw, in1=zT[:].rearrange("p h t -> p (h t)"), op0=ALU.mult,
                                       op1=ALU.mult).then_inc(o_s, 1)
        for n, (kind, c) in enumerate(UNITS):
            if kind in BY_ACT:
                continue
            dve.wait_ge(unit_t, n + 1)
            o = ps[:, n % 2, 0:T]
            if kind == "c":
                dve.wait_ge(act_s, c + 1)
                dve.wait_ge(halo, c + 1)
                if c >= 2:
                    dve.wait_ge(ptail, c - 1)
                e, a = ext[:, c % 2, :], acc[:, c % 2, :]
                nc.vector.tensor_tensor(e[:, SW - 1:PEXT], o[:, 0:SEQ], hb[:, c, 0:SEQ], ALU.mult)
                nc.vector.tensor_tensor(seq_view(e[:, PEXT:PW])[:, :, SW - 1:PSEXT], seq_view(o[:, SEQ:T]),
                                        seq_view(hb[:, c, SEQ:T]), ALU.mult).then_inc(pre_s, 1)
                dve.wait_ge(pre_s, c + 1)
                m = PW - SW + 1
                link(nc.vector.tensor_scalar(a[:, 0:m], e[:, 0:m], scw[:, 0, c:c + 1], None, ALU.mult))
                link(nc.vector.scalar_tensor_tensor(out=a[:, 0:m], in0=e[:, 1:m + 1], scalar=scw[:, 1, c:c + 1], in1=a[:, 0:m],
                                                    op0=ALU.mult, op1=ALU.add))
                nc.vector.scalar_tensor_tensor(out=hb[:, c, 0:SEQ], in0=e[:, 2:SEQ + 2], scalar=scw[:, 2, c:c + 1],
                                               in1=a[:, 0:SEQ], op0=ALU.mult, op1=ALU.add)
                s0 = PEXT - SW + 1
                nc.vector.scalar_tensor_tensor(out=seq_view(hb[:, c, SEQ:T]), in0=seq_view(e[:, PEXT:PW])[:, :, 2:PSEXT],
                                               scalar=scw[:, 2, c:c + 1],
                                               in1=seq_view(a[:, s0:s0 + NS * PSEXT])[:, :, SW - 1:PSEXT],
                                               op0=ALU.mult, op1=ALU.add).then_inc(dve_s, 1)
            if kind == "b":
                if c == 0:
                    dve.wait_ge(dve_s, NC)
                nc.vector.tensor_tensor(hb[:, c, :], hb[:, c, :], o, ALU.mult).then_inc(dve_s, 1)
            if kind == "wb":
                dve.wait_ge(act_s, NC + c + 1)
                nc.vector.tensor_tensor(gb[:, c, :], gb[:, c, :], o, ALU.mult).then_inc(dve_s, 1)
            if kind == "wa":
                dve.wait_ge(act_s, 2 * NC + c + 1)
                link(nc.vector.tensor_tensor(ga[:, c, :], ga[:, c, :], o, ALU.mult))
                nc.vector.tensor_tensor(ga[:, c, :], ga[:, c, :], gb[:, c, :], ALU.add).then_inc(dve_s, 1)
            if kind == "wo":
                nc.vector.scalar_tensor_tensor(out=x2T[:, c, 0:SEQ], in0=o[:, 0:SEQ], scalar=G1[:, c, 0:1],
                                               in1=x2T[:, c, 0:SEQ], op0=ALU.mult, op1=ALU.add)
                link(nc.vector.tensor_tensor(seq_view(gtmp[:, c % 2, :]), seq_view(o[:, SEQ:T]),
                                             G1[:, c, 1:NSEQ].unsqueeze(2).to_broadcast([P, NS, ST]), ALU.mult))
                nc.vector.tensor_tensor(x2T[:, c, SEQ:T], x2T[:, c, SEQ:T], gtmp[:, c % 2, :], ALU.add).then_inc(dve_s, 1)


def experts(nc, t, top, sb, sem, ring, ident, ones, causal, vecs, adaT, biasT, x2T, h2tok, order, norm, slot_full,
            load_expert_half, dbg, stop):
    n2w, nfw = vecs[:, 8:16], vecs[:, 16:24]
    SH2, SC2, G2 = adaT[:, 24:32, :], adaT[:, 32:40, :], adaT[:, 40:48, :]
    yacc = sb("yacc", [P, NC, T])
    route = sb("route", [P, E + 1, 2, NTILE])
    iota = sb("iota", [P, CAP])
    count = sb("count", [P, E + 1], dt=I32)
    FAR = 1000.0

    def seq_view(a):
        return a.rearrange("p (s t) -> p s t", s=NS)

    with ExitStack() as st:
        ps = st.enter_context(nc.psum_tensor("ps_rt", [P, 8, 512], F32))
        h2T = sb("h2T", [P, NC, T], st)
        sq = sb("sq_r", [P, 2, T], st)
        rstd = sb("rstd_r", [P, T], st)
        gw = sb("gw_r", [P, NC, NSEQ], st)
        wr = sb("wr", [P, NC, E], st)
        br = sb("br", [P, E], st)
        strict = sb("strict", [P, P], st)
        L = sb("logits", [P, NTILE, E], st)
        m8 = sb("m8", [P, NTILE, 8], st)
        gt = sb("gt", [P, NTILE, E], st)
        eq = sb("eq", [P, NTILE, E], st)
        ceq = sb("ceq", [P, NTILE, E], st)
        need = sb("need", [P, NTILE], st)
        sel = sb("sel", [P, NTILE, E], st)
        wt = sb("wt", [P, NTILE, E], st)
        rank = sb("rank", [P, NTILE, E], st)
        zero = sb("zero32", [P, E], st)
        cmax = sb("cmax", [P, 1], st)
        ld, h_s, hr_t, hr_s, lg_t, arg_s, exp_s, sel_s, rank_t, pk = (
            sem("rt_" + x) for x in ("ld", "h_s", "hr_t", "hr_s", "lg_t", "arg_s", "exp_s", "sel_s", "rank_t", "pk"))
        sq_s, sum_t, mean_s, log_s, rs_s = norm
        block = st.enter_context(nc.Block())

        @block.gpsimd
        def _(pool):
            nc.gpsimd.iota(iota[:], pattern=[[1, CAP]], base=0, channel_multiplier=0,
                           allow_small_or_imprecise_dtypes=True).then_inc(pk, 1)
            nc.gpsimd.tensor_tensor(strict[:], causal[:], ident[:], ALU.subtract).then_inc(pk, 1)
            nc.gpsimd.memset(yacc[:], 0.0).then_inc(pk, 1)
            nc.gpsimd.memset(route[:], FAR).then_inc(pk, 1)

        @block.scalar
        def _(act):
            act.dma_start(wr[:], t["w_router"][0].rearrange("(c p) e -> p c e", p=P)).then_inc(ld, 16)
            act.dma_start(br[:], t["b_router"].to_broadcast([P, E])).then_inc(ld, 16)
            for c in range(NC):
                if c >= 2:
                    act.wait_ge(sum_t, 1 * NC + c - 1)
                nc.scalar.activation(sq[:, c % 2, :], x2T[:, c, :], ACT.Square).then_inc(sq_s, 1)
            act.wait_ge(mean_s, 2)
            nc.scalar.activation(rstd[:], rstd[:], ACT.Ln).then_inc(log_s, 1)
            act.wait_ge(log_s, 2)
            nc.scalar.activation(rstd[:], rstd[:], ACT.Exp, scale=-0.5).then_inc(rs_s, 1)
            for tau, (t0, n) in enumerate(TILE):
                act.wait_ge(hr_t, tau + 1)
                nc.scalar.activation(h2tok[0:n, tau, :].rearrange("p (a b) -> p a b", a=2),
                                     ps[0:n, 2 * tau:2 * tau + 2, :], ACT.Copy).then_inc(hr_s, 1)
            act.wait_ge(arg_s, 1)
            nc.scalar.activation(wt[:], wt[:], ACT.Exp).then_inc(exp_s, 1)

        @block.tensor
        def _(pe):
            for c in range(NC):
                pe.wait_ge(sq_s, 1 * NC + c + 1)
                nc.tensor.matmul(ps[:, 7, 0:T], ones[:], sq[:, c % 2, :], start=c == 0, stop=c == NC - 1).then_inc(sum_t, 1)
            pe.wait_ge(h_s, 1)
            pe.wait_ge(ld, 32)
            for tau, (t0, n) in enumerate(TILE):
                for k in range(NC):
                    last = nc.tensor.matmul(ps[0:n, 6, E * tau:E * tau + E], h2T[:, k, t0:t0 + n], wr[:, k, :],
                                            start=k == 0, stop=k == NC - 1)
            last.then_inc(lg_t, 1)
            for tau, (t0, n) in enumerate(TILE):
                for k in range(NC):
                    last = nc.tensor.transpose(ps[0:n, 2 * tau + k // 4, P * (k % 4):P * (k % 4) + P], h2T[:, k, t0:t0 + n],
                                               ident[:])
                last.then_inc(hr_t, 1)
            pe.wait_ge(pk, 4)
            pe.wait_ge(sel_s, 1)
            for tau, (t0, n) in enumerate(TILE):
                o = ps[0:n, 7, E * tau:E * tau + E]
                for u in range(tau):
                    nc.tensor.matmul(o, ones[:, 0:n], sel[:, u, :], start=u == 0, stop=False)
                nc.tensor.matmul(o, strict[0:n, 0:n], sel[0:n, tau, :], start=tau == 0, stop=True)
            for tau, (t0, n) in enumerate(TILE):
                last = nc.tensor.matmul(ps[:, 7, 3 * E:4 * E], ones[0:n, :], sel[0:n, tau, :], start=tau == 0, stop=tau == 2)
            last.then_inc(rank_t, 1)

        @block.vector
        def _(dve):
            def link(ins):
                order.link(dve, ins)

            def over_e(a):
                return a.unsqueeze(2).to_broadcast([P, NTILE, E])

            link(nc.vector.tensor_scalar(gw[:], SC2, 1.0, None, ALU.add))
            link(nc.vector.tensor_tensor(gw[:], gw[:], n2w.unsqueeze(2).to_broadcast([P, NC, NSEQ]), ALU.mult))
            link(nc.vector.memset(L[:], 0.0))
            link(nc.vector.memset(zero[:], 0.0))
            link(nc.vector.memset(rank[:], 0.0))
            dve.wait_ge(sum_t, 2 * NC)
            nc.vector.tensor_scalar(rstd[:], ps[:, 7, 0:T], 1.0 / D, EPS, ALU.mult, ALU.add).then_inc(mean_s, 1)
            dve.wait_ge(rs_s, 2)
            link(nc.vector.tensor_tensor(h2T[:], x2T[:], rstd[:].unsqueeze(1).to_broadcast([P, NC, T]), ALU.mult))
            for c in range(NC):
                nc.vector.tensor_scalar(h2T[:, c, 0:SEQ], h2T[:, c, 0:SEQ], gw[:, c, 0:1], SH2[:, c, 0:1], ALU.mult, ALU.add)
                link(nc.vector.tensor_tensor(seq_view(h2T[:, c, SEQ:T]), seq_view(h2T[:, c, SEQ:T]),
                                             gw[:, c, 1:NSEQ].unsqueeze(2).to_broadcast([P, NS, ST]), ALU.mult))
                ins = nc.vector.tensor_tensor(seq_view(h2T[:, c, SEQ:T]), seq_view(h2T[:, c, SEQ:T]),
                                              SH2[:, c, 1:NSEQ].unsqueeze(2).to_broadcast([P, NS, ST]), ALU.add)
            ins.then_inc(h_s, 1)
            dve.wait_ge(lg_t, 1)
            dve.wait_ge(ld, 32)
            for tau, (t0, n) in enumerate(TILE):
                ins = nc.vector.tensor_tensor(L[0:n, tau, :], ps[0:n, 6, E * tau:E * tau + E], br[0:n, :], ALU.add)
            link(ins)
            for tau in range(NTILE):
                ins = nc.vector.max(m8[:, tau, :], L[:, tau, :])
            link(ins)
            nc.vector.tensor_tensor(wt[:], L[:], over_e(m8[:, :, 0]), ALU.subtract).then_inc(arg_s, 1)
            nc.vector.tensor_tensor(gt[:], L[:], over_e(m8[:, :, TOPK - 1]), ALU.is_gt)
            link(nc.vector.tensor_tensor(eq[:], L[:], over_e(m8[:, :, TOPK - 1]), ALU.is_equal))
            nc.vector.tensor_reduce(need[:], gt[:], AX.X, ALU.add)
            for tau in range(NTILE):
                ins = nc.vector.tensor_tensor_scan(ceq[:, tau, :], eq[:, tau, :], zero[:], 0.0, ALU.add, ALU.add)
            link(ins)
            link(nc.vector.tensor_scalar(need[:], need[:], -1.0, float(TOPK), ALU.mult, ALU.add))
            link(nc.vector.tensor_tensor(ceq[:], ceq[:], over_e(need[:]), ALU.is_le))
            link(nc.vector.tensor_tensor(eq[:], eq[:], ceq[:], ALU.mult))
            nc.vector.tensor_tensor(sel[:], gt[:], eq[:], ALU.add).then_inc(sel_s, 1)
            dve.wait_ge(sel_s, 1)
            dve.wait_ge(exp_s, 1)
            link(nc.vector.tensor_tensor(wt[:], wt[:], sel[:], ALU.mult))
            link(nc.vector.tensor_reduce(need[:], wt[:], AX.X, ALU.add))
            link(nc.vector.reciprocal(need[:], need[:]))
            dve.wait_ge(pk, 4)
            for tau in range(NTILE):
                nc.vector.tensor_scalar(route[:, 0:E, 1, tau], wt[:, tau, :], need[:, tau:tau + 1], None, ALU.mult)
            dve.wait_ge(rank_t, 1)
            for tau, (t0, n) in enumerate(TILE):
                ins = nc.vector.tensor_scalar(rank[0:n, tau, :], ps[0:n, 7, E * tau:E * tau + E], -FAR, None, ALU.add)
            link(ins)
            link(nc.vector.tensor_tensor(rank[:], rank[:], sel[:], ALU.mult))
            for tau in range(NTILE):
                nc.vector.tensor_scalar(route[:, 0:E, 0, tau], rank[:, tau, :], FAR, None, ALU.add)
            nc.vector.tensor_copy(count[:, 0:E], ps[:, 7, 3 * E:4 * E])
            link(nc.vector.tensor_reduce(cmax[:], ps[:, 7, 3 * E:4 * E], AX.X, ALU.max))
            link(nc.vector.tensor_copy(count[:, E:E + 1], cmax[:]))

    if "route" in dbg:
        dump(nc, sem("dbg_route"), dbg["route"], route[:])
    if stop <= 4:
        return

    with ExitStack() as st:
        ps = st.enter_context(nc.psum_tensor("ps_moe", [P, 8, 512], F32))
        xe = sb("xe", [P, NC, CAP], st)
        gate = sb("gate", [P, NC, CAP], st)
        sig = sb("sig", [P, NC, CAP], st)
        up = sb("up", [P, NC, CAP], st)
        hid = sb("hid", [P, NC, CAP], st)
        yT = sb("yT", [P, NC, CAP], st)
        yrow = sb("yrow", [P, D], st)
        pick = sb("pick", [P, NTILE, CAP], st)
        wpick = sb("wpick", [P, NTILE, CAP], st)
        put = sb("put", [P, T], st)
        cur = sb("cur", [P, 2, NTILE], st)
        nxt = sb("nxt", [P, 2, NTILE], st)
        (pick_s, wpick_s, gath_t, xe_s, gate_s, sig_s, hid_s, yT_s, turn_t, yrow_s, put_s, comb_t, comb_s, ech, half_t) = (sem("ex_" + x) for x in (
             "pick_s", "wpick_s", "gath_t", "xe_s", "gate_s", "sig_s", "hid_s", "yT_s", "turn_t", "yrow_s", "put_s", "comb_t", "comb_s", "ech", "half_t"))
        LINKS = 5

        def flat(a):
            return a.rearrange("p c n -> p (c n)")

        def run_pass(eng, b, body):
            body(b * E, 0, b, True)
            with eng.Fori(1, E) as e:
                body(b * E + e, e, b, False)

        def over_passes(eng, body, prologue, epilogue):
            prologue(0)
            run_pass(eng, 0, body)
            epilogue(0)
            most = eng.value_load(count[0:1, E:E + 1], min_val=0, max_val=T)
            for b in range(1, (T + CAP - 1) // CAP):
                with eng.If(most > CAP * b):
                    prologue(b)
                    run_pass(eng, b, body)
                    epilogue(b)

        block = st.enter_context(nc.Block())

        @block.sync
        def _(sp):
            def body(i, e, b, first):
                if first and b == 0:
                    return
                for j in range(RING):
                    sp.wait_ge(half_t, RING * (i - 1) + j + 1)
                    load_expert_half(sp, e, j)

            over_passes(sp, body, lambda b: None, lambda b: None)

        @block.scalar
        def _(act):
            def take_xe(i):
                act.wait_ge(gath_t, i + 1)
                nc.scalar.activation(xe[:].rearrange("p (a c) n -> p a (c n)", a=2), ps[:, 6:8, :], ACT.Copy).then_inc(xe_s, 1)

            def take_rows(i):
                act.wait_ge(turn_t, 2 * i + 1)
                nc.scalar.activation(yrow[:].rearrange("p (a n) -> p a n", a=2), ps[:, 6:8, :], ACT.Copy).then_inc(yrow_s, 1)
                act.wait_ge(turn_t, 2 * i + 2)
                nc.scalar.activation(put[:], ps[:, 4, 0:T], ACT.Copy).then_inc(put_s, 1)

            def body(i, e, b, first):
                if not first:
                    take_rows(i - 1)
                act.wait_ge(gate_s, i + 1)
                nc.scalar.activation(sig[:], gate[:], ACT.Sigmoid, scale=ALPHA).then_inc(sig_s, 1)
                act.wait_ge(half_t, RING * i + 4)
                take_xe(i + 1 + b)

            over_passes(act, body, lambda b: take_xe(b * (E + 1)), lambda b: take_rows(b * E + E - 1))

        @block.tensor
        def _(pe):
            def gather(i):
                pe.wait_ge(pick_s, i + 1)
                for c in range(NC):
                    for tau, (t0, n) in enumerate(TILE):
                        last = nc.tensor.matmul(ps[:, 6 + c // 4, CAP * (c % 4):CAP * (c % 4) + CAP],
                                                h2tok[0:n, tau, P * c:P * c + P], pick[0:n, tau, :],
                                                start=tau == 0, stop=tau == NTILE - 1)
                last.then_inc(gath_t, 1)

            def half(j, bank, w, x):
                for f in range(4):
                    for k in range(NC):
                        last = nc.tensor.matmul(ps[:, bank, CAP * f:CAP * f + w], ring[:, j, k, P * f:P * f + P], x[:, k, 0:w],
                                                start=k == 0, stop=k == NC - 1)
                last.then_inc(half_t, 1)

            def wide_or_narrow(n_tok, b, j, bank, x):
                with pe.If(n_tok > CAP * b + NARROW):
                    half(j, bank, CAP, x)
                with pe.Else():
                    half(j, bank, NARROW, x)

            def turn(i):
                pe.wait_ge(yT_s, i + 1)
                for c in range(NC):
                    last = nc.tensor.transpose(ps[:, 6 + c // 4, P * (c % 4):P * (c % 4) + P], yT[:, c, :], ident[:])
                last.then_inc(turn_t, 1)
                pe.wait_ge(wpick_s, i + 1)
                for tau, (t0, n) in enumerate(TILE):
                    last = nc.tensor.transpose(ps[:, 4, t0:t0 + n], wpick[0:n, tau, :], ident[0:n, 0:n])
                last.then_inc(turn_t, 1)

            def combine(i):
                pe.wait_ge(yrow_s, i + 1)
                pe.wait_ge(put_s, i + 1)
                for c in range(NC):
                    if c >= 3:
                        pe.wait_ge(comb_s, NC * i + c - 2)
                    nc.tensor.matmul(ps[:, 5 + c % 3, 0:T], yrow[:, P * c:P * c + P], put[:], start=True,
                                     stop=True).then_inc(comb_t, 1)

            def body(i, e, b, first):
                n_tok = pe.value_load(count[0:1, bass.ds(e, 1)], min_val=0, max_val=T)
                pe.wait_ge(xe_s, i + b + 1)
                pe.wait_ge(slot_full[0], full0(0) + 16 * (i + 1))
                if not (first and b == 0):
                    pe.wait_ge(gate_s, i)
                wide_or_narrow(n_tok, b, 0, 0, xe)
                if not first:
                    turn(i - 1)
                pe.wait_ge(slot_full[1], full0(1) + 16 * (i + 1))
                wide_or_narrow(n_tok, b, 1, 1, xe)
                if not first:
                    combine(i - 1)
                pe.wait_ge(slot_full[2], full0(2) + 16 * (i + 1))
                if not (first and b == 0):
                    pe.wait_ge(hid_s, i)
                wide_or_narrow(n_tok, b, 2, 2, xe)
                pe.wait_ge(slot_full[3], full0(3) + 16 * (i + 1))
                wide_or_narrow(n_tok, b, 3, 3, xe)
                if not (first and b == 0):
                    pe.wait_ge(comb_s, NC * i)
                gather(i + b + 1)
                pe.wait_ge(hid_s, i + 1)
                for j in (4, 5):
                    pe.wait_ge(slot_full[j], full0(j) + 16 * (i + 1))
                    wide_or_narrow(n_tok, b, j, j, hid)

            def prologue(b):
                if b:
                    pe.wait_ge(comb_s, NC * b * E)
                gather(b * (E + 1))

            def epilogue(b):
                pe.wait_ge(xe_s, (b + 1) * (E + 1))
                turn(b * E + E - 1)
                combine(b * E + E - 1)

            over_passes(pe, body, prologue, epilogue)

        @block.vector
        def _(dve):
            def picks(i, e, b, link_no):
                if not isinstance(i, int) or i > 0:
                    dve.wait_ge(gath_t, i)
                nc.vector.tensor_scalar(nxt[:], route[:, e], float(-CAP * b), None, ALU.add).then_inc(ech, 1)
                dve.wait_ge(ech, link_no)
                for tau in range(NTILE):
                    ins = nc.vector.tensor_scalar(pick[:, tau, :], iota[:], nxt[:, 0, tau:tau + 1], None, ALU.is_equal)
                ins.then_inc(pick_s, 1)

            def add_up(i):
                for c in range(NC):
                    dve.wait_ge(comb_t, NC * i + c + 1)
                    nc.vector.tensor_tensor(yacc[:, c, :], yacc[:, c, :], ps[:, 5 + c % 3, 0:T], ALU.add).then_inc(comb_s, 1)

            def over_tokens(n, e):
                return biasT[:, n, :, e].unsqueeze(2).to_broadcast([P, NC, CAP])

            def banks(k):
                return ps[:, k:k + 2, :].rearrange("p a (c n) -> p (a c) n", n=CAP)

            def body(i, e, b, first):
                chain = b + 1 + LINKS * i
                picks(i + b + 1, e + 1, b, chain + 1)
                dve.wait_ge(half_t, RING * i + 2)
                nc.vector.tensor_tensor(gate[:], banks(0), over_tokens(0, e), ALU.add).then_inc(ech, 1)
                dve.wait_ge(ech, chain + 2)
                nc.vector.tensor_scalar(flat(gate[:]), flat(gate[:]), LIMIT, None, ALU.min).then_inc(gate_s, 1)
                if not first:
                    add_up(i - 1)
                dve.wait_ge(half_t, RING * i + 4)
                nc.vector.tensor_tensor(up[:], banks(2), over_tokens(1, e), ALU.add).then_inc(ech, 1)
                dve.wait_ge(ech, chain + 3)
                nc.vector.tensor_scalar(flat(up[:]), flat(up[:]), LIMIT, -LIMIT, ALU.min, ALU.max)
                dve.wait_ge(sig_s, i + 1)
                nc.vector.tensor_tensor(flat(gate[:]), flat(gate[:]), flat(sig[:]), ALU.mult).then_inc(ech, 1)
                dve.wait_ge(ech, chain + 4)
                nc.vector.scalar_tensor_tensor(out=flat(hid[:]), in0=flat(up[:]), scalar=1.0, in1=flat(gate[:]), op0=ALU.add,
                                               op1=ALU.mult).then_inc(hid_s, 1)
                nc.vector.tensor_scalar(cur[:, 1, :], route[:, e, 1, :], 1.0, None, ALU.mult)
                nc.vector.tensor_scalar(cur[:, 0, :], route[:, e, 0, :], float(-CAP * b), None, ALU.add).then_inc(ech, 1)
                dve.wait_ge(ech, chain + 5)
                for tau in range(NTILE):
                    ins = nc.vector.tensor_scalar(wpick[:, tau, :], iota[:], cur[:, 0, tau:tau + 1], cur[:, 1, tau:tau + 1],
                                                  ALU.is_equal, ALU.mult)
                ins.then_inc(wpick_s, 1)
                dve.wait_ge(half_t, RING * i + 6)
                nc.vector.tensor_tensor(yT[:], banks(4), over_tokens(2, e), ALU.add).then_inc(yT_s, 1)

            nc.vector.memset(ps[:, 0:6, :].rearrange("p a n -> p (a n)"), 0.0)
            over_passes(dve, body, lambda b: picks(b * (E + 1), 0, b, b + LINKS * b * E + 1), lambda b: add_up(b * E + E - 1))

    if "yacc" in dbg:
        dump(nc, sem("dbg_yacc"), dbg["yacc"], yacc[:])
    with ExitStack() as st:
        ps = st.enter_context(nc.psum_tensor("ps_fin", [P, 8, 512], F32))
        sq = sb("sq_f", [P, 2, T], st)
        rstd = sb("rstd_f", [P, T], st)
        yrows = sb("yrows", [P, NTILE, D], st)
        x_s, y_s, yt_t, yo_s, out_d = (sem("fn_" + x) for x in ("x_s", "y_s", "yt_t", "yo_s", "out_d"))
        sq_s, sum_t, mean_s, log_s, rs_s = norm
        block = st.enter_context(nc.Block())

        @block.vector
        def _(dve):
            for c in range(NC):
                nc.vector.scalar_tensor_tensor(out=x2T[:, c, 0:SEQ], in0=yacc[:, c, 0:SEQ], scalar=G2[:, c, 0:1],
                                               in1=x2T[:, c, 0:SEQ], op0=ALU.mult, op1=ALU.add)
                nc.vector.tensor_tensor(seq_view(yacc[:, c, SEQ:T]), seq_view(yacc[:, c, SEQ:T]),
                                        G2[:, c, 1:NSEQ].unsqueeze(2).to_broadcast([P, NS, ST]), ALU.mult).then_inc(order.semaphore, 1)
                order.count += 1
                dve.wait_ge(order.semaphore, order.count)
                nc.vector.tensor_tensor(x2T[:, c, SEQ:T], x2T[:, c, SEQ:T], yacc[:, c, SEQ:T], ALU.add).then_inc(x_s, 1)
            dve.wait_ge(sum_t, 3 * NC)
            nc.vector.tensor_scalar(rstd[:], ps[:, 7, 0:T], 1.0 / D, EPS, ALU.mult, ALU.add).then_inc(mean_s, 1)
            dve.wait_ge(rs_s, 3)
            for c in range(NC):
                nc.vector.scalar_tensor_tensor(out=x2T[:, c, :], in0=x2T[:, c, :], scalar=nfw[:, c:c + 1], in1=rstd[:],
                                               op0=ALU.mult, op1=ALU.mult).then_inc(y_s, 1)

        @block.scalar
        def _(act):
            for c in range(NC):
                act.wait_ge(x_s, c + 1)
                if c >= 2:
                    act.wait_ge(sum_t, 2 * NC + c - 1)
                nc.scalar.activation(sq[:, c % 2, :], x2T[:, c, :], ACT.Square).then_inc(sq_s, 1)
            act.wait_ge(mean_s, 3)
            nc.scalar.activation(rstd[:], rstd[:], ACT.Ln).then_inc(log_s, 1)
            act.wait_ge(log_s, 3)
            nc.scalar.activation(rstd[:], rstd[:], ACT.Exp, scale=-0.5).then_inc(rs_s, 1)
            for tau, (t0, n) in enumerate(TILE):
                act.wait_ge(yt_t, tau + 1)
                nc.scalar.activation(yrows[0:n, tau, :].rearrange("p (a b) -> p a b", a=2), ps[0:n, 2 * tau:2 * tau + 2, :],
                                     ACT.Copy).then_inc(yo_s, 1)

        @block.tensor
        def _(pe):
            for c in range(NC):
                pe.wait_ge(sq_s, 2 * NC + c + 1)
                nc.tensor.matmul(ps[:, 7, 0:T], ones[:], sq[:, c % 2, :], start=c == 0, stop=c == NC - 1).then_inc(sum_t, 1)
            for tau, (t0, n) in enumerate(TILE):
                for k in range(NC):
                    if tau == 0:
                        pe.wait_ge(y_s, k + 1)
                    last = nc.tensor.transpose(ps[0:n, 2 * tau + k // 4, P * (k % 4):P * (k % 4) + P], x2T[:, k, t0:t0 + n],
                                               ident[:])
                last.then_inc(yt_t, 1)

        @block.sync
        def _(sp):
            for tau in range(2):
                sp.wait_ge(yo_s, tau + 1)
                sp.dma_start(t["y_prompt"][0, P * tau:P * tau + P, :], yrows[:, tau, :]).then_inc(out_d, 16)
            sp.wait_ge(yo_s, 3)
            sp.dma_start(t["y_sample"].rearrange("s t d -> (s t) d"), yrows[0:64, 2, :]).then_inc(out_d, 16)
            sp.wait_ge(out_d, 48)


def full0(r):
    return 16 * (NSLOT1 // RING1) if r < RING1 else 0


def dump(nc, s, dst, src):
    with nc.Block() as block:
        @block.sync
        def _(sp):
            sp.dma_start(dst, src).then_inc(s, 16)
            sp.wait_ge(s, 16)


INS = ["x_prompt", "x_sample", "c_prompt", "c_sample", "state_gdn_conv", "state_gdn_rec", "state_sc_conv", "w_ada",
       "b_ada", "norm1_w", "w_in", "gdn_conv_w", "gdn_a_log", "gdn_dt_bias", "gdn_norm_w", "w_branch_a", "sc_conv_w",
       "w_branch_b", "w_out", "norm2_w", "w_router", "b_router", "w_gate", "b_gate", "w_up", "b_up", "w_down",
       "b_down", "final_norm_w"]
OUTS = [("y_prompt", (1, SEQ, D)), ("y_sample", (NS, ST, D)), ("conv_prompt", (1, 1, 3, QKV)),
        ("rec_prompt", (1, 1, H, P, P)), ("sc_prompt", (1, 1, 2, D)), ("conv_sample", (1, NS, 3, QKV)),
        ("rec_sample", (1, NS, H, P, P)), ("sc_sample", (1, NS, 2, D))]


def kernel(**inputs):
    import numpy as np
    import concourse.bacc as bacc
    from concourse.bass_utils import run_bass_kernel_spmd

    nc = bacc.Bacc("TRN2", target_bir_lowering=False, num_devices=1)
    arrays, t = {}, {}
    for name in INS:
        arrays["in_" + name] = np.ascontiguousarray(inputs[name])
        t[name] = nc.dram_tensor("in_" + name, arrays["in_" + name].shape, F32, kind="ExternalInput").ap()
    for name, shape in OUTS:
        t[name] = nc.dram_tensor("out_" + name, shape, F32, kind="ExternalOutput").ap()
    build(nc, t)
    r = run_bass_kernel_spmd(nc, [arrays], core_ids=[0])
    return tuple(r.results[0]["out_" + name] for name, _ in OUTS)
```

```python
from contextlib import ExitStack

import concourse.bass as bass
from concourse import mybir

F32 = mybir.dt.float32
F32R = mybir.dt.float32r
I32 = mybir.dt.int32
ALU = mybir.AluOpType
ACT = mybir.ActivationFunctionType
AX = mybir.AxisListType

P = 128
D = 1024
NC = D // P
SEQ = 256
NS = 8
ST = 8
T = SEQ + NS * ST
H = 8
QKV = 3 * D
E = 32
TOPK = 4
NSEQ = 1 + NS
EPS = 1e-6
LIMIT = 7.0
ALPHA = 1.702
NTILE = 3
TILE = [(0, 128), (128, 128), (256, 64)]
KW = 4
EXT = SEQ + KW - 1
SEXT = ST + KW - 1
EW = EXT + NS * SEXT
SW = 3
PEXT = SEQ + SW - 1
PSEXT = ST + SW - 1
PW = PEXT + NS * PSEXT
TAILS = 3 * NSEQ
PTAILS = 2 * NSEQ
HALF = 512
RING1 = 4
C_AB, C_B, C_C, C_H, C_GA, C_GB = 4096, 4112, 5136, 6160, 7184, 8208
LEVELS = 7
SLEVELS = 3
CAP = 128
QUART = NC // 2
PIECES = 3 * 2 * 2
RAW = 6
SPLIT = 4
LINKS = 4

ADA1 = [("ada", n * HALF) for n in range(4)]
QKVS = [("in", c * HALF) for c in (2, 3, 0, 1, 4, 5)]
ZS = [("in", 3072), ("in", 3584)]
ADA2 = [("ada", n * HALF) for n in range(4, 12)]
HS = [("in", C_H), ("in", C_H + HALF)]
CS = [("in", C_C), ("in", C_C + HALF)]
BS = [("in", C_B), ("in", C_B + HALF)]
GBS = [("in", C_GB), ("in", C_GB + HALF)]
WBS = [("wb", 0), ("wb", HALF)]
GAS = [("in", C_GA), ("in", C_GA + HALF)]
WAS = [("wa", 0), ("wa", HALF)]
WOS = [("wo", 0), ("wo", HALF)]
SLOTS = ADA1 + QKVS + ZS + ADA2 + HS + CS + BS + GBS + WBS + GAS + WAS + WOS
S_QKV, S_Z = 4, 10
S_ADA2 = 12
S_H = 20
NSLOT1 = len(SLOTS)
assert NSLOT1 == 36 and NSLOT1 % RING1 == 0


class Order:

    def __init__(self, semaphore):
        self.semaphore, self.count = semaphore, 0

    def link(self, engine, instruction):
        self.count += 1
        instruction.then_inc(self.semaphore, 1)
        engine.wait_ge(self.semaphore, self.count)


def build(nc, t, stop=9, dbg=None):
    dbg = dbg or {}
    with ExitStack() as top:
        def sb(name, shape, stack=top, dt=F32):
            return stack.enter_context(nc.sbuf_tensor(name, shape, dt))

        sems = {}

        def sem(name):
            if name not in sems:
                sems[name] = top.enter_context(nc.semaphore(name))
            return sems[name]

        order = Order(sem("vector_order"))
        norm = [sem("norm_" + x) for x in ("square", "sum", "mean", "log", "rstd")]
        ring = sb("ring", [P, RING1, NC, HALF])
        ident = sb("ident", [P, P])
        ones = sb("ones", [P, P])
        causal = sb("causal", [P, P])
        scausal = sb("scausal", [64, 64])
        sblock = sb("sblock", [64, NS])
        ssame = sb("ssame", [64, 64])
        vecs = sb("vecs", [P, 193])
        adaT = sb("adaT", [P, 48, NSEQ])
        work = sb("work", [P, 6 * 1024])
        gbuf = work[:].rearrange("p (k a n) -> p k a n", k=6, a=2)
        x2T = work[:, 0:NC * T].rearrange("p (c t) -> p c t", c=NC)
        rows_of = work[:, NC * T:NC * T + NTILE * D].rearrange("p (a d) -> p a d", a=NTILE)
        slot_full = [sem(f"slot_full{r}") for r in range(RING1)]
        raw_full = [sem(f"raw_full{r}") for r in range(RAW)]
        ada_t, raw_t, z_t, ada2_t, unit_t, st_out = (sem(x) for x in (
            "ada_t", "raw_t", "z_t", "ada2_t", "unit_t", "st_out"))

        n1w = vecs[:, 0:8]
        n2w = vecs[:, 8:16]
        nfw = vecs[:, 16:24]
        gnw = vecs[:, 24:25]
        convw = vecs[:, 25:121].rearrange("p (j c) -> p j c", j=KW)
        scw = vecs[:, 121:145].rearrange("p (j c) -> p j c", j=SW)
        bada = vecs[:, 145:193]
        A_SH1, A_SC1, A_G1, A_SH2, A_SC2, A_G2 = (adaT[:, 8 * n:8 * n + 8, :] for n in range(6))

        w_in = t["w_in"][0]
        dram = {"ada": t["w_ada"][0], "in": w_in, "wb": t["w_branch_b"][0], "wa": t["w_branch_a"][0],
                "wo": t["w_out"][0]}

        def slot_done(i):
            if i < S_QKV:
                return ada_t, i + 1
            if i < S_Z:
                return raw_t, 4 * (i - S_QKV + 1)
            if i < S_ADA2:
                return z_t, 4 * (i - S_Z + 1)
            if i < S_H:
                return ada2_t, i - S_ADA2 + 1
            return unit_t, 4 * (i - S_H + 1)

        def load_slot(sp, i):
            kind, n0 = SLOTS[i]
            r = i % RING1
            if i >= RING1:
                sp.wait_ge(*slot_done(i - RING1))
            src = dram[kind][:, n0:n0 + HALF].rearrange("(c p) n -> p c n", p=P)
            sp.dma_start(ring[:, r], src).then_inc(slot_full[r], 16)

        def load_piece(sp, e, p):
            name, a, q = ("w_gate", "w_up", "w_down")[p // 4], p // 2 % 2, p % 2
            src = t[name][0, e, QUART * P * q:QUART * P * (q + 1), HALF * a:HALF * a + HALF].rearrange("(c p) n -> p c n", p=P)
            sp.dma_start(raw_piece(ring, p), src).then_inc(raw_full[p % RAW], 16)

        def wait_slot(pe, i):
            pe.wait_ge(slot_full[i % RING1], 16 * (i // RING1 + 1))

        with ExitStack() as st12:
            hT = sb("hT", [P, NC, T], st12)
            cT = sb("cT", [P, NC, NSEQ], st12)
            gst = sb("gst", [P, 3 * NC, 3 * NS], st12)
            sst = sb("sst", [P, NC, 2 * NS], st12)
            with ExitStack() as st:
                ps = st.enter_context(nc.psum_tensor("ps_pro", [P, 8, 512], F32))
                xrow = sb("xrow", [P, NTILE, D], st)
                crow = sb("crow", [NSEQ, D], st)
                vrow1 = sb("vrow1", [121, P], st)
                vrow2 = sb("vrow2", [72, P], st)
                gstrow = sb("gstrow", [3 * NS, QKV], st)
                sstrow = sb("sstrow", [2 * NS, D], st)
                xT = sb("xT", [P, NC, T], st)
                sq = sb("sq", [P, 2, T], st)
                rstd = sb("rstd", [P, T], st)
                gw = sb("gw", [P, NC, NSEQ], st)
                ld_c, ld_v, ld_x, ld_s = (sem(f"ld_{n}") for n in "cvxs")
                k_ones, k_ident, k_masks = sem("k_ones"), sem("k_ident"), sem("k_masks")
                silu_c, vec_t, vec_s, c_sb = sem("silu_c"), sem("vec_t"), sem("vec_s"), sem("c_sb")
                st_t, st_s = sem("st_t"), sem("st_s")
                x_t, x_s = sem("x_t"), sem("x_s")
                sq_s, sum_t, mean_s, log_s, rstd_s = norm
                block = st.enter_context(nc.Block())

                @block.sync
                def _(sp):
                    for i in range(6):
                        load_slot(sp, i)

                @block.gpsimd
                def _(pool):
                    nc.gpsimd.memset(ones[:], 1.0).then_inc(k_ones, 1)
                    nc.gpsimd.memset(ident[:], 0.0).then_inc(k_ones, 1)
                    nc.gpsimd.memset(causal[:], 1.0).then_inc(k_ones, 1)
                    nc.gpsimd.memset(sblock[:], 1.0).then_inc(k_ones, 1)
                    pool.wait_ge(k_ones, 4)
                    nc.gpsimd.affine_select(out=ident[:], in_=ident[:], compare_op=ALU.not_equal, fill=1.0,
                                            base=0, pattern=[[-1, P]], channel_multiplier=1).then_inc(k_ident, 1)
                    nc.gpsimd.affine_select(out=causal[:], in_=causal[:], compare_op=ALU.is_ge, fill=0.0,
                                            base=0, pattern=[[1, P]], channel_multiplier=-1).then_inc(k_masks, 1)
                    nc.gpsimd.affine_select(out=sblock[:], in_=sblock[:], compare_op=ALU.is_ge, fill=0.0,
                                            base=0, pattern=[[-ST, NS]], channel_multiplier=1).then_inc(k_masks, 1)
                    pool.wait_ge(k_masks, 2)
                    nc.gpsimd.affine_select(out=sblock[:], in_=sblock[:], compare_op=ALU.is_ge, fill=0.0,
                                            base=ST - 1, pattern=[[ST, NS]], channel_multiplier=-1).then_inc(k_masks, 1)
                    pool.wait_ge(k_masks, 3)
                    nc.gpsimd.tensor_copy(ssame[:].rearrange("p (s t) -> p s t", s=NS),
                                          sblock[:].unsqueeze(2).to_broadcast([64, NS, ST])).then_inc(k_masks, 1)
                    pool.wait_ge(k_masks, 4)
                    nc.gpsimd.tensor_tensor(scausal[:], ssame[:], causal[0:64, 0:64], ALU.mult).then_inc(k_masks, 1)

                @block.scalar
                def _(act):
                    act.dma_start(crow[0:1, :], t["c_prompt"]).then_inc(ld_c, 16)
                    act.dma_start(crow[1:NSEQ, :], t["c_sample"]).then_inc(ld_c, 16)
                    for tau in range(2):
                        act.dma_start(xrow[:, tau, :], t["x_prompt"][0, P * tau:P * tau + P, :]).then_inc(ld_x, 16)
                    act.dma_start(xrow[0:64, 2, :], t["x_sample"].rearrange("s t d -> (s t) d")).then_inc(ld_x, 16)
                    rows = lambda a: a.rearrange("a (c p) -> (a c) p", p=P)
                    act.dma_start(vrow1[0:8, :], rows(t["norm1_w"])).then_inc(ld_v, 16)
                    act.dma_start(vrow1[8:16, :], rows(t["norm2_w"])).then_inc(ld_v, 16)
                    act.dma_start(vrow1[16:24, :], t["final_norm_w"].rearrange("(c p) -> c p", p=P)).then_inc(ld_v, 16)
                    act.dma_start(vrow1[24:25, :], t["gdn_norm_w"]).then_inc(ld_v, 16)
                    act.dma_start(vrow1[25:121, :], rows(t["gdn_conv_w"][0])).then_inc(ld_v, 16)
                    act.dma_start(vrow2[0:24, :], rows(t["sc_conv_w"][0])).then_inc(ld_v, 16)
                    act.dma_start(vrow2[24:72, :], rows(t["b_ada"])).then_inc(ld_v, 16)
                    act.dma_start(gstrow[:], t["state_gdn_conv"][0].rearrange("s j c -> (s j) c")).then_inc(ld_s, 16)
                    act.dma_start(sstrow[:], t["state_sc_conv"][0].rearrange("s j c -> (s j) c")).then_inc(ld_s, 16)
                    act.wait_ge(ld_c, 32)
                    nc.scalar.activation(crow[:], crow[:], ACT.Silu).then_inc(silu_c, 1)
                    for c in range(NC):
                        act.wait_ge(x_t, c + 1)
                        if c >= 2:
                            act.wait_ge(sum_t, c - 1)
                        nc.scalar.activation(xT[:, c, :], ps[:, 3 + c % 4, 0:T], ACT.Copy).then_inc(x_s, 1)
                        nc.scalar.activation(sq[:, c % 2, :], ps[:, 3 + c % 4, 0:T], ACT.Square).then_inc(sq_s, 1)
                    act.wait_ge(mean_s, 1)
                    nc.scalar.activation(rstd[:], rstd[:], ACT.Ln).then_inc(log_s, 1)
                    act.wait_ge(log_s, 1)
                    nc.scalar.activation(rstd[:], rstd[:], ACT.Exp, scale=-0.5).then_inc(rstd_s, 1)

                @block.tensor
                def _(pe):
                    pe.wait_ge(k_ident, 1)
                    pe.wait_ge(ld_v, 7 * 16)
                    nc.tensor.transpose(ps[:, 0, 0:121], vrow1[:], ident[0:121, 0:121])
                    nc.tensor.transpose(ps[:, 0, 121:193], vrow2[:], ident[0:72, 0:72]).then_inc(vec_t, 1)
                    pe.wait_ge(silu_c, 1)
                    for c in range(NC):
                        last = nc.tensor.transpose(ps[:, 0, 256 + NSEQ * c:256 + NSEQ * c + NSEQ],
                                                   crow[:, P * c:P * c + P], ident[0:NSEQ, 0:NSEQ])
                    last.then_inc(vec_t, 1)
                    pe.wait_ge(ld_x, 48)
                    pe.wait_ge(k_ones, 4)

                    def add_square(c):
                        pe.wait_ge(sq_s, c + 1)
                        nc.tensor.matmul(ps[:, 7, 0:T], ones[:], sq[:, c % 2, :], start=c == 0,
                                         stop=c == NC - 1).then_inc(sum_t, 1)

                    for c in range(NC):
                        if c >= 4:
                            pe.wait_ge(sq_s, c - 3)
                        for tau, (t0, n) in enumerate(TILE):
                            last = nc.tensor.transpose(ps[:, 3 + c % 4, t0:t0 + n], xrow[0:n, tau, P * c:P * c + P],
                                                       ident[0:n, 0:n])
                        last.then_inc(x_t, 1)
                        if c >= 1:
                            add_square(c - 1)
                    add_square(NC - 1)
                    pe.wait_ge(ld_s, 32)
                    pe.wait_ge(sq_s, NC)
                    for c in range(3 * NC):
                        nc.tensor.transpose(ps[:, 3 + c // 16, 24 * (c % 16):24 * (c % 16) + 24],
                                            gstrow[:, P * c:P * c + P], ident[0:24, 0:24])
                    for c in range(NC):
                        last = nc.tensor.transpose(ps[:, 4, 384 + 16 * c:400 + 16 * c], sstrow[:, P * c:P * c + P],
                                                   ident[0:16, 0:16])
                    last.then_inc(st_t, 1)
                    pe.wait_ge(c_sb, 1)
                    for i in range(4):
                        wait_slot(pe, i)
                        for j in range(4):
                            o = ps[:, 5, NSEQ * (4 * i + j):NSEQ * (4 * i + j) + NSEQ]
                            for k in range(NC):
                                last = nc.tensor.matmul(o, ring[:, i % RING1, k, P * j:P * j + P], cT[:, k, :],
                                                        start=k == 0, stop=k == NC - 1)
                        last.then_inc(ada_t, 1)

                @block.vector
                def _(dve):
                    def link(ins):
                        order.link(dve, ins)

                    dve.wait_ge(vec_t, 2)
                    nc.vector.tensor_copy(vecs[:], ps[:, 0, 0:193]).then_inc(vec_s, 1)
                    nc.vector.tensor_copy(cT[:].rearrange("p c s -> p (c s)"), ps[:, 0, 256:256 + NC * NSEQ]).then_inc(c_sb, 1)
                    dve.wait_ge(sum_t, NC)
                    nc.vector.tensor_scalar(rstd[:], ps[:, 7, 0:T], 1.0 / D, EPS, ALU.mult, ALU.add).then_inc(mean_s, 1)
                    dve.wait_ge(st_t, 1)
                    g2 = gst[:].rearrange("p c j -> p (c j)")
                    nc.vector.tensor_copy(g2[:, 0:384], ps[:, 3, 0:384])
                    nc.vector.tensor_copy(g2[:, 384:576], ps[:, 4, 0:192])
                    nc.vector.tensor_copy(sst[:].rearrange("p c j -> p (c j)"), ps[:, 4, 384:512]).then_inc(st_s, 1)
                    dve.wait_ge(rstd_s, 1)
                    dve.wait_ge(x_s, NC)
                    link(nc.vector.tensor_tensor(xT[:], xT[:], rstd[:].unsqueeze(1).to_broadcast([P, NC, T]), ALU.mult))
                    dve.wait_ge(ada_t, 4)
                    dve.wait_ge(vec_s, 1)
                    link(nc.vector.tensor_tensor(adaT[:, 0:16, :], ps[:, 5, 0:16 * NSEQ].rearrange("p (c s) -> p c s", s=NSEQ),
                                                 bada[:, 0:16].unsqueeze(2).to_broadcast([P, 16, NSEQ]), ALU.add))
                    link(nc.vector.tensor_scalar(gw[:], A_SC1, 1.0, None, ALU.add))
                    link(nc.vector.tensor_tensor(gw[:], gw[:], n1w.unsqueeze(2).to_broadcast([P, NC, NSEQ]), ALU.mult))
                    for c in range(NC):
                        nc.vector.tensor_scalar(hT[:, c, 0:SEQ], xT[:, c, 0:SEQ], gw[:, c, 0:1], A_SH1[:, c, 0:1],
                                                ALU.mult, ALU.add)
                    for c in range(NC):
                        link(nc.vector.tensor_tensor(
                            hT[:, c, SEQ:T].rearrange("p (s t) -> p s t", s=NS),
                            xT[:, c, SEQ:T].rearrange("p (s t) -> p s t", s=NS),
                            gw[:, c, 1:NSEQ].unsqueeze(2).to_broadcast([P, NS, ST]), ALU.mult))
                        nc.vector.tensor_tensor(
                            hT[:, c, SEQ:T].rearrange("p (s t) -> p s t", s=NS),
                            hT[:, c, SEQ:T].rearrange("p (s t) -> p s t", s=NS),
                            A_SH1[:, c, 1:NSEQ].unsqueeze(2).to_broadcast([P, NS, ST]), ALU.add)

            for name, ap in (("hT", hT), ("gst", gst), ("sst", sst), ("ada1", adaT[:, 0:16, :])):
                if name in dbg:
                    dump(nc, sem("dbg_" + name), dbg[name], ap[:] if name != "ada1" else ap)
            if stop <= 1:
                return

            z_and_o = ExitStack()
            with z_and_o:
                oT = sb("oT", [P, H, T], z_and_o)
                zT = sb("zT", [P, H, T], z_and_o)
                tails = sb("tails", [P, 3 * NC, TAILS], z_and_o)
                with ExitStack() as st:
                    mixer(nc, t, st, sb, sem, ring, ident, ones, causal, scausal, sblock, ssame, convw,
                          bada, adaT, hT, cT, gst, oT, zT, tails, gbuf, order, load_slot, wait_slot)
                for name, ap in (("oT", oT), ("zT", zT), ("tails", tails), ("adaT", adaT)):
                    if name in dbg:
                        dump(nc, sem("dbg_" + name), dbg[name], ap[:])
                if stop <= 2:
                    return
                with ExitStack() as st:
                    branches(nc, t, st, sb, sem, ring, ident, scw, gnw, sst, adaT, hT, oT, zT, tails, x2T, rows_of, order,
                             load_slot, wait_slot, load_piece)
                if "x2T" in dbg:
                    dump(nc, sem("dbg_x2T"), dbg["x2T"], x2T)
            if stop <= 3:
                return
        experts(nc, t, top, sb, sem, ring, ident, ones, causal, vecs, adaT, x2T, rows_of, order, norm,
                raw_full, load_piece, dbg, stop)



def head_block(buf, tau, h):
    if tau < 2:
        return buf[:, h // 4, P * (h % 4):P * (h % 4) + P]
    return buf[0:64, 0, 64 * h:64 * h + 64]


def head_values(buf, tau, h):
    n = TILE[tau][1]
    return buf[0:n, h // 4, P * (h % 4):P * (h % 4) + P]


def groups(tau):
    return [(0, 2 * tau, range(0, 4), P), (1, 2 * tau + 1, range(4, 8), P)] if tau < 2 else [(0, 4, range(H), 64)]


def levels(tau):
    return LEVELS if tau < 2 else SLEVELS


def level_no(tau, lev, g):
    return 2 * LEVELS * tau + (2 * lev + g if tau < 2 else lev)


def wide_no(tau, lev, g):
    return 2 * (LEVELS - 1) * tau + (2 * (lev - 1) + g if tau < 2 else lev - 1)


GDN_STEPS = [(tau, kind, lev) for tau in range(NTILE) for kind, lev in
             [("tok", 0), ("rows", 0)] + [("level", x) for x in range(levels(tau))] +
             [("state", 0), ("value", 0), ("out", 0), ("turn", 0)]]


def mixer(nc, t, st, sb, sem, ring, ident, ones, causal, scausal, sblock, ssame, convw, bada, adaT, hT, cT, gst,
          oT, zT, tails, gbuf, order, load_slot, wait_slot):
    ps = st.enter_context(nc.psum_tensor("ps_mix", [P, 8, 512], F32))
    qkT = sb("qkT", [P, 2, H, T], st)
    states = sb("states", [P, H, NS, P], st)
    ktok = sb("ktok", [P, 2, 512], st)
    vtok = sb("vtok", [P, 2, 512], st)
    nb, mb, tb, xb, wb, qb = (gbuf[:, i] for i in range(6))
    rowsum = gbuf[:, 0:5].rearrange("p a b c -> p (a b c)").rearrange("p (m t) -> p m t", t=T)
    cbuf = sb("cbuf", [P, 2 * EW + 2 * (EW - KW + 1)], st)
    ext = cbuf[:, 0:2 * EW].rearrange("p (a n) -> p a n", a=2)
    acc = cbuf[:, 2 * EW:].rearrange("p (a n) -> p a n", a=2)
    sqb = sb("sqb", [P, 2, T], st)
    S = cbuf[:, 0:1024].rearrange("p (a n) -> p a n", a=2)
    masks = sb("masks", [P, LEVELS, P], st)
    wab = sb("wab", [P, NC, 16], st)
    par = sb("par", [P, 2, H], st)
    ab = sb("ab", [P, NTILE, 16], st)
    earg = sb("earg", [P, NTILE, 16], st)
    beta = sb("beta", [P, NTILE, H], st)
    g = sb("g", [P, NTILE, H], st)
    pos = sb("pos_part", [P, NTILE, H], st)
    dec = sb("dec", [P, NTILE, 3, H], st)
    edec = sb("edec", [P, NTILE, 3, H], st)
    bdec = sb("bdec", [P, NTILE, H], st)
    gm = sb("gm", [64, H, NS], st)
    cds = sb("cds", [P, H, NS], st)
    oss = sb("oss", [P, 2, 4], st)

    (ld_w, ld_st, halo0, halo_s, raw_t, raw_s, tail_s, conv_s, silu_s, sq_s2, ss_t, ss_s, lnn_s, rs_s, nrm_s,
     mask0, mask_s) = (sem(x) for x in (
         "ld_w", "ld_st", "halo0", "halo_s", "raw_t", "raw_s", "tail_s", "conv_s", "qkv_silu_s", "qkv_sq_s", "ss_t",
         "ss_s", "lnn_s", "rs_s", "nrm_s", "mask0", "mask_s"))
    ab_t, ab_arg, ab_exp, ab_ln, g_s, dec_t, dec_s, edec_s, bdec_s = (sem(x) for x in (
        "ab_t", "ab_arg", "ab_exp", "ab_ln", "g_s", "dec_t", "dec_s", "edec_s", "bdec_s"))
    (tok_t, ktok_s, vtok_s, src_s, rows_t, darg_s, dexp_s, n_s, masked, w_t, w_s, tx_t, tx_s, ks_t, kq_t, kq_s, r_s,
     u_t, u_s, o_t, s_t, S_s, oln_s, orr_s, o_s, turn_t, turn_s) = (sem(x) for x in (
         "tok_t", "ktok_s", "vtok_s", "src_s", "rows_t", "darg_s", "dexp_s", "n_s", "masked", "w_t", "w_s", "tx_t",
         "tx_s", "ks_t", "kq_t", "kq_s", "r_s", "u_t", "u_s", "o_t", "s_t", "S_s", "oln_s", "orr_s", "o_s", "turn_t",
         "turn_s"))
    z_t, z_s, ada2_t, ada_s2, um_s, su_t, scaled_s, so_s, st_out = (sem(x) for x in (
        "z_t", "z_s", "ada2_t", "ada_s2", "um_s", "su_t", "scaled_s", "so_s", "st_out"))

    def chan(q):
        return (8 + q, q - 8, q)[q // 8]

    def dest(q):
        return (qkT[:, 1, q % 8], qkT[:, 0, q % 8], oT[:, q % 8])[q // 8]

    fills = [[] for _ in GDN_STEPS]
    units = [("z", m) for m in range(8)] + [("ada", m) for m in range(32)]
    for n, u in enumerate(units):
        fills[n * len(GDN_STEPS) // len(units)].append(u)

    block = st.enter_context(nc.Block())

    @block.sync
    def _(sp):
        for h in range(H):
            sp.dma_start(states[:, h], t["state_gdn_rec"][0, :, h].rearrange("s k v -> k s v")).then_inc(ld_st, 16)
        for i in range(6, 20):
            load_slot(sp, i)
        sp.wait_ge(S_s, 4)
        sp.dma_start(t["rec_prompt"][0, 0].rearrange("h k v -> k h v"),
                     S[:].rearrange("p a n -> p (a n)").rearrange("p (h v) -> p h v", h=H)).then_inc(st_out, 16)
        for h in range(H):
            sp.wait_ge(so_s, h + 1)
            sp.dma_start(t["rec_sample"][0, :, h].rearrange("s k v -> k s v"), states[:, h]).then_inc(st_out, 16)
        for i in range(20, 24):
            load_slot(sp, i)
        sp.wait_ge(st_out, 16 * (1 + H))

    @block.gpsimd
    def _(pool):
        nc.gpsimd.memset(ext[:, :, 0:KW - 1], 0.0).then_inc(halo0, 1)
        nc.gpsimd.memset(masks[:], 0.0).then_inc(mask0, 1)
        pool.wait_ge(mask0, 1)
        k = 0
        for lev in range(LEVELS):
            b = 1 << lev
            v = masks[:, lev].rearrange("p (m z r) -> p m z r", z=2, r=b)[:, :, 1, :]
            nc.gpsimd.memset(v, 1.0).then_inc(mask_s, 1)
            k += 1
            pool.wait_ge(mask_s, k)
            nc.gpsimd.affine_select(out=v, in_=v, compare_op=ALU.is_ge, fill=0.0, base=0,
                                    pattern=[[-2 * b, P // (2 * b)], [0, b]], channel_multiplier=1).then_inc(mask_s, 1)
            k += 1
            pool.wait_ge(mask_s, k)
            nc.gpsimd.affine_select(out=v, in_=v, compare_op=ALU.is_ge, fill=0.0, base=b - 1,
                                    pattern=[[2 * b, P // (2 * b)], [0, b]], channel_multiplier=-1).then_inc(mask_s, 1)
            k += 1
        pool.wait_ge(mask_s, k)
        for q in range(24):
            if q >= 2:
                pool.wait_ge(conv_s, q - 1)
            e = ext[:, q % 2, EXT:EW].rearrange("p (s j) -> p s j", s=NS)
            nc.gpsimd.tensor_copy(e[:, :, 0:KW - 1], gst[:, chan(q)].rearrange("p (s j) -> p s j", s=NS)).then_inc(halo_s, 1)
            pool.wait_ge(raw_s, q + 1)
            nc.gpsimd.tensor_copy(tails[:, chan(q), 0:3], ext[:, q % 2, EXT - 3:EXT])
            nc.gpsimd.tensor_copy(tails[:, chan(q), 3:TAILS].rearrange("p (s j) -> p s j", s=NS),
                                  e[:, :, SEXT - 3:SEXT]).then_inc(tail_s, 1)
        for tau, kind, lev in GDN_STEPS:
            if kind == "level":
                for gr, gi, heads, w in groups(tau):
                    n = TILE[tau][1]
                    pool.wait_ge(n_s, gi + 1)
                    if lev == 1:
                        pool.wait_ge(tx_s, level_no(tau, 0, gr) + 1)
                    if lev >= 2:
                        pool.wait_ge(w_t, level_no(tau, lev - 1, gr) + 1)
                    nc.gpsimd.tensor_tensor(
                        mb[0:n, gr, :].rearrange("p (h i) -> p h i", i=w),
                        nb[0:n, gr, :].rearrange("p (h i) -> p h i", i=w),
                        masks[0:n, lev, 0:w].unsqueeze(1).to_broadcast([n, 512 // w, w]), ALU.mult).then_inc(masked, 1)
            if (tau, kind) == (2, "state"):
                pool.wait_ge(kq_t, 2)
                pool.wait_ge(edec_s, 2)
                for h in range(H):
                    nc.gpsimd.tensor_tensor(states[:, h], states[:, h],
                                            cds[:, h, :].unsqueeze(2).to_broadcast([P, NS, P]), ALU.mult).then_inc(scaled_s, 1)

    @block.scalar
    def _(act):
        act.dma_start(wab[:], t["w_in"][0][:, C_AB:C_AB + 16].rearrange("(c p) n -> p c n", p=P)).then_inc(ld_w, 16)
        act.dma_start(par[:, 0, :], t["gdn_a_log"].to_broadcast([P, H])).then_inc(ld_w, 16)
        act.dma_start(par[:, 1, :], t["gdn_dt_bias"].to_broadcast([P, H])).then_inc(ld_w, 16)

        def silu(q):
            act.wait_ge(conv_s, q + 1)
            a = acc[:, q % 2]
            nc.scalar.activation(dest(q)[:, 0:SEQ], a[:, 0:SEQ], ACT.Silu)
            nc.scalar.activation(dest(q)[:, SEQ:T].rearrange("p (s t) -> p s t", s=NS), sample_cols(a),
                                 ACT.Silu).then_inc(silu_s, 1)
            if q < 16:
                act.wait_ge(silu_s, q + 1)
                if q >= 2:
                    act.wait_ge(ss_t, q - 1)
                nc.scalar.activation(sqb[:, q % 2, :], dest(q), ACT.Square).then_inc(sq_s2, 1)

        for q in range(24):
            act.wait_ge(raw_t, q + 1)
            if q >= 2:
                act.wait_ge(conv_s, q - 1)
                act.wait_ge(tail_s, q - 1)
            nc.scalar.activation(ext[:, q % 2, KW - 1:EXT], ps[:, q % 2, 0:SEQ], ACT.Copy)
            nc.scalar.activation(ext[:, q % 2, EXT:EW].rearrange("p (s j) -> p s j", s=NS)[:, :, KW - 1:SEXT],
                                 ps[:, q % 2, SEQ:T].rearrange("p (s t) -> p s t", s=NS), ACT.Copy).then_inc(raw_s, 1)
            if q >= 1:
                silu(q - 1)
            if q == 18:
                act.wait_ge(ss_s, 16)
                for i in range(2):
                    nc.scalar.activation(rowsum[:, 8 * i:8 * i + 8], rowsum[:, 8 * i:8 * i + 8], ACT.Ln).then_inc(lnn_s, 1)
                for i in range(2):
                    act.wait_ge(lnn_s, i + 1)
                    nc.scalar.activation(rowsum[:, 8 * i:8 * i + 8], rowsum[:, 8 * i:8 * i + 8], ACT.Exp,
                                         scale=-0.5).then_inc(rs_s, 1)
                act.wait_ge(ab_arg, 1)
                nc.scalar.activation(earg[:], earg[:], ACT.Exp)
                nc.scalar.activation(par[:, 0, :], par[:, 0, :], ACT.Exp).then_inc(ab_exp, 1)
                act.wait_ge(ab_exp, 1)
                nc.scalar.activation(ab[:, :, 0:8], earg[:, :, 8:16], ACT.Ln, bias=1.0).then_inc(ab_ln, 1)
        silu(23)
        act.wait_ge(dec_s, 1)
        nc.scalar.activation(edec[:], dec[:], ACT.Exp).then_inc(edec_s, 1)
        nc.scalar.activation(cds[:], ps[:, 7, 128:192].rearrange("p (h s) -> p h s", h=H), ACT.Exp).then_inc(edec_s, 1)

        for n_step, (tau, kind, lev) in enumerate(GDN_STEPS):
            t0, n = TILE[tau]
            if kind == "tok":
                act.wait_ge(tok_t, tau + 1)
                for gr in range(2):
                    nc.scalar.activation(vtok[0:n, gr, :], ps[0:n, 4 + gr, :], ACT.Copy).then_inc(vtok_s, 1)
            if kind == "rows":
                for gr, gi, heads, w in groups(tau):
                    act.wait_ge(darg_s, gi + 1)
                    nc.scalar.activation(tb[0:n, gr, :], xb[0:n, gr, :], ACT.Exp).then_inc(dexp_s, 1)
            if kind == "level" and lev >= 1:
                for gr, gi, heads, w in groups(tau):
                    act.wait_ge(w_t, level_no(tau, lev, gr) + 1)
                    nc.scalar.activation(wb[0:n, gr, :], ps[0:n, 2 + gr, :], ACT.Copy).then_inc(w_s, 1)
            if (tau, kind) == (2, "state"):
                for gr in range(2):
                    act.wait_ge(kq_t, gr + 1)
                    nc.scalar.activation(wb[:, gr, :], ps[:, 2 + gr, :], ACT.Copy).then_inc(kq_s, 1)
            if kind == "value":
                for gr in range(2):
                    act.wait_ge(u_t, 2 * tau + gr + 1)
                    nc.scalar.activation(mb[0:n, gr, :], ps[0:n, u_bank(tau) + gr, :], ACT.Copy).then_inc(u_s, 1)
            if kind == "out":
                for gr in range(2):
                    i = 2 * tau + gr
                    act.wait_ge(oln_s, i + 1)
                    nc.scalar.activation(oss[0:n, gr, :], oss[0:n, gr, :], ACT.Ln).then_inc(orr_s, 1)
                    act.wait_ge(orr_s, 2 * i + 1)
                    nc.scalar.activation(oss[0:n, gr, :], oss[0:n, gr, :], ACT.Exp, scale=-0.5).then_inc(orr_s, 1)
            if kind == "turn":
                for gr in range(2):
                    act.wait_ge(turn_t, 2 * tau + gr + 1)
                    nc.scalar.activation(oT[:, 4 * gr:4 * gr + 4, t0:t0 + n],
                                         ps[:, 6 + gr, 0:4 * n].rearrange("p (h t) -> p h t", h=4), ACT.Copy).then_inc(turn_s, 1)
            for what, m in fills[n_step]:
                if what == "z":
                    act.wait_ge(z_t, m + 1)
                    nc.scalar.activation(zT[:, m], ps[:, 0, 0:T], ACT.Copy).then_inc(z_s, 1)

    @block.tensor
    def _(pe):
        def sums(m):
            pe.wait_ge(sq_s2, m + 1)
            if m >= 2:
                pe.wait_ge(ss_s, m - 1)
            nc.tensor.matmul(ps[:, 2 + m % 2, 0:T], ones[:], sqb[:, m % 2, :], start=True, stop=True).then_inc(ss_t, 1)

        def chunk(i, j, out, rhs):
            for k in range(NC):
                last = nc.tensor.matmul(out, ring[:, i % RING1, k, P * j:P * j + P], rhs[:, k, :],
                                        start=k == 0, stop=k == NC - 1)
            return last

        pe.wait_ge(ld_w, 48)
        for tau, (t0, n) in enumerate(TILE):
            for k in range(NC):
                last = nc.tensor.matmul(ps[0:n, 6, 16 * tau:16 * tau + 16], hT[:, k, t0:t0 + n], wab[:, k, :],
                                        start=k == 0, stop=k == NC - 1)
        last.then_inc(ab_t, 1)
        for q in range(24):
            i, j = S_QKV + q // 4, q % 4
            if j == 0:
                wait_slot(pe, i)
            if q >= 2:
                pe.wait_ge(raw_s, q - 1)
            chunk(i, j, ps[:, q % 2, 0:T], hT).then_inc(raw_t, 1)
            if 3 <= q < 19:
                sums(q - 3)
            if q == 22:
                pe.wait_ge(g_s, 1)
                for tau, (t0, n) in enumerate(TILE):
                    o = ps[0:n, 7, 16 * tau:16 * tau + 16]
                    nc.tensor.matmul(o[:, 0:8], (scausal if tau == 2 else causal)[:], g[0:n, tau, :], start=True, stop=True)
                    nc.tensor.matmul(o[:, 8:16], (ssame if tau == 2 else ones)[:], g[0:n, tau, :], start=True, stop=True)
                nc.tensor.matmul(ps[:, 7, 128:192], ones[0:64, :], gm[:].rearrange("p h s -> p (h s)"),
                                 start=True, stop=True).then_inc(dec_t, 1)

        def tok(tau):
            t0, n = TILE[tau]
            if tau == 0:
                pe.wait_ge(nrm_s, 1)
                pe.wait_ge(silu_s, 24)
            else:
                pe.wait_ge(turn_s, 2 * tau)
                pe.wait_ge(S_s, 2 * tau)
            for src, bank in ((qkT[:, 1], 2), (oT, 4)):
                for h in range(H):
                    last = nc.tensor.transpose(ps[0:n, bank + h // 4, P * (h % 4):P * (h % 4) + P], src[:, h, t0:t0 + n],
                                               ident[:])
            last.then_inc(tok_t, 1)

        def rows(tau):
            t0, n = TILE[tau]
            for gr, gi, heads, w in groups(tau):
                pe.wait_ge(src_s, gi + 1)
                if gr == 0:
                    pe.wait_ge(ktok_s, tau + 1)
                    pe.wait_ge(vtok_s, 2 * tau + 2)
                    pe.wait_ge(nrm_s, 2)
                else:
                    pe.wait_ge(n_s, gi)
                nc.tensor.matmul(ps[0:n, 6, :], ones[0:n, 0:n], nb[0:n, gr, :], start=True, stop=True)
                nc.tensor.matmul(ps[0:n, 7, :], ones[0:n, 0:n], wb[0:n, gr, :], start=True, stop=True)
                for x, h in enumerate(heads):
                    nc.tensor.matmul(ps[0:n, 2 + 2 * gr, w * x:w * x + w], qkT[:, 1, h, t0:t0 + n],
                                     qkT[:, 1, h, t0:t0 + n], start=True, stop=True)
                for x, h in enumerate(heads):
                    last = nc.tensor.matmul(ps[0:n, 3 + 2 * gr, w * x:w * x + w], qkT[:, 1, h, t0:t0 + n],
                                            qkT[:, 0, h, t0:t0 + n], start=True, stop=True)
                last.then_inc(rows_t, 1)

        def level(tau, lev):
            n = TILE[tau][1]
            for gr, gi, heads, w in groups(tau):
                pe.wait_ge(masked, level_no(tau, lev, gr) + 1)
                if lev == 0:
                    pe.wait_ge(n_s, 2 * tau + len(groups(tau)))
                else:
                    pe.wait_ge(tx_s, level_no(tau, lev - 1, gr) + 1)
                for x, h in enumerate(heads):
                    rhs = ident[0:w, 0:w] if lev == 0 else head_block(tb, tau, h)
                    last = nc.tensor.matmul(ps[0:n, 2 + gr, w * x:w * x + w], head_block(mb, tau, h), rhs,
                                            start=True, stop=True)
                last.then_inc(w_t, 1)
            if lev == 0:
                return
            for gr, gi, heads, w in groups(tau):
                pe.wait_ge(w_s, wide_no(tau, lev, gr) + 1)
                if lev < levels(tau) - 1:
                    for x, h in enumerate(heads):
                        nc.tensor.matmul(ps[0:n, 4 + gr, w * x:w * x + w], head_block(xb, tau, h), head_block(wb, tau, h),
                                         start=True, stop=True)
                for x, h in enumerate(heads):
                    last = nc.tensor.matmul(ps[0:n, 6 + gr, w * x:w * x + w], head_block(wb, tau, h),
                                            head_block(xb, tau, h), start=True, stop=True)
                last.then_inc(tx_t, 1)

        def state(tau):
            t0, n = TILE[tau]
            pe.wait_ge(tx_s, level_no(tau, levels(tau) - 1, len(groups(tau)) - 1) + 1)
            if tau == 1:
                pe.wait_ge(S_s, 2)
                for gr in range(2):
                    for kq, bank in ((1, 2), (0, 4)):
                        for h in range(4 * gr, 4 * gr + 4):
                            last = nc.tensor.matmul(ps[:, bank + gr, P * (h % 4):P * (h % 4) + P], qkT[:, kq, h, t0:t0 + n],
                                                    head_values(S, 0, h), start=True, stop=True)
                    last.then_inc(ks_t, 1)
            if tau == 2:
                pe.wait_ge(ld_st, 16 * H)
                for h in range(H):
                    o = ps[:, 2 + h // 4, P * (h % 4):P * (h % 4) + P].rearrange("p (k t) -> p k t", k=2)
                    for s in range(NS):
                        last = nc.tensor.matmul(o[:, :, ST * s:ST * s + ST], states[:, h, s, :],
                                                qkT[:, :, h, SEQ + ST * s:SEQ + ST * s + ST], start=True, stop=True)
                    if h % 4 == 3:
                        last.then_inc(kq_t, 1)
                pe.wait_ge(kq_s, 2)
                for gr in range(2):
                    for kq, bank in ((1, 4), (0, 6)):
                        for x in range(4):
                            last = nc.tensor.transpose(ps[0:64, bank + gr, P * x:P * x + P],
                                                       wb[:, gr, P * x + 64 * kq:P * x + 64 * kq + 64], ident[:])
                    last.then_inc(ks_t, 1)

        def value(tau):
            n = TILE[tau][1]
            for gr in range(2):
                pe.wait_ge(r_s, 2 * tau + gr + 1)
                for h in range(4 * gr, 4 * gr + 4):
                    last = nc.tensor.matmul(head_values(ps[:, u_bank(tau):u_bank(tau) + 2], tau, h), head_block(xb, tau, h),
                                            head_values(nb, tau, h), start=True, stop=True)
                last.then_inc(u_t, 1)

        def out(tau):
            n = TILE[tau][1]
            for gr in range(2):
                pe.wait_ge(u_s, 2 * tau + gr + 1)
                for h in range(4 * gr, 4 * gr + 4):
                    last = nc.tensor.matmul(head_values(ps[:, o_bank(tau):o_bank(tau) + 2], tau, h), head_block(qb, tau, h),
                                            head_values(mb, tau, h), start=True, stop=True)
                last.then_inc(o_t, 1)
                if tau < 2:
                    for h in range(4 * gr, 4 * gr + 4):
                        last = nc.tensor.matmul(ps[:, 4 + gr, P * (h % 4):P * (h % 4) + P], head_values(ktok, tau, h),
                                                head_values(mb, tau, h), start=True, stop=True)
                    last.then_inc(s_t, 1)
            if tau == 2:
                for h in range(H):
                    pe.wait_ge(um_s, h + 1)
                    bank = 2 + 2 * (h % 2)
                    if h >= 2:
                        pe.wait_ge(so_s, h - 1)
                    elif h == 1:
                        pe.wait_ge(o_s, 6)
                    um = (xb, qb)[h % 2]
                    for x in range(2):
                        last = nc.tensor.matmul(ps[:, bank + x, :], head_values(ktok, tau, h), um[0:64, x, :],
                                                start=True, stop=True)
                    last.then_inc(su_t, 1)

        def turn(tau):
            n = TILE[tau][1]
            for gr in range(2):
                pe.wait_ge(o_s, 2 * tau + gr + 1)
                for h in range(4 * gr, 4 * gr + 4):
                    last = nc.tensor.transpose(ps[:, 6 + gr, n * (h % 4):n * (h % 4) + n], head_values(wb, tau, h),
                                               ident[0:n, 0:n])
                last.then_inc(turn_t, 1)

        for n_step, (tau, kind, lev) in enumerate(GDN_STEPS):
            {"tok": tok, "rows": rows, "state": state, "value": value, "out": out, "turn": turn}.get(
                kind, lambda tau: level(tau, lev))(tau)
            for what, m in fills[n_step]:
                if what == "z":
                    i, j = S_Z + m // 4, m % 4
                    if j == 0:
                        wait_slot(pe, i)
                    if m >= 1:
                        pe.wait_ge(z_s, m)
                    else:
                        pe.wait_ge(raw_s, 24)
                    chunk(i, j, ps[:, 0, 0:T], hT).then_inc(z_t, 1)
                else:
                    i, j = S_ADA2 + m // 4, m % 4
                    if j == 0:
                        wait_slot(pe, i)
                    last = chunk(i, j, ps[:, 1, NSEQ * m:NSEQ * m + NSEQ], cT)
                    if j == 3:
                        last.then_inc(ada2_t, 1)

    @block.vector
    def _(dve):
        def link(ins):
            order.link(dve, ins)

        def wide(ap, n, w=P):
            return ap.rearrange("p (h i) -> p h i", i=w)

        def conv(q):
            dve.wait_ge(raw_s, q + 1)
            dve.wait_ge(halo_s, q + 1)
            if q >= 2:
                dve.wait_ge(silu_s, q - 1)
            a, e, c = acc[:, q % 2, :], ext[:, q % 2, :], chan(q)
            m = EW - KW + 1
            link(nc.vector.tensor_scalar(a, e[:, 0:m], convw[:, 0, c:c + 1], None, ALU.mult))
            for j in range(1, KW):
                ins = nc.vector.scalar_tensor_tensor(out=a, in0=e[:, j:j + m], scalar=convw[:, j, c:c + 1], in1=a,
                                                     op0=ALU.mult, op1=ALU.add)
                if j < KW - 1:
                    link(ins)
                else:
                    ins.then_inc(conv_s, 1)

        def sum_out(m):
            dve.wait_ge(ss_t, m + 1)
            s = 1.0 if m < 8 else float(P)
            nc.vector.tensor_scalar(rowsum[:, m], ps[:, 2 + m % 2, 0:T], s, s * 1e-6, ALU.mult, ALU.add).then_inc(ss_s, 1)

        dve.wait_ge(halo0, 1)
        link(nc.vector.memset(ab[:], 0.0))
        dve.wait_ge(ab_t, 1)
        nc.vector.tensor_copy(ab[:, 0:2, :], ps[:, 6, 0:32].rearrange("p (a b) -> p a b", b=16))
        link(nc.vector.tensor_copy(ab[0:64, 2, :], ps[0:64, 6, 32:48]))
        dve.wait_ge(ld_w, 48)
        link(nc.vector.tensor_tensor(ab[:, :, 8:16], ab[:, :, 8:16], par[:, 1:2, :].to_broadcast([P, NTILE, H]), ALU.add))
        nc.vector.tensor_scalar(earg[:, :, 0:8], ab[:, :, 0:8], -1.0, None, ALU.mult)
        nc.vector.tensor_scalar(pos[:], ab[:, :, 8:16], 0.0, None, ALU.max)
        link(nc.vector.scalar_tensor_tensor(out=earg[:, :, 8:16], in0=ab[:, :, 8:16], scalar=-1.0, in1=ab[:, :, 8:16],
                                            op0=ALU.mult, op1=ALU.max))
        nc.vector.tensor_scalar(earg[:, :, 8:16], earg[:, :, 8:16], -1.0, None, ALU.mult).then_inc(ab_arg, 1)
        for q in range(24):
            conv(q)
            if 3 <= q < 19:
                sum_out(q - 3)
            if q == 20:
                for i in range(2):
                    dve.wait_ge(rs_s, i + 1)
                    x = qkT[:, 1 - i].rearrange("p h t -> p (h t)")
                    r = rowsum[:, 8 * i:8 * i + 8].rearrange("p h t -> p (h t)")
                    nc.vector.tensor_tensor(x, x, r, ALU.mult).then_inc(nrm_s, 1)
                dve.wait_ge(ab_ln, 1)
                link(nc.vector.tensor_scalar(earg[:, :, 0:8], earg[:, :, 0:8], 1.0, None, ALU.add))
                nc.vector.reciprocal(beta[:], earg[:, :, 0:8])
                link(nc.vector.tensor_tensor(g[:], pos[:], ab[:, :, 0:8], ALU.add))
                link(nc.vector.scalar_tensor_tensor(out=g[:], in0=g[:], scalar=-1.0,
                                                    in1=par[:, 0:1, :].to_broadcast([P, NTILE, H]), op0=ALU.mult, op1=ALU.mult))
                nc.vector.tensor_tensor(gm[:], g[0:64, 2, :].unsqueeze(2).to_broadcast([64, H, NS]),
                                        sblock[:].unsqueeze(1).to_broadcast([64, H, NS]), ALU.mult).then_inc(g_s, 1)
        link(nc.vector.memset(dec[:], 0.0))
        dve.wait_ge(dec_t, 1)
        for tau, (t0, n) in enumerate(TILE):
            nc.vector.tensor_copy(dec[0:n, tau, 0, :], ps[0:n, 7, 16 * tau:16 * tau + 8])
            link(nc.vector.tensor_copy(dec[0:n, tau, 2, :], ps[0:n, 7, 16 * tau + 8:16 * tau + 16]))
        nc.vector.tensor_tensor(dec[:, :, 1, :], dec[:, :, 2, :], dec[:, :, 0, :], ALU.subtract).then_inc(dec_s, 1)
        dve.wait_ge(edec_s, 1)
        link(nc.vector.tensor_tensor(bdec[:], beta[:], edec[:, :, 0, :], ALU.mult))

        for n_step, (tau, kind, lev) in enumerate(GDN_STEPS):
            t0, n = TILE[tau]
            causes = scausal if tau == 2 else causal
            if kind == "tok":
                if tau:
                    dve.wait_ge(turn_t, 2 * tau)
                for gr, gi, heads, w in groups(tau):
                    k = len(heads)
                    h0 = heads[0]
                    nc.vector.tensor_tensor(wide(nb[0:n, gr, :], n, w), causes[0:n, 0:w].unsqueeze(1).to_broadcast([n, k, w]),
                                            g[0:n, tau, h0:h0 + k].unsqueeze(2).to_broadcast([n, k, w]), ALU.mult)
                    nc.vector.tensor_tensor(wide(wb[0:n, gr, :], n, w), ident[0:n, 0:w].unsqueeze(1).to_broadcast([n, k, w]),
                                            beta[0:n, tau, h0:h0 + k].unsqueeze(2).to_broadcast([n, k, w]),
                                            ALU.mult).then_inc(src_s, 1)
                dve.wait_ge(tok_t, tau + 1)
                for gr in range(2):
                    ins = nc.vector.tensor_tensor(wide(ktok[0:n, gr, :], n), wide(ps[0:n, 2 + gr, :], n),
                                                  edec[0:n, tau, 1, 4 * gr:4 * gr + 4].unsqueeze(2).to_broadcast([n, 4, P]),
                                                  ALU.mult)
                ins.then_inc(ktok_s, 1)
            if kind == "rows":
                for gr, gi, heads, w in groups(tau):
                    k = len(heads)
                    h0 = heads[0]
                    dve.wait_ge(rows_t, gi + 1)
                    link(nc.vector.tensor_tensor(wide(xb[0:n, gr, :], n, w), wide(ps[0:n, 6, :], n, w),
                                                 dec[0:n, tau, 0, h0:h0 + k].unsqueeze(2).to_broadcast([n, k, w]), ALU.subtract))
                    nc.vector.tensor_scalar(xb[0:n, gr, :], xb[0:n, gr, :], 0.0, None, ALU.min).then_inc(darg_s, 1)
                    dve.wait_ge(dexp_s, gi + 1)
                    link(nc.vector.tensor_tensor(wide(tb[0:n, gr, :], n, w), wide(tb[0:n, gr, :], n, w),
                                                 causes[0:n, 0:w].unsqueeze(1).to_broadcast([n, k, w]), ALU.mult))
                    nc.vector.tensor_tensor(qb[0:n, gr, :], ps[0:n, 3 + 2 * gr, :], tb[0:n, gr, :], ALU.mult)
                    link(nc.vector.tensor_tensor(nb[0:n, gr, :], ps[0:n, 2 + 2 * gr, :], tb[0:n, gr, :], ALU.mult))
                    nc.vector.tensor_tensor(nb[0:n, gr, :], nb[0:n, gr, :], ps[0:n, 7, :], ALU.mult).then_inc(n_s, 1)
            if kind == "level":
                for gr, gi, heads, w in groups(tau):
                    k = len(heads)
                    if lev == 0:
                        eye = ident[0:n, 0:w].unsqueeze(1).to_broadcast([n, k, w])
                        dve.wait_ge(masked, level_no(tau, 0, gr) + 1)
                        nc.vector.tensor_tensor(wide(xb[0:n, gr, :], n, w), eye, wide(mb[0:n, gr, :], n, w), ALU.subtract)
                        dve.wait_ge(w_t, level_no(tau, 0, gr) + 1)
                        nc.vector.tensor_tensor(wide(tb[0:n, gr, :], n, w), eye, wide(ps[0:n, 2 + gr, :], n, w),
                                                ALU.subtract).then_inc(tx_s, 1)
                    else:
                        dve.wait_ge(tx_t, wide_no(tau, lev, gr) + 1)
                        dve.wait_ge(tx_s, level_no(tau, lev - 1, gr) + 1)
                        if lev < levels(tau) - 1:
                            nc.vector.tensor_tensor(tb[0:n, gr, :], tb[0:n, gr, :], ps[0:n, 4 + gr, :], ALU.subtract)
                        nc.vector.tensor_tensor(xb[0:n, gr, :], xb[0:n, gr, :], ps[0:n, 6 + gr, :],
                                                ALU.subtract).then_inc(tx_s, 1)
            if kind == "state":
                kb, qbank = (2, 4) if tau == 1 else (4, 6)
                for gr in range(2):
                    bc = lambda a: a[0:n, 4 * gr:4 * gr + 4].unsqueeze(2).to_broadcast([n, 4, P])
                    if gr == 0:
                        dve.wait_ge(vtok_s, 2 * tau + 2)
                    ins = nc.vector.tensor_tensor(wide(nb[0:n, gr, :], n), wide(vtok[0:n, gr, :], n), bc(beta[:, tau, :]),
                                                  ALU.mult)
                    if tau == 0:
                        ins.then_inc(r_s, 1)
                        continue
                    link(ins)
                    dve.wait_ge(ks_t, 2 * (tau - 1) + (gr + 1 if tau == 1 else 2))
                    nc.vector.tensor_tensor(wide(tb[0:n, gr, :], n), wide(ps[0:n, qbank + gr, :], n), bc(edec[:, tau, 0, :]),
                                            ALU.mult)
                    link(nc.vector.tensor_tensor(wide(wb[0:n, gr, :], n), wide(ps[0:n, kb + gr, :], n), bc(bdec[:, tau, :]),
                                                 ALU.mult))
                    nc.vector.tensor_tensor(nb[0:n, gr, :], nb[0:n, gr, :], wb[0:n, gr, :], ALU.subtract).then_inc(r_s, 1)
            if kind == "out":
                for gr in range(2):
                    i = 2 * tau + gr
                    dve.wait_ge(o_t, i + 1)
                    if tau == 0:
                        link(nc.vector.tensor_copy(wb[0:n, gr, :], ps[0:n, o_bank(tau) + gr, :]))
                    else:
                        link(nc.vector.tensor_tensor(wb[0:n, gr, :], ps[0:n, o_bank(tau) + gr, :], tb[0:n, gr, :], ALU.add))
                    link(nc.vector.tensor_tensor(nb[0:n, gr, :], wb[0:n, gr, :], wb[0:n, gr, :], ALU.mult))
                    link(nc.vector.tensor_reduce(oss[0:n, gr, :], wide(nb[0:n, gr, :], n), AX.X, ALU.add))
                    nc.vector.tensor_scalar(oss[0:n, gr, :], oss[0:n, gr, :], 1.0 / P, EPS, ALU.mult, ALU.add).then_inc(oln_s, 1)
                    if tau == 1:
                        sv = wide(S[:, gr, :], P)
                        link(nc.vector.tensor_tensor(sv, sv, edec[:, tau, 2, 4 * gr:4 * gr + 4].unsqueeze(2).to_broadcast([P, 4, P]),
                                                     ALU.mult))
                    if tau < 2:
                        dve.wait_ge(s_t, i + 1)
                    if tau == 0:
                        nc.vector.tensor_copy(S[:, gr, :], ps[:, 4 + gr, :]).then_inc(S_s, 1)
                    if tau == 1:
                        nc.vector.tensor_tensor(S[:, gr, :], S[:, gr, :], ps[:, 4 + gr, :], ALU.add).then_inc(S_s, 1)
                for gr in range(2):
                    i = 2 * tau + gr
                    dve.wait_ge(orr_s, 2 * i + 2)
                    nc.vector.tensor_tensor(wide(wb[0:n, gr, :], n), wide(wb[0:n, gr, :], n),
                                            oss[0:n, gr, :].unsqueeze(2).to_broadcast([n, 4, P]), ALU.mult).then_inc(o_s, 1)
                if tau == 2:
                    def spread(h):
                        if h >= 2:
                            dve.wait_ge(su_t, h - 1)
                        um = (xb, qb)[h % 2][0:64].rearrange("p a n -> p (a n)").rearrange("p (s v) -> p s v", s=NS)
                        nc.vector.tensor_tensor(um, head_values(mb, 2, h).unsqueeze(1).to_broadcast([64, NS, P]),
                                                sblock[:].unsqueeze(2).to_broadcast([64, NS, P]), ALU.mult).then_inc(um_s, 1)
                    dve.wait_ge(u_s, 6)
                    spread(0)
                    spread(1)
                    for h in range(H):
                        dve.wait_ge(su_t, h + 1)
                        dve.wait_ge(scaled_s, h + 1)
                        for x in range(2):
                            sv = states[:, h, 4 * x:4 * x + 4, :].rearrange("p s v -> p (s v)")
                            ins = nc.vector.tensor_tensor(sv, sv, ps[:, 2 + 2 * (h % 2) + x, :], ALU.add)
                        ins.then_inc(so_s, 1)
                        if h + 2 < H:
                            spread(h + 2)
        dve.wait_ge(ada2_t, 8)
        nc.vector.tensor_tensor(adaT[:, 16:48, :], ps[:, 1, 0:32 * NSEQ].rearrange("p (c s) -> p c s", s=NSEQ),
                                bada[:, 16:48].unsqueeze(2).to_broadcast([P, 32, NSEQ]), ALU.add).then_inc(ada_s2, 1)


def u_bank(tau):
    return 6 if tau < 2 else 2


def o_bank(tau):
    return 2 if tau < 2 else 4


def sample_cols(a):
    return a[:, EXT - KW + 1:EXT - KW + 1 + NS * SEXT].rearrange("p (s j) -> p s j", s=NS)[:, :, KW - 1:SEXT]


UNITS = [(kind, c) for kind in ("h", "c", "b", "gb", "wb", "ga", "wa", "wo") for c in range(NC)]
BY_ACT = ("h", "gb", "ga")


def taken(n):
    mine = UNITS[n][0] in BY_ACT
    return mine, sum((kind in BY_ACT) == mine for kind, _ in UNITS[:n + 1])


def branches(nc, t, st, sb, sem, ring, ident, scw, gnw, sst, adaT, hT, oT, zT, tails, x2T, xrow, order, load_slot,
             wait_slot, load_piece):
    ps = st.enter_context(nc.psum_tensor("ps_br", [P, 8, 512], F32))
    hb = sb("hb", [P, NC, T], st)
    gb = sb("gb", [P, NC, T], st)
    trow = sb("trow", [P, QKV], st)
    ga = trow[:, 0:NC * T].rearrange("p (c t) -> p c t", c=NC)
    ext = sb("ext2", [P, 2, PW], st)
    acc = sb("acc2", [P, 2, PW], st)
    gtmp = sb("gtmp", [P, 2, NS * ST], st)
    ptails = sb("ptails", [P, NC, PTAILS], st)
    prow = sb("prow", [PTAILS, D], st)
    unit_t, act_s, dve_s, x_ld, x_t, x_s, tr_t, tr_s, pt_t, pt_s, z_silu, o_s, halo0, halo, pre_s, ptail, out_d = (
        sem("br_" + x) if x != "unit_t" else sem(x) for x in (
            "unit_t", "act_s", "dve_s", "x_ld", "x_t", "x_s", "tr_t", "tr_s", "pt_t", "pt_s", "z_silu", "o_s", "halo0",
            "halo", "pre_s", "ptail", "out_d"))
    st_out = sem("st_out")
    SH, SC1, G1 = adaT[:, 0:8, :], adaT[:, 8:16, :], adaT[:, 16:24, :]

    def wait_taken(eng, n):
        mine, k = taken(n)
        eng.wait_ge(act_s if mine else dve_s, k)

    def seq_view(a):
        return a.rearrange("p (s t) -> p s t", s=NS)

    block = st.enter_context(nc.Block())

    @block.sync
    def _(sp):
        for i in range(24, NSLOT1):
            load_slot(sp, i)
            if i == 28:
                sp.wait_ge(tr_s, 6)
                sp.dma_start(t["conv_prompt"][0, 0], trow[0:3, :]).then_inc(out_d, 16)
                sp.dma_start(t["conv_sample"][0].rearrange("s j c -> (s j) c"), trow[3:TAILS, :]).then_inc(out_d, 16)
                sp.wait_ge(pt_s, 2)
                sp.dma_start(t["sc_prompt"][0, 0], prow[0:2, :]).then_inc(out_d, 16)
                sp.dma_start(t["sc_sample"][0].rearrange("s j c -> (s j) c"), prow[2:PTAILS, :]).then_inc(out_d, 16)
        for p in range(RAW):
            if p % 2 == 0:
                sp.wait_ge(unit_t, 4 * (NSLOT1 - RING1 + p // 2 - S_H + 1))
            load_piece(sp, 0, p)
        sp.wait_ge(out_d, 64)

    @block.gpsimd
    def _(pool):
        nc.gpsimd.memset(ext[:, :, 0:SW - 1], 0.0).then_inc(halo0, 1)
        for c in range(NC):
            if c >= 2:
                pool.wait_ge(dve_s, c - 1)
            e = seq_view(ext[:, c % 2, PEXT:PW])
            nc.gpsimd.tensor_copy(e[:, :, 0:SW - 1], seq_view(sst[:, c])).then_inc(halo, 1)
            pool.wait_ge(pre_s, c + 1)
            nc.gpsimd.tensor_copy(ptails[:, c, 0:2], ext[:, c % 2, PEXT - 2:PEXT])
            nc.gpsimd.tensor_copy(seq_view(ptails[:, c, 2:PTAILS]), e[:, :, PSEXT - 2:PSEXT]).then_inc(ptail, 1)

    @block.scalar
    def _(act):
        for tau in range(2):
            act.dma_start(xrow[:, tau, :], t["x_prompt"][0, P * tau:P * tau + P, :]).then_inc(x_ld, 16)
        act.dma_start(xrow[0:64, 2, :], t["x_sample"].rearrange("s t d -> (s t) d")).then_inc(x_ld, 16)
        nc.scalar.activation(zT[:], zT[:], ACT.Silu).then_inc(z_silu, 1)
        for c in range(NC):
            act.wait_ge(x_t, c + 1)
            nc.scalar.activation(x2T[:, c, :], ps[:, 2 + c % 4, 0:T], ACT.Copy).then_inc(x_s, 1)

        def take(kinds):
            for n, (kind, c) in enumerate(UNITS):
                if kind in kinds:
                    act.wait_ge(unit_t, n + 1)
                    dst = {"h": hb, "gb": gb, "ga": ga}[kind]
                    nc.scalar.activation(dst[:, c, :], ps[:, n % 2, 0:T], ACT.Copy if kind == "h" else ACT.Sigmoid).then_inc(act_s, 1)

        take(("h",))
        act.wait_ge(tr_t, 1)
        for i in range(6):
            nc.scalar.activation(trow[0:TAILS, HALF * i:HALF * i + HALF], ps[0:TAILS, 2 + i, :], ACT.Copy).then_inc(tr_s, 1)
        act.wait_ge(pt_t, 1)
        for i in range(2):
            nc.scalar.activation(prow[:, HALF * i:HALF * i + HALF], ps[0:PTAILS, 2 + i, :], ACT.Copy).then_inc(pt_s, 1)
        take(("gb",))
        act.wait_ge(out_d, 64)
        take(("ga",))

    @block.tensor
    def _(pe):
        pe.wait_ge(x_ld, 48)
        for c in range(NC):
            if c >= 4:
                pe.wait_ge(x_s, c - 3)
            for tau, (t0, n) in enumerate(TILE):
                last = nc.tensor.transpose(ps[:, 2 + c % 4, t0:t0 + n], xrow[0:n, tau, P * c:P * c + P], ident[0:n, 0:n])
            last.then_inc(x_t, 1)
        for n, (kind, c) in enumerate(UNITS):
            if (kind, c) == ("c", 0):
                pe.wait_ge(x_s, NC)
                for k in range(3 * NC):
                    last = nc.tensor.transpose(ps[0:TAILS, 2 + k // 4, P * (k % 4):P * (k % 4) + P], tails[:, k, :], ident[:])
                last.then_inc(tr_t, 1)
            if (kind, c) == ("b", 2):
                pe.wait_ge(ptail, NC)
                pe.wait_ge(tr_s, 6)
                for k in range(NC):
                    last = nc.tensor.transpose(ps[0:PTAILS, 2 + k // 4, P * (k % 4):P * (k % 4) + P], ptails[:, k, :], ident[:])
                last.then_inc(pt_t, 1)
            i, j = S_H + n // 4, n % 4
            if j == 0:
                wait_slot(pe, i)
            if n >= 2:
                wait_taken(pe, n - 2)
            if (kind, c) in (("wb", 0), ("wo", 0)):
                wait_taken(pe, n - 1 if kind == "wo" else n - NC - 1)
            if (kind, c) == ("wa", 0):
                pe.wait_ge(o_s, 1)
            rhs = {"wb": hb, "wa": oT, "wo": ga}.get(kind, hT)
            for k in range(NC):
                last = nc.tensor.matmul(ps[:, n % 2, 0:T], ring[:, i % RING1, k, P * j:P * j + P], rhs[:, k, :],
                                        start=k == 0, stop=k == NC - 1)
            last.then_inc(unit_t, 1)

    @block.vector
    def _(dve):
        def link(ins):
            order.link(dve, ins)

        dve.wait_ge(z_silu, 1)
        dve.wait_ge(halo0, 1)
        nc.vector.scalar_tensor_tensor(out=oT[:].rearrange("p h t -> p (h t)"), in0=oT[:].rearrange("p h t -> p (h t)"),
                                       scalar=gnw, in1=zT[:].rearrange("p h t -> p (h t)"), op0=ALU.mult,
                                       op1=ALU.mult).then_inc(o_s, 1)
        for n, (kind, c) in enumerate(UNITS):
            if kind in BY_ACT:
                continue
            dve.wait_ge(unit_t, n + 1)
            o = ps[:, n % 2, 0:T]
            if kind == "c":
                dve.wait_ge(act_s, c + 1)
                dve.wait_ge(halo, c + 1)
                if c >= 2:
                    dve.wait_ge(ptail, c - 1)
                e, a = ext[:, c % 2, :], acc[:, c % 2, :]
                nc.vector.tensor_tensor(e[:, SW - 1:PEXT], o[:, 0:SEQ], hb[:, c, 0:SEQ], ALU.mult)
                nc.vector.tensor_tensor(seq_view(e[:, PEXT:PW])[:, :, SW - 1:PSEXT], seq_view(o[:, SEQ:T]),
                                        seq_view(hb[:, c, SEQ:T]), ALU.mult).then_inc(pre_s, 1)
                dve.wait_ge(pre_s, c + 1)
                m = PW - SW + 1
                link(nc.vector.tensor_scalar(a[:, 0:m], e[:, 0:m], scw[:, 0, c:c + 1], None, ALU.mult))
                link(nc.vector.scalar_tensor_tensor(out=a[:, 0:m], in0=e[:, 1:m + 1], scalar=scw[:, 1, c:c + 1], in1=a[:, 0:m],
                                                    op0=ALU.mult, op1=ALU.add))
                nc.vector.scalar_tensor_tensor(out=hb[:, c, 0:SEQ], in0=e[:, 2:SEQ + 2], scalar=scw[:, 2, c:c + 1],
                                               in1=a[:, 0:SEQ], op0=ALU.mult, op1=ALU.add)
                s0 = PEXT - SW + 1
                nc.vector.scalar_tensor_tensor(out=seq_view(hb[:, c, SEQ:T]), in0=seq_view(e[:, PEXT:PW])[:, :, 2:PSEXT],
                                               scalar=scw[:, 2, c:c + 1],
                                               in1=seq_view(a[:, s0:s0 + NS * PSEXT])[:, :, SW - 1:PSEXT],
                                               op0=ALU.mult, op1=ALU.add).then_inc(dve_s, 1)
            if kind == "b":
                if c == 0:
                    dve.wait_ge(dve_s, NC)
                nc.vector.tensor_tensor(hb[:, c, :], hb[:, c, :], o, ALU.mult).then_inc(dve_s, 1)
            if kind == "wb":
                dve.wait_ge(act_s, NC + c + 1)
                nc.vector.tensor_tensor(gb[:, c, :], gb[:, c, :], o, ALU.mult).then_inc(dve_s, 1)
            if kind == "wa":
                dve.wait_ge(act_s, 2 * NC + c + 1)
                link(nc.vector.tensor_tensor(ga[:, c, :], ga[:, c, :], o, ALU.mult))
                nc.vector.tensor_tensor(ga[:, c, :], ga[:, c, :], gb[:, c, :], ALU.add).then_inc(dve_s, 1)
            if kind == "wo":
                nc.vector.scalar_tensor_tensor(out=x2T[:, c, 0:SEQ], in0=o[:, 0:SEQ], scalar=G1[:, c, 0:1],
                                               in1=x2T[:, c, 0:SEQ], op0=ALU.mult, op1=ALU.add)
                link(nc.vector.tensor_tensor(seq_view(gtmp[:, c % 2, :]), seq_view(o[:, SEQ:T]),
                                             G1[:, c, 1:NSEQ].unsqueeze(2).to_broadcast([P, NS, ST]), ALU.mult))
                nc.vector.tensor_tensor(x2T[:, c, SEQ:T], x2T[:, c, SEQ:T], gtmp[:, c % 2, :], ALU.add).then_inc(dve_s, 1)


def experts(nc, t, top, sb, sem, ring, ident, ones, causal, vecs, adaT, x2T, h2tok, order, norm, raw_full,
            load_piece, dbg, stop):
    n2w, nfw = vecs[:, 8:16], vecs[:, 16:24]
    SH2, SC2, G2 = adaT[:, 24:32, :], adaT[:, 32:40, :], adaT[:, 40:48, :]
    yacc = sb("yacc", [P, NC, T])
    route = sb("route", [P, E + 1, 2, NTILE])
    iota = sb("iota", [P, CAP])
    brow = sb("brow", [P, 2, D])
    expert_row = sb("expert_row", [P, E])
    count = sb("count", [P, E + 1], dt=I32)
    FAR = 1000.0

    def seq_view(a):
        return a.rearrange("p (s t) -> p s t", s=NS)

    with ExitStack() as st:
        ps = st.enter_context(nc.psum_tensor("ps_rt", [P, 8, 512], F32))
        h2T = sb("h2T", [P, NC, T], st)
        sq = sb("sq_r", [P, 2, T], st)
        rstd = sb("rstd_r", [P, T], st)
        gw = sb("gw_r", [P, NC, NSEQ], st)
        wr = sb("wr", [P, NC, E], st)
        br = sb("br", [P, E], st)
        strict = sb("strict", [P, P], st)
        L = sb("logits", [P, NTILE, E], st)
        m8 = sb("m8", [P, NTILE, 8], st)
        gt = sb("gt", [P, NTILE, E], st)
        eq = sb("eq", [P, NTILE, E], st)
        ceq = sb("ceq", [P, NTILE, E], st)
        need = sb("need", [P, NTILE], st)
        sel = sb("sel", [P, NTILE, E], st)
        wt = sb("wt", [P, NTILE, E], st)
        rank = sb("rank", [P, NTILE, E], st)
        zero = sb("zero32", [P, E], st)
        cmax = sb("cmax", [P, 1], st)
        whole = sb("whole", [P, 2, D], st)
        ld, h_s, hr_t, hr_s, lg_t, arg_s, exp_s, sel_s, rank_t, pk, rows_d, row_s, bias_s = (
            sem("rt_" + x) for x in ("ld", "h_s", "hr_t", "hr_s", "lg_t", "arg_s", "exp_s", "sel_s", "rank_t", "pk",
                                     "rows_d", "row_s", "bias_s"))
        sq_s, sum_t, mean_s, log_s, rs_s = norm
        block = st.enter_context(nc.Block())

        @block.gpsimd
        def _(pool):
            nc.gpsimd.iota(iota[:], pattern=[[1, CAP]], base=0, channel_multiplier=0,
                           allow_small_or_imprecise_dtypes=True).then_inc(pk, 1)
            nc.gpsimd.tensor_tensor(strict[:], causal[:], ident[:], ALU.subtract).then_inc(pk, 1)
            nc.gpsimd.memset(yacc[:], 0.0).then_inc(pk, 1)
            nc.gpsimd.memset(route[:], FAR).then_inc(pk, 1)
            nc.gpsimd.memset(expert_row[:], 0.0).then_inc(row_s, 1)
            for q in range(P // E):
                pool.wait_ge(row_s, q + 1)
                nc.gpsimd.affine_select(out=expert_row[:], in_=expert_row[:], compare_op=ALU.not_equal, fill=1.0,
                                        base=-E * q, pattern=[[-1, E]], channel_multiplier=1).then_inc(row_s, 1)

        @block.scalar
        def _(act):
            act.dma_start(wr[:], t["w_router"][0].rearrange("(c p) e -> p c e", p=P)).then_inc(ld, 16)
            act.dma_start(br[:], t["b_router"].to_broadcast([P, E])).then_inc(ld, 16)
            for q, (name, m) in enumerate((("b_gate", 0), ("b_gate", 0), ("b_up", 0), ("b_up", 0), ("b_down", 1), ("b_down", 1))):
                act.dma_start(whole[E * (q % 4):E * (q % 4) + E, m, :], t[name][0]).then_inc(rows_d, 16)
            for c in range(NC):
                if c >= 2:
                    act.wait_ge(sum_t, 1 * NC + c - 1)
                nc.scalar.activation(sq[:, c % 2, :], x2T[:, c, :], ACT.Square).then_inc(sq_s, 1)
            act.wait_ge(mean_s, 2)
            nc.scalar.activation(rstd[:], rstd[:], ACT.Ln).then_inc(log_s, 1)
            act.wait_ge(log_s, 2)
            nc.scalar.activation(rstd[:], rstd[:], ACT.Exp, scale=-0.5).then_inc(rs_s, 1)
            for tau, (t0, n) in enumerate(TILE):
                act.wait_ge(hr_t, tau + 1)
                nc.scalar.activation(h2tok[0:n, tau, :].rearrange("p (a b) -> p a b", a=2),
                                     ps[0:n, 2 * tau:2 * tau + 2, :], ACT.Copy).then_inc(hr_s, 1)
            act.wait_ge(arg_s, 1)
            nc.scalar.activation(wt[:], wt[:], ACT.Exp).then_inc(exp_s, 1)
            act.wait_ge(rows_d, 96)
            nc.scalar.activation(brow[:, 0, :].bitcast(F32R), whole[:, 0, :], ACT.Copy)
            nc.scalar.activation(brow[0:2 * E, 1, :].bitcast(F32R), whole[0:2 * E, 1, :], ACT.Copy).then_inc(bias_s, 1)

        @block.tensor
        def _(pe):
            for c in range(NC):
                pe.wait_ge(sq_s, 1 * NC + c + 1)
                nc.tensor.matmul(ps[:, 7, 0:T], ones[:], sq[:, c % 2, :], start=c == 0, stop=c == NC - 1).then_inc(sum_t, 1)
            pe.wait_ge(h_s, 1)
            pe.wait_ge(ld, 32)
            for tau, (t0, n) in enumerate(TILE):
                for k in range(NC):
                    last = nc.tensor.matmul(ps[0:n, 6, E * tau:E * tau + E], h2T[:, k, t0:t0 + n], wr[:, k, :],
                                            start=k == 0, stop=k == NC - 1)
            last.then_inc(lg_t, 1)
            for tau, (t0, n) in enumerate(TILE):
                for k in range(NC):
                    last = nc.tensor.transpose(ps[0:n, 2 * tau + k // 4, P * (k % 4):P * (k % 4) + P], h2T[:, k, t0:t0 + n],
                                               ident[:])
                last.then_inc(hr_t, 1)
            pe.wait_ge(pk, 4)
            pe.wait_ge(sel_s, 1)
            for tau, (t0, n) in enumerate(TILE):
                o = ps[0:n, 7, E * tau:E * tau + E]
                for u in range(tau):
                    nc.tensor.matmul(o, ones[:, 0:n], sel[:, u, :], start=u == 0, stop=False)
                nc.tensor.matmul(o, strict[0:n, 0:n], sel[0:n, tau, :], start=tau == 0, stop=True)
            for tau, (t0, n) in enumerate(TILE):
                last = nc.tensor.matmul(ps[:, 7, 3 * E:4 * E], ones[0:n, :], sel[0:n, tau, :], start=tau == 0, stop=tau == 2)
            last.then_inc(rank_t, 1)

        @block.vector
        def _(dve):
            def link(ins):
                order.link(dve, ins)

            def over_e(a):
                return a.unsqueeze(2).to_broadcast([P, NTILE, E])

            link(nc.vector.tensor_scalar(gw[:], SC2, 1.0, None, ALU.add))
            link(nc.vector.tensor_tensor(gw[:], gw[:], n2w.unsqueeze(2).to_broadcast([P, NC, NSEQ]), ALU.mult))
            link(nc.vector.memset(L[:], 0.0))
            link(nc.vector.memset(zero[:], 0.0))
            link(nc.vector.memset(rank[:], 0.0))
            dve.wait_ge(sum_t, 2 * NC)
            nc.vector.tensor_scalar(rstd[:], ps[:, 7, 0:T], 1.0 / D, EPS, ALU.mult, ALU.add).then_inc(mean_s, 1)
            dve.wait_ge(rs_s, 2)
            link(nc.vector.tensor_tensor(h2T[:], x2T[:], rstd[:].unsqueeze(1).to_broadcast([P, NC, T]), ALU.mult))
            for c in range(NC):
                nc.vector.tensor_scalar(h2T[:, c, 0:SEQ], h2T[:, c, 0:SEQ], gw[:, c, 0:1], SH2[:, c, 0:1], ALU.mult, ALU.add)
                link(nc.vector.tensor_tensor(seq_view(h2T[:, c, SEQ:T]), seq_view(h2T[:, c, SEQ:T]),
                                             gw[:, c, 1:NSEQ].unsqueeze(2).to_broadcast([P, NS, ST]), ALU.mult))
                ins = nc.vector.tensor_tensor(seq_view(h2T[:, c, SEQ:T]), seq_view(h2T[:, c, SEQ:T]),
                                              SH2[:, c, 1:NSEQ].unsqueeze(2).to_broadcast([P, NS, ST]), ALU.add)
            ins.then_inc(h_s, 1)
            dve.wait_ge(lg_t, 1)
            dve.wait_ge(ld, 32)
            for tau, (t0, n) in enumerate(TILE):
                ins = nc.vector.tensor_tensor(L[0:n, tau, :], ps[0:n, 6, E * tau:E * tau + E], br[0:n, :], ALU.add)
            link(ins)
            for tau in range(NTILE):
                ins = nc.vector.max(m8[:, tau, :], L[:, tau, :])
            link(ins)
            nc.vector.tensor_tensor(wt[:], L[:], over_e(m8[:, :, 0]), ALU.subtract).then_inc(arg_s, 1)
            nc.vector.tensor_tensor(gt[:], L[:], over_e(m8[:, :, TOPK - 1]), ALU.is_gt)
            link(nc.vector.tensor_tensor(eq[:], L[:], over_e(m8[:, :, TOPK - 1]), ALU.is_equal))
            nc.vector.tensor_reduce(need[:], gt[:], AX.X, ALU.add)
            for tau in range(NTILE):
                ins = nc.vector.tensor_tensor_scan(ceq[:, tau, :], eq[:, tau, :], zero[:], 0.0, ALU.add, ALU.add)
            link(ins)
            link(nc.vector.tensor_scalar(need[:], need[:], -1.0, float(TOPK), ALU.mult, ALU.add))
            link(nc.vector.tensor_tensor(ceq[:], ceq[:], over_e(need[:]), ALU.is_le))
            link(nc.vector.tensor_tensor(eq[:], eq[:], ceq[:], ALU.mult))
            nc.vector.tensor_tensor(sel[:], gt[:], eq[:], ALU.add).then_inc(sel_s, 1)
            dve.wait_ge(sel_s, 1)
            dve.wait_ge(exp_s, 1)
            link(nc.vector.tensor_tensor(wt[:], wt[:], sel[:], ALU.mult))
            link(nc.vector.tensor_reduce(need[:], wt[:], AX.X, ALU.add))
            link(nc.vector.reciprocal(need[:], need[:]))
            dve.wait_ge(pk, 4)
            for tau in range(NTILE):
                nc.vector.tensor_scalar(route[:, 0:E, 1, tau], wt[:, tau, :], need[:, tau:tau + 1], None, ALU.mult)
            dve.wait_ge(rank_t, 1)
            for tau, (t0, n) in enumerate(TILE):
                ins = nc.vector.tensor_scalar(rank[0:n, tau, :], ps[0:n, 7, E * tau:E * tau + E], -FAR, None, ALU.add)
            link(ins)
            link(nc.vector.tensor_tensor(rank[:], rank[:], sel[:], ALU.mult))
            for tau in range(NTILE):
                nc.vector.tensor_scalar(route[:, 0:E, 0, tau], rank[:, tau, :], FAR, None, ALU.add)
            nc.vector.tensor_copy(count[:, 0:E], ps[:, 7, 3 * E:4 * E])
            link(nc.vector.tensor_reduce(cmax[:], ps[:, 7, 3 * E:4 * E], AX.X, ALU.max))
            link(nc.vector.tensor_copy(count[:, E:E + 1], cmax[:]))
            dve.wait_ge(bias_s, 1)
            for r0, m in ((E, 0), (3 * E, 0), (E, 1)):
                rows = slice(r0, r0 + E)
                nc.vector.tensor_tensor(brow[rows, m, :].bitcast(F32R), whole[rows, m, :], brow[rows, m, :], ALU.subtract)

    if "route" in dbg:
        dump(nc, sem("dbg_route"), dbg["route"], route[:])
    if stop <= 4:
        return

    with ExitStack() as st:
        ps = st.enter_context(nc.psum_tensor("ps_moe", [P, 8, 512], F32))
        high = sb("high", [P, SPLIT, QUART, HALF], st)
        low = sb("low", [P, SPLIT, QUART, HALF], st)
        xh = sb("xh", [P, NC, CAP], st)
        xl = sb("xl", [P, NC, CAP], st)
        hh = sb("hh", [P, D], st)
        hl = sb("hl", [P, D], st)
        gate, sig, hid, yrow = (ring[:, RING1 - 1, 2 * n:2 * n + 2, :].rearrange("p a n -> p (a n)") for n in range(4))
        pick = sb("pick", [P, NTILE, CAP], st)
        wpick = sb("wpick", [P, NTILE, CAP], st)
        put = sb("put", [P, T], st)
        chosen = sb("chosen", [P, P], st)
        cur = sb("cur", [P, 2, NTILE], st)
        nxt = sb("nxt", [P, NTILE], st)
        (pick_s, wpick_s, gath_t, xh_s, x_s, high_s, low_s, piece_t, gate_s, sig_s, hid_s, hidT_t, hh_s, hl_s, yrow_s,
         put_t, put_s, comb_t, comb_s, ech, chosen_s) = (sem("ex_" + x) for x in (
             "pick_s", "wpick_s", "gath_t", "xh_s", "x_s", "high_s", "low_s", "piece_t", "gate_s", "sig_s", "hid_s",
             "hidT_t", "hh_s", "hl_s", "yrow_s", "put_t", "put_s", "comb_t", "comb_s", "ech", "chosen_s"))

        def r(a):
            return a.bitcast(F32R)

        def run_pass(eng, b, body):
            body(b * E, 0, b, True)
            with eng.Fori(1, E) as e:
                body(b * E + e, e, b, False)

        def over_passes(eng, body, prologue, epilogue):
            prologue(0)
            run_pass(eng, 0, body)
            epilogue(0)
            most = eng.value_load(count[0:1, E:E + 1], min_val=0, max_val=T)
            for b in range(1, (T + CAP - 1) // CAP):
                with eng.If(most > CAP * b):
                    prologue(b)
                    run_pass(eng, b, body)
                    epilogue(b)

        block = st.enter_context(nc.Block())

        @block.sync
        def _(sp):
            def body(i, e, b, first):
                for p in range(RAW if first and b == 0 else 0, PIECES):
                    sp.wait_ge(low_s, PIECES * i + p - RAW + 1)
                    load_piece(sp, e, p)

            over_passes(sp, body, lambda b: None, lambda b: None)

        @block.scalar
        def _(act):
            def body(i, e, b, first):
                start = first and b == 0

                def round_piece(p):
                    act.wait_ge(raw_full[p % RAW], 16 * (PIECES // RAW * i + p // RAW + 1))
                    if not start or p >= SPLIT:
                        act.wait_ge(piece_t, PIECES * i + p + 1 - SPLIT)
                    nc.scalar.activation(r(high[:, p % SPLIT]), raw_piece(ring, p), ACT.Copy).then_inc(high_s, 1)

                act.wait_ge(gath_t, i + b + 1)
                if not start:
                    act.wait_ge(piece_t, PIECES * (i - 1) + 8)
                nc.scalar.activation(r(xh[:]).rearrange("p (a c) n -> p a (c n)", a=2), ps[:, 2:4, :], ACT.Copy).then_inc(xh_s, 1)
                for p in range(3):
                    round_piece(p)
                if not first:
                    take_rows(i - 1)
                for p in range(3, 8):
                    round_piece(p)
                for a in range(2):
                    act.wait_ge(gate_s, 2 * i + a + 1)
                    half = slice(HALF * a, HALF * a + HALF)
                    nc.scalar.activation(sig[:, half], gate[:, half], ACT.Sigmoid, scale=ALPHA).then_inc(sig_s, 1)
                for p in range(8, 11):
                    round_piece(p)
                for a in range(2):
                    act.wait_ge(hidT_t, 2 * i + a + 1)
                    nc.scalar.activation(r(hh[:, HALF * a:HALF * a + HALF]), ps[:, a, :], ACT.Copy).then_inc(hh_s, 1)
                round_piece(11)

            def take_rows(i):
                act.wait_ge(piece_t, PIECES * i + PIECES)
                nc.scalar.activation(yrow.rearrange("p (a n) -> p a n", a=2), ps[:, 4:6, :], ACT.Copy).then_inc(yrow_s, 1)
                act.wait_ge(put_t, i + 1)
                nc.scalar.activation(put[:], ps[:, 2, 0:T], ACT.Copy).then_inc(put_s, 1)

            over_passes(act, body, lambda b: None, lambda b: take_rows(b * E + E - 1))

        @block.tensor
        def _(pe):
            def gather(i):
                pe.wait_ge(pick_s, i + 1)
                for c in range(NC):
                    for tau, (t0, n) in enumerate(TILE):
                        last = nc.tensor.matmul(ps[:, 2 + c // 4, CAP * (c % 4):CAP * (c % 4) + CAP],
                                                h2tok[0:n, tau, P * c:P * c + P], pick[0:n, tau, :],
                                                start=tau == 0, stop=tau == NTILE - 1)
                last.then_inc(gath_t, 1)

            def half(i, j, bank, high_x, low_x):
                m, a = j // 2, j % 2
                rows = slice(64, 128) if m == 1 else slice(0, 64)
                for q in range(2):
                    pe.wait_ge(low_s, PIECES * i + 2 * j + q + 1)
                    hb, lb = high[:, (2 * j + q) % SPLIT], low[:, (2 * j + q) % SPLIT]
                    for k in range(QUART):
                        c = P * (QUART * q + k)
                        nc.tensor.matmul(ps[:, bank, :], r(high_x[:, c:c + P]), r(hb[:, k, :]), start=c == 0, stop=False)
                        nc.tensor.matmul(ps[:, bank, :], r(low_x[:, c:c + P]), r(hb[:, k, :]), start=False, stop=False)
                        last = nc.tensor.matmul(ps[:, bank, :], r(high_x[:, c:c + P]), r(lb[:, k, :]), start=False, stop=False)
                    if q == 1:
                        if j == 0:
                            pe.wait_ge(chosen_s, i + 1)
                        last = nc.tensor.matmul(ps[:, bank, :], r(chosen[rows, :]),
                                                r(brow[rows, m // 2, HALF * a:HALF * a + HALF]), start=False, stop=True)
                    last.then_inc(piece_t, 1)

            def scatter_matrix(i):
                pe.wait_ge(wpick_s, i + 1)
                for tau, (t0, n) in enumerate(TILE):
                    last = nc.tensor.transpose(ps[:, 2, t0:t0 + n], wpick[0:n, tau, :], ident[0:n, 0:n])
                last.then_inc(put_t, 1)

            def combine(i, a):
                pe.wait_ge(yrow_s, i + 1)
                pe.wait_ge(put_s, i + 1)
                for c in range(4 * a, 4 * a + 4):
                    if c >= 4:
                        pe.wait_ge(comb_s, NC * i + c - 3)
                    nc.tensor.matmul(ps[:, 4 + c % 4, 0:T], yrow[:, P * c:P * c + P], put[:], start=True,
                                     stop=True).then_inc(comb_t, 1)

            def body(i, e, b, first):
                start = first and b == 0
                xf = [x[:].rearrange("p c n -> p (c n)") for x in (xh, xl)]
                pe.wait_ge(x_s, i + 1)
                if not first:
                    scatter_matrix(i - 1)
                if not start:
                    pe.wait_ge(hh_s, 2 * i)
                half(i, 0, 0, *xf)
                half(i, 1, 1, *xf)
                if not first:
                    pe.wait_ge(put_s, i)
                half(i, 2, 2, *xf)
                if not first:
                    combine(i - 1, 0)
                half(i, 3, 3, *xf)
                if not first:
                    combine(i - 1, 1)
                for a in range(2):
                    pe.wait_ge(hid_s, 2 * i + a + 1)
                    for c in range(4):
                        last = nc.tensor.transpose(ps[:, a, P * c:P * c + P],
                                                   hid[:, HALF * a + P * c:HALF * a + P * c + P], ident[:])
                    last.then_inc(hidT_t, 1)
                gather(i + b + 1)
                if not first:
                    pe.wait_ge(comb_s, NC * i)
                pe.wait_ge(hl_s, 2 * i + 2)
                half(i, 4, 4, hh, hl)
                half(i, 5, 5, hh, hl)

            def prologue(b):
                if b:
                    pe.wait_ge(put_s, b * E)
                gather(b * (E + 1))

            def epilogue(b):
                scatter_matrix(b * E + E - 1)
                combine(b * E + E - 1, 0)
                combine(b * E + E - 1, 1)

            over_passes(pe, body, prologue, epilogue)

        @block.vector
        def _(dve):
            def picks(i, e, b, link_no):
                if not isinstance(i, int) or i > 0:
                    dve.wait_ge(gath_t, i)
                nc.vector.tensor_scalar(nxt[:], route[:, e, 0, :], float(-CAP * b), None, ALU.add).then_inc(ech, 1)
                dve.wait_ge(ech, link_no)
                for tau in range(NTILE):
                    ins = nc.vector.tensor_scalar(pick[:, tau, :], iota[:], nxt[:, tau:tau + 1], None, ALU.is_equal)
                ins.then_inc(pick_s, 1)

            def add_up(i, a):
                for c in range(4 * a, 4 * a + 4):
                    dve.wait_ge(comb_t, NC * i + c + 1)
                    nc.vector.tensor_tensor(yacc[:, c, :], yacc[:, c, :], ps[:, 4 + c % 4, 0:T], ALU.add).then_inc(comb_s, 1)

            def body(i, e, b, first):
                start = first and b == 0
                chain = b + 1 + LINKS * i

                def left(p):
                    dve.wait_ge(high_s, PIECES * i + p + 1)
                    nc.vector.tensor_tensor(r(low[:, p % SPLIT]), raw_piece(ring, p), high[:, p % SPLIT], ALU.subtract).then_inc(low_s, 1)

                dve.wait_ge(xh_s, i + 1)
                nc.vector.tensor_tensor(r(xl[:]).rearrange("p (a c) n -> p a (c n)", a=2), ps[:, 2:4, :],
                                        xh[:].rearrange("p (a c) n -> p a (c n)", a=2), ALU.subtract).then_inc(x_s, 1)
                for p in range(3):
                    left(p)
                if not start:
                    dve.wait_ge(piece_t, PIECES * i)
                nc.vector.tensor_scalar(r(chosen[:]), ones[:], expert_row[:, bass.ds(e, 1)], None, ALU.mult).then_inc(chosen_s, 1)
                for p in range(3, 7):
                    left(p)
                for a in range(2):
                    dve.wait_ge(piece_t, PIECES * i + 2 * a + 2)
                    nc.vector.tensor_scalar(gate[:, HALF * a:HALF * a + HALF], ps[:, a, :], LIMIT, None, ALU.min).then_inc(gate_s, 1)
                left(7)
                picks(i + b + 1, e + 1, b, chain + 1)
                left(8)
                for a in range(2):
                    half = slice(HALF * a, HALF * a + HALF)
                    dve.wait_ge(piece_t, PIECES * i + 2 * a + 6)
                    nc.vector.tensor_scalar(hid[:, half], ps[:, 2 + a, :], LIMIT, -LIMIT, ALU.min, ALU.max)
                    dve.wait_ge(sig_s, 2 * i + a + 1)
                    nc.vector.tensor_tensor(gate[:, half], gate[:, half], sig[:, half], ALU.mult).then_inc(ech, 1)
                    dve.wait_ge(ech, chain + 2 + a)
                    nc.vector.scalar_tensor_tensor(out=hid[:, half], in0=hid[:, half], scalar=1.0, in1=gate[:, half],
                                                   op0=ALU.add, op1=ALU.mult).then_inc(hid_s, 1)
                    if not first:
                        add_up(i - 1, a)
                    if a == 0:
                        left(9)
                if not start:
                    dve.wait_ge(put_t, i)
                nc.vector.tensor_scalar(cur[:, 1, :], route[:, e, 1, :], 1.0, None, ALU.mult)
                nc.vector.tensor_scalar(cur[:, 0, :], route[:, e, 0, :], float(-CAP * b), None, ALU.add).then_inc(ech, 1)
                for a in range(2):
                    dve.wait_ge(hh_s, 2 * i + a + 1)
                    half = slice(HALF * a, HALF * a + HALF)
                    nc.vector.tensor_tensor(r(hl[:, half]), ps[:, a, :], hh[:, half], ALU.subtract).then_inc(hl_s, 1)
                dve.wait_ge(ech, chain + 4)
                for p in range(10, 12):
                    left(p)
                for tau in range(NTILE):
                    ins = nc.vector.tensor_scalar(wpick[:, tau, :], iota[:], cur[:, 0, tau:tau + 1], cur[:, 1, tau:tau + 1],
                                                  ALU.is_equal, ALU.mult)
                ins.then_inc(wpick_s, 1)

            def last_sums(b):
                for a in range(2):
                    add_up(b * E + E - 1, a)

            over_passes(dve, body, lambda b: picks(b * (E + 1), 0, b, b + LINKS * b * E + 1), last_sums)

    if "yacc" in dbg:
        dump(nc, sem("dbg_yacc"), dbg["yacc"], yacc[:])
    with ExitStack() as st:
        ps = st.enter_context(nc.psum_tensor("ps_fin", [P, 8, 512], F32))
        sq = sb("sq_f", [P, 2, T], st)
        rstd = sb("rstd_f", [P, T], st)
        yrows = sb("yrows", [P, NTILE, D], st)
        x_s, y_s, yt_t, yo_s, out_d = (sem("fn_" + x) for x in ("x_s", "y_s", "yt_t", "yo_s", "out_d"))
        sq_s, sum_t, mean_s, log_s, rs_s = norm
        block = st.enter_context(nc.Block())

        @block.vector
        def _(dve):
            for c in range(NC):
                nc.vector.scalar_tensor_tensor(out=x2T[:, c, 0:SEQ], in0=yacc[:, c, 0:SEQ], scalar=G2[:, c, 0:1],
                                               in1=x2T[:, c, 0:SEQ], op0=ALU.mult, op1=ALU.add)
                nc.vector.tensor_tensor(seq_view(yacc[:, c, SEQ:T]), seq_view(yacc[:, c, SEQ:T]),
                                        G2[:, c, 1:NSEQ].unsqueeze(2).to_broadcast([P, NS, ST]), ALU.mult).then_inc(order.semaphore, 1)
                order.count += 1
                dve.wait_ge(order.semaphore, order.count)
                nc.vector.tensor_tensor(x2T[:, c, SEQ:T], x2T[:, c, SEQ:T], yacc[:, c, SEQ:T], ALU.add).then_inc(x_s, 1)
            dve.wait_ge(sum_t, 3 * NC)
            nc.vector.tensor_scalar(rstd[:], ps[:, 7, 0:T], 1.0 / D, EPS, ALU.mult, ALU.add).then_inc(mean_s, 1)
            dve.wait_ge(rs_s, 3)
            for c in range(NC):
                nc.vector.scalar_tensor_tensor(out=x2T[:, c, :], in0=x2T[:, c, :], scalar=nfw[:, c:c + 1], in1=rstd[:],
                                               op0=ALU.mult, op1=ALU.mult).then_inc(y_s, 1)

        @block.scalar
        def _(act):
            for c in range(NC):
                act.wait_ge(x_s, c + 1)
                if c >= 2:
                    act.wait_ge(sum_t, 2 * NC + c - 1)
                nc.scalar.activation(sq[:, c % 2, :], x2T[:, c, :], ACT.Square).then_inc(sq_s, 1)
            act.wait_ge(mean_s, 3)
            nc.scalar.activation(rstd[:], rstd[:], ACT.Ln).then_inc(log_s, 1)
            act.wait_ge(log_s, 3)
            nc.scalar.activation(rstd[:], rstd[:], ACT.Exp, scale=-0.5).then_inc(rs_s, 1)
            for tau, (t0, n) in enumerate(TILE):
                act.wait_ge(yt_t, tau + 1)
                nc.scalar.activation(yrows[0:n, tau, :].rearrange("p (a b) -> p a b", a=2), ps[0:n, 2 * tau:2 * tau + 2, :],
                                     ACT.Copy).then_inc(yo_s, 1)

        @block.tensor
        def _(pe):
            for c in range(NC):
                pe.wait_ge(sq_s, 2 * NC + c + 1)
                nc.tensor.matmul(ps[:, 7, 0:T], ones[:], sq[:, c % 2, :], start=c == 0, stop=c == NC - 1).then_inc(sum_t, 1)
            for tau, (t0, n) in enumerate(TILE):
                for k in range(NC):
                    if tau == 0:
                        pe.wait_ge(y_s, k + 1)
                    last = nc.tensor.transpose(ps[0:n, 2 * tau + k // 4, P * (k % 4):P * (k % 4) + P], x2T[:, k, t0:t0 + n],
                                               ident[:])
                last.then_inc(yt_t, 1)

        @block.sync
        def _(sp):
            for tau in range(2):
                sp.wait_ge(yo_s, tau + 1)
                sp.dma_start(t["y_prompt"][0, P * tau:P * tau + P, :], yrows[:, tau, :]).then_inc(out_d, 16)
            sp.wait_ge(yo_s, 3)
            sp.dma_start(t["y_sample"].rearrange("s t d -> (s t) d"), yrows[0:64, 2, :]).then_inc(out_d, 16)
            sp.wait_ge(out_d, 48)


def raw_piece(ring, p):
    s = p % RAW
    return ring[:, s // 2, QUART * (s % 2):QUART * (s % 2) + QUART, :]


def dump(nc, s, dst, src):
    with nc.Block() as block:
        @block.sync
        def _(sp):
            sp.dma_start(dst, src).then_inc(s, 16)
            sp.wait_ge(s, 16)


INS = ["x_prompt", "x_sample", "c_prompt", "c_sample", "state_gdn_conv", "state_gdn_rec", "state_sc_conv", "w_ada",
       "b_ada", "norm1_w", "w_in", "gdn_conv_w", "gdn_a_log", "gdn_dt_bias", "gdn_norm_w", "w_branch_a", "sc_conv_w",
       "w_branch_b", "w_out", "norm2_w", "w_router", "b_router", "w_gate", "b_gate", "w_up", "b_up", "w_down",
       "b_down", "final_norm_w"]
OUTS = [("y_prompt", (1, SEQ, D)), ("y_sample", (NS, ST, D)), ("conv_prompt", (1, 1, 3, QKV)),
        ("rec_prompt", (1, 1, H, P, P)), ("sc_prompt", (1, 1, 2, D)), ("conv_sample", (1, NS, 3, QKV)),
        ("rec_sample", (1, NS, H, P, P)), ("sc_sample", (1, NS, 2, D))]


def kernel(**inputs):
    import numpy as np
    import concourse.bacc as bacc
    from concourse.bass_utils import run_bass_kernel_spmd

    nc = bacc.Bacc("TRN2", target_bir_lowering=False, num_devices=1)
    arrays, t = {}, {}
    for name in INS:
        arrays["in_" + name] = np.ascontiguousarray(inputs[name])
        t[name] = nc.dram_tensor("in_" + name, arrays["in_" + name].shape, F32, kind="ExternalInput").ap()
    for name, shape in OUTS:
        t[name] = nc.dram_tensor("out_" + name, shape, F32, kind="ExternalOutput").ap()
    build(nc, t)
    r = run_bass_kernel_spmd(nc, [arrays], core_ids=[0])
    return tuple(r.results[0]["out_" + name] for name, _ in OUTS)
```

```python
from contextlib import ExitStack

import concourse.bass as bass
from concourse import mybir

F32 = mybir.dt.float32
F32R = mybir.dt.float32r
I32 = mybir.dt.int32
ALU = mybir.AluOpType
ACT = mybir.ActivationFunctionType
AX = mybir.AxisListType

P = 128
D = 1024
NC = D // P
SEQ = 256
NS = 8
ST = 8
T = SEQ + NS * ST
H = 8
QKV = 3 * D
E = 32
TOPK = 4
NSEQ = 1 + NS
EPS = 1e-6
LIMIT = 7.0
ALPHA = 1.702
NTILE = 3
TILE = [(0, 128), (128, 128), (256, 64)]
KW = 4
EXT = SEQ + KW - 1
SEXT = ST + KW - 1
EW = EXT + NS * SEXT
SW = 3
PEXT = SEQ + SW - 1
PSEXT = ST + SW - 1
PW = PEXT + NS * PSEXT
TAILS = 3 * NSEQ
PTAILS = 2 * NSEQ
HALF = 512
RING1 = 4
C_AB, C_B, C_C, C_H, C_GA, C_GB = 4096, 4112, 5136, 6160, 7184, 8208
LEVELS = 7
SLEVELS = 3
CAP = 128
QUART = NC // 2
PIECES = 3 * 2 * 2
RAW = 6
SPLIT = 4
LINKS = 4

ADA1 = [("ada", n * HALF) for n in range(4)]
QKVS = [("in", c * HALF) for c in (2, 3, 0, 1, 4, 5)]
ZS = [("in", 3072), ("in", 3584)]
ADA2 = [("ada", n * HALF) for n in range(4, 12)]
HS = [("in", C_H), ("in", C_H + HALF)]
CS = [("in", C_C), ("in", C_C + HALF)]
BS = [("in", C_B), ("in", C_B + HALF)]
GBS = [("in", C_GB), ("in", C_GB + HALF)]
WBS = [("wb", 0), ("wb", HALF)]
GAS = [("in", C_GA), ("in", C_GA + HALF)]
WAS = [("wa", 0), ("wa", HALF)]
WOS = [("wo", 0), ("wo", HALF)]
SLOTS = ADA1 + QKVS + ZS + ADA2 + HS + CS + BS + GBS + WBS + GAS + WAS + WOS
S_QKV, S_Z = 4, 10
S_ADA2 = 12
S_H = 20
S_GB = 26
NSLOT1 = len(SLOTS)
assert NSLOT1 == 36 and (NSLOT1 - S_ADA2) % (RING1 - 1) == 0


def place(i):
    return i % RING1 if i < S_ADA2 else (i - S_ADA2) % (RING1 - 1)


def before(i):
    return i - RING1 if i < S_ADA2 + RING1 - 1 else i - (RING1 - 1)


def loads(i):
    return sum(place(j) == place(i) for j in range(i + 1))


class Order:

    def __init__(self, semaphore):
        self.semaphore, self.count = semaphore, 0

    def link(self, engine, instruction):
        self.count += 1
        instruction.then_inc(self.semaphore, 1)
        engine.wait_ge(self.semaphore, self.count)


def build(nc, t):
    with ExitStack() as top:
        def sb(name, shape, stack=top, dt=F32):
            return stack.enter_context(nc.sbuf_tensor(name, shape, dt))

        sems = {}

        def sem(name):
            if name not in sems:
                sems[name] = top.enter_context(nc.semaphore(name))
            return sems[name]

        order = Order(sem("vector_order"))
        norm = [sem("norm_" + x) for x in ("square", "sum", "mean", "log", "rstd")]
        ring = sb("ring", [P, RING1, NC, HALF])
        ident = sb("ident", [P, P])
        ones = sb("ones", [P, P])
        causal = sb("causal", [P, P])
        scausal = sb("scausal", [64, 64])
        sblock = sb("sblock", [64, NS])
        ssame = sb("ssame", [64, 64])
        vecs = sb("vecs", [P, 193])
        adaT = sb("adaT", [P, 48, NSEQ])
        work = sb("work", [P, 6 * 1024])
        gbuf = work[:].rearrange("p (k a n) -> p k a n", k=6, a=2)
        x2T = work[:, 0:NC * T].rearrange("p (c t) -> p c t", c=NC)
        rows_of = work[:, NC * T:NC * T + NTILE * D].rearrange("p (a d) -> p a d", a=NTILE)
        slot_full = [sem(f"slot_full{r}") for r in range(RING1)]
        raw_full = [sem(f"raw_full{r}") for r in range(RAW)]
        ada_t, raw_t, z_t, ada2_t, unit_t = (sem(x) for x in ("ada_t", "raw_t", "z_t", "ada2_t", "unit_t"))

        n1w = vecs[:, 0:8]
        gnw = vecs[:, 24:25]
        convw = vecs[:, 25:121].rearrange("p (j c) -> p j c", j=KW)
        scw = vecs[:, 121:145].rearrange("p (j c) -> p j c", j=SW)
        bada = vecs[:, 145:193]
        A_SH1, A_SC1 = adaT[:, 0:8, :], adaT[:, 8:16, :]

        w_in = t["w_in"][0]
        dram = {"ada": t["w_ada"][0], "in": w_in, "wb": t["w_branch_b"][0], "wa": t["w_branch_a"][0],
                "wo": t["w_out"][0]}

        def slot_done(i):
            if i < S_QKV:
                return ada_t, i + 1
            if i < S_Z:
                return raw_t, 4 * (i - S_QKV + 1)
            if i < S_ADA2:
                return z_t, 4 * (i - S_Z + 1)
            if i < S_H:
                return ada2_t, i - S_ADA2 + 1
            return unit_t, 4 * (i - S_H + 1)

        def load_slot(sp, i):
            kind, n0 = SLOTS[i]
            r = place(i)
            if i >= RING1:
                sp.wait_ge(*slot_done(before(i)))
            src = dram[kind][:, n0:n0 + HALF].rearrange("(c p) n -> p c n", p=P)
            sp.dma_start(ring[:, r], src).then_inc(slot_full[r], 16)

        def load_piece(sp, e, p):
            name, a, q = ("w_gate", "w_up", "w_down")[p // 4], p // 2 % 2, p % 2
            src = t[name][0, e, QUART * P * q:QUART * P * (q + 1), HALF * a:HALF * a + HALF].rearrange("(c p) n -> p c n", p=P)
            sp.dma_start(raw_piece(ring, p), src).then_inc(raw_full[p % RAW], 16)

        def wait_slot(pe, i):
            pe.wait_ge(slot_full[place(i)], 16 * loads(i))

        with ExitStack() as st12:
            hT = sb("hT", [P, NC, T], st12)
            cT = sb("cT", [P, NC, NSEQ], st12)
            ptails = sb("ptails", [P, NC, PTAILS], st12)
            spare = ring[:, RING1 - 1].rearrange("p c n -> p (c n)")
            short = (spare[:, 0:NC * T].rearrange("p (c t) -> p c t", c=NC),
                     spare[:, NC * T:NC * T + 2 * PW].rearrange("p (a n) -> p a n", a=2),
                     spare[:, NC * T + 2 * PW:NC * T + 4 * PW].rearrange("p (a n) -> p a n", a=2), ptails)
            gst = sb("gst", [P, 3 * NC, 3 * NS], st12)
            sst = sb("sst", [P, NC, 2 * NS], st12)
            wab = sb("wab", [P, NC, 16], st12)
            par = sb("par", [P, 2, H], st12)
            states = sb("states", [P, H, NS, P], st12)
            ld_w = sem("ld_w")
            with ExitStack() as st:
                ps = st.enter_context(nc.psum_tensor("ps_pro", [P, 8, 512], F32))
                xrow = sb("xrow", [P, NTILE, D], st)
                crow = sb("crow", [NSEQ, D], st)
                vrow1 = sb("vrow1", [121, P], st)
                vrow2 = sb("vrow2", [72, P], st)
                gstrow = sb("gstrow", [3 * NS, QKV], st)
                sstrow = sb("sstrow", [2 * NS, D], st)
                xT = sb("xT", [P, NC, T], st)
                sq = sb("sq", [P, 2, T], st)
                rstd = sb("rstd", [P, T], st)
                gw = sb("gw", [P, NC, NSEQ], st)
                arow = sb("arow", [NSEQ, 4, HALF], st)
                arow_s, adaT_t = sem("arow_s"), sem("adaT_t")
                ld_c, ld_v, ld_x, ld_s = (sem(f"ld_{n}") for n in "cvxs")
                k_ones, k_ident, k_masks = sem("k_ones"), sem("k_ident"), sem("k_masks")
                silu_c, vec_t, vec_s, c_sb = sem("silu_c"), sem("vec_t"), sem("vec_s"), sem("c_sb")
                st_t, st_s = sem("st_t"), sem("st_s")
                x_t, x_s = sem("x_t"), sem("x_s")
                sq_s, sum_t, mean_s, log_s, rstd_s = norm
                block = st.enter_context(nc.Block())

                @block.sync
                def _(sp):
                    sp.dma_start(crow[0:1, :], t["c_prompt"]).then_inc(ld_c, 16)
                    sp.dma_start(crow[1:NSEQ, :], t["c_sample"]).then_inc(ld_c, 16)
                    rows = lambda a: a.rearrange("a (c p) -> (a c) p", p=P)
                    sp.dma_start(vrow1[0:8, :], rows(t["norm1_w"])).then_inc(ld_v, 16)
                    sp.dma_start(vrow1[8:16, :], rows(t["norm2_w"])).then_inc(ld_v, 16)
                    sp.dma_start(vrow1[16:24, :], t["final_norm_w"].rearrange("(c p) -> c p", p=P)).then_inc(ld_v, 16)
                    sp.dma_start(vrow1[24:25, :], t["gdn_norm_w"]).then_inc(ld_v, 16)
                    sp.dma_start(vrow1[25:121, :], rows(t["gdn_conv_w"][0])).then_inc(ld_v, 16)
                    sp.dma_start(vrow2[0:24, :], rows(t["sc_conv_w"][0])).then_inc(ld_v, 16)
                    sp.dma_start(vrow2[24:72, :], rows(t["b_ada"])).then_inc(ld_v, 16)
                    for tau in range(2):
                        sp.dma_start(xrow[:, tau, :], t["x_prompt"][0, P * tau:P * tau + P, :]).then_inc(ld_x, 16)
                    sp.dma_start(xrow[0:64, 2, :], t["x_sample"].rearrange("s t d -> (s t) d")).then_inc(ld_x, 16)
                    for i in range(4):
                        load_slot(sp, i)
                    sp.dma_start(gstrow[:], t["state_gdn_conv"][0].rearrange("s j c -> (s j) c")).then_inc(ld_s, 16)
                    sp.dma_start(sstrow[:], t["state_sc_conv"][0].rearrange("s j c -> (s j) c")).then_inc(ld_s, 16)
                    sp.dma_start(wab[:], t["w_in"][0][:, C_AB:C_AB + 16].rearrange("(c p) n -> p c n", p=P)).then_inc(ld_w, 16)
                    sp.dma_start(par[:, 0, :], t["gdn_a_log"].to_broadcast([P, H])).then_inc(ld_w, 16)
                    sp.dma_start(par[:, 1, :], t["gdn_dt_bias"].to_broadcast([P, H])).then_inc(ld_w, 16)
                    for i in range(4, 8):
                        load_slot(sp, i)

                @block.gpsimd
                def _(pool):
                    nc.gpsimd.memset(ones[:], 1.0).then_inc(k_ones, 1)
                    nc.gpsimd.memset(ident[:], 0.0).then_inc(k_ones, 1)
                    nc.gpsimd.memset(causal[:], 1.0).then_inc(k_ones, 1)
                    nc.gpsimd.memset(sblock[:], 1.0).then_inc(k_ones, 1)
                    pool.wait_ge(k_ones, 4)
                    nc.gpsimd.affine_select(out=ident[:], in_=ident[:], compare_op=ALU.not_equal, fill=1.0,
                                            base=0, pattern=[[-1, P]], channel_multiplier=1).then_inc(k_ident, 1)
                    nc.gpsimd.affine_select(out=causal[:], in_=causal[:], compare_op=ALU.is_ge, fill=0.0,
                                            base=0, pattern=[[1, P]], channel_multiplier=-1).then_inc(k_masks, 1)
                    nc.gpsimd.affine_select(out=sblock[:], in_=sblock[:], compare_op=ALU.is_ge, fill=0.0,
                                            base=0, pattern=[[-ST, NS]], channel_multiplier=1).then_inc(k_masks, 1)
                    pool.wait_ge(k_masks, 2)
                    nc.gpsimd.affine_select(out=sblock[:], in_=sblock[:], compare_op=ALU.is_ge, fill=0.0,
                                            base=ST - 1, pattern=[[ST, NS]], channel_multiplier=-1).then_inc(k_masks, 1)
                    pool.wait_ge(k_masks, 3)
                    nc.gpsimd.tensor_copy(ssame[:].rearrange("p (s t) -> p s t", s=NS),
                                          sblock[:].unsqueeze(2).to_broadcast([64, NS, ST])).then_inc(k_masks, 1)
                    pool.wait_ge(k_masks, 4)
                    nc.gpsimd.tensor_tensor(scausal[:], ssame[:], causal[0:64, 0:64], ALU.mult).then_inc(k_masks, 1)

                @block.scalar
                def _(act):
                    act.wait_ge(ld_c, 32)
                    nc.scalar.activation(crow[:], crow[:], ACT.Silu).then_inc(silu_c, 1)
                    for c in range(NC):
                        act.wait_ge(x_t, c + 1)
                        if c >= 2:
                            act.wait_ge(sum_t, c - 1)
                        nc.scalar.activation(xT[:, c, :], ps[:, 3 + c % 4, 0:T], ACT.Copy).then_inc(x_s, 1)
                        nc.scalar.activation(sq[:, c % 2, :], ps[:, 3 + c % 4, 0:T], ACT.Square).then_inc(sq_s, 1)
                    act.wait_ge(mean_s, 1)
                    nc.scalar.activation(rstd[:], rstd[:], ACT.Ln).then_inc(log_s, 1)
                    act.wait_ge(log_s, 1)
                    nc.scalar.activation(rstd[:], rstd[:], ACT.Exp, scale=-0.5).then_inc(rstd_s, 1)
                    for i in range(4):
                        act.wait_ge(ada_t, i + 1)
                        nc.scalar.activation(arow[:, i, :], ps[0:NSEQ, 1 + i % 2, :], ACT.Copy).then_inc(arow_s, 1)

                @block.tensor
                def _(pe):
                    pe.wait_ge(k_ident, 1)
                    pe.wait_ge(ld_v, 7 * 16)
                    nc.tensor.transpose(ps[:, 0, 0:121], vrow1[:], ident[0:121, 0:121])
                    nc.tensor.transpose(ps[:, 0, 121:193], vrow2[:], ident[0:72, 0:72]).then_inc(vec_t, 1)
                    pe.wait_ge(silu_c, 1)
                    for c in range(NC):
                        last = nc.tensor.transpose(ps[:, 0, 256 + NSEQ * c:256 + NSEQ * c + NSEQ],
                                                   crow[:, P * c:P * c + P], ident[0:NSEQ, 0:NSEQ])
                    last.then_inc(vec_t, 1)
                    pe.wait_ge(ld_x, 48)
                    pe.wait_ge(k_ones, 4)

                    def add_square(c):
                        pe.wait_ge(sq_s, c + 1)
                        nc.tensor.matmul(ps[:, 7, 0:T], ones[:], sq[:, c % 2, :], start=c == 0,
                                         stop=c == NC - 1).then_inc(sum_t, 1)

                    for c in range(NC):
                        if c >= 4:
                            pe.wait_ge(sq_s, c - 3)
                        for tau, (t0, n) in enumerate(TILE):
                            last = nc.tensor.transpose(ps[:, 3 + c % 4, t0:t0 + n], xrow[0:n, tau, P * c:P * c + P],
                                                       ident[0:n, 0:n])
                        last.then_inc(x_t, 1)
                        if c >= 1:
                            add_square(c - 1)
                    add_square(NC - 1)
                    def turn_ada(i):
                        pe.wait_ge(arow_s, i + 1)
                        for j in range(4):
                            last = nc.tensor.transpose(ps[:, 5, NSEQ * (4 * i + j):NSEQ * (4 * i + j) + NSEQ],
                                                       arow[:, i, P * j:P * j + P], ident[0:NSEQ, 0:NSEQ])
                        last.then_inc(adaT_t, 1)

                    pe.wait_ge(c_sb, 1)
                    pe.wait_ge(sq_s, NC)
                    for i in range(4):
                        wait_slot(pe, i)
                        if i >= 2:
                            pe.wait_ge(arow_s, i - 1)
                        for k in range(NC):
                            last = nc.tensor.matmul(ps[0:NSEQ, 1 + i % 2, :], cT[:, k, :], ring[:, i % RING1, k, :],
                                                    start=k == 0, stop=k == NC - 1)
                        last.then_inc(ada_t, 1)
                        if i >= 1:
                            turn_ada(i - 1)
                    turn_ada(3)
                    pe.wait_ge(ld_s, 32)
                    for c in range(3 * NC):
                        nc.tensor.transpose(ps[:, 3 + c // 16, 24 * (c % 16):24 * (c % 16) + 24],
                                            gstrow[:, P * c:P * c + P], ident[0:24, 0:24])
                    for c in range(NC):
                        last = nc.tensor.transpose(ps[:, 4, 384 + 16 * c:400 + 16 * c], sstrow[:, P * c:P * c + P],
                                                   ident[0:16, 0:16])
                    last.then_inc(st_t, 1)

                @block.vector
                def _(dve):
                    def link(ins):
                        order.link(dve, ins)

                    dve.wait_ge(vec_t, 2)
                    nc.vector.tensor_copy(vecs[:], ps[:, 0, 0:193]).then_inc(vec_s, 1)
                    nc.vector.tensor_copy(cT[:].rearrange("p c s -> p (c s)"), ps[:, 0, 256:256 + NC * NSEQ]).then_inc(c_sb, 1)
                    dve.wait_ge(sum_t, NC)
                    nc.vector.tensor_scalar(rstd[:], ps[:, 7, 0:T], 1.0 / D, EPS, ALU.mult, ALU.add).then_inc(mean_s, 1)
                    dve.wait_ge(rstd_s, 1)
                    dve.wait_ge(x_s, NC)
                    link(nc.vector.tensor_tensor(xT[:], xT[:], rstd[:].unsqueeze(1).to_broadcast([P, NC, T]), ALU.mult))
                    dve.wait_ge(adaT_t, 4)
                    dve.wait_ge(vec_s, 1)
                    link(nc.vector.tensor_tensor(adaT[:, 0:16, :], ps[:, 5, 0:16 * NSEQ].rearrange("p (c s) -> p c s", s=NSEQ),
                                                 bada[:, 0:16].unsqueeze(2).to_broadcast([P, 16, NSEQ]), ALU.add))
                    link(nc.vector.tensor_scalar(gw[:], A_SC1, 1.0, None, ALU.add))
                    link(nc.vector.tensor_tensor(gw[:], gw[:], n1w.unsqueeze(2).to_broadcast([P, NC, NSEQ]), ALU.mult))
                    samples = hT[:, :, SEQ:T].rearrange("p c (s t) -> p c s t", s=NS)
                    link(nc.vector.tensor_tensor(samples, xT[:, :, SEQ:T].rearrange("p c (s t) -> p c s t", s=NS),
                                                 gw[:, :, 1:NSEQ].unsqueeze(3).to_broadcast([P, NC, NS, ST]), ALU.mult))
                    nc.vector.tensor_tensor(samples, samples, A_SH1[:, :, 1:NSEQ].unsqueeze(3).to_broadcast([P, NC, NS, ST]), ALU.add)
                    for c in range(NC):
                        nc.vector.tensor_scalar(hT[:, c, 0:SEQ], xT[:, c, 0:SEQ], gw[:, c, 0:1], A_SH1[:, c, 0:1],
                                                ALU.mult, ALU.add)
                    dve.wait_ge(st_t, 1)
                    g2 = gst[:].rearrange("p c j -> p (c j)")
                    nc.vector.tensor_copy(g2[:, 0:384], ps[:, 3, 0:384])
                    nc.vector.tensor_copy(g2[:, 384:576], ps[:, 4, 0:192])
                    nc.vector.tensor_copy(sst[:].rearrange("p c j -> p (c j)"), ps[:, 4, 384:512]).then_inc(st_s, 1)

            z_and_o = ExitStack()
            with z_and_o:
                oT = sb("oT", [P, H, T], z_and_o)
                zT = sb("zT", [P, H, T], z_and_o)
                tails = sb("tails", [P, 3 * NC, TAILS], z_and_o)
                with ExitStack() as st:
                    mixer(nc, t, st, sb, sem, ring, ident, ones, causal, scausal, sblock, ssame, convw,
                          bada, adaT, hT, cT, gst, wab, par, states, oT, zT, tails, gbuf, order, load_slot, wait_slot, scw,
                          sst, short)
                with ExitStack() as st:
                    branches(nc, t, st, sb, sem, ring, ident, gnw, short, adaT, hT, oT, zT, tails, x2T, rows_of, order,
                             load_slot, wait_slot, load_piece)
        experts(nc, t, sb, sem, ring, ident, ones, causal, vecs, adaT, x2T, rows_of, order, norm,
                raw_full, load_piece)



def head_block(buf, tau, h):
    if tau < 2:
        return buf[:, h // 4, P * (h % 4):P * (h % 4) + P]
    return buf[0:64, 0, 64 * h:64 * h + 64]


def head_values(buf, tau, h):
    n = TILE[tau][1]
    return buf[0:n, h // 4, P * (h % 4):P * (h % 4) + P]


def groups(tau):
    return [(0, 2 * tau, range(0, 4), P), (1, 2 * tau + 1, range(4, 8), P)] if tau < 2 else [(0, 4, range(H), 64)]


def levels(tau):
    return LEVELS if tau < 2 else SLEVELS


def level_no(tau, lev, g):
    return 2 * LEVELS * tau + (2 * lev + g if tau < 2 else lev)


def wide_no(tau, lev, g):
    return 2 * (LEVELS - 1) * tau + (2 * (lev - 1) + g if tau < 2 else lev - 1)


GDN_STEPS = [(tau, kind, lev) for tau in range(NTILE) for kind, lev in
             [("tok", 0), ("rows", 0)] + [("level", x) for x in range(levels(tau))] +
             [("state", 0), ("value", 0), ("out", 0), ("turn", 0)]]


def mixer(nc, t, st, sb, sem, ring, ident, ones, causal, scausal, sblock, ssame, convw, bada, adaT, hT, cT, gst,
          wab, par, states, oT, zT, tails, gbuf, order, load_slot, wait_slot, scw, sst, short):
    ps = st.enter_context(nc.psum_tensor("ps_mix", [P, 8, 512], F32))
    qkT = sb("qkT", [P, 2, H, T], st)
    ktok = sb("ktok", [P, 2, 512], st)
    vtok = sb("vtok", [P, 2, 512], st)
    nb, mb, tb, xb, wb, qb = (gbuf[:, i] for i in range(6))
    rowsum = gbuf[:, 0:5].rearrange("p a b c -> p (a b c)").rearrange("p (m t) -> p m t", t=T)
    cbuf = sb("cbuf", [P, 2 * EW + 2 * (EW - KW + 1)], st)
    ext = cbuf[:, 0:2 * EW].rearrange("p (a n) -> p a n", a=2)
    acc = cbuf[:, 2 * EW:].rearrange("p (a n) -> p a n", a=2)
    sqb = sb("sqb", [P, 2, T], st)
    S = cbuf[:, 0:1024].rearrange("p (a n) -> p a n", a=2)
    masks = sb("masks", [P, LEVELS, P], st)
    ab = sb("ab", [P, NTILE, 16], st)
    earg = sb("earg", [P, NTILE, 16], st)
    beta = sb("beta", [P, NTILE, H], st)
    g = sb("g", [P, NTILE, H], st)
    pos = sb("pos_part", [P, NTILE, H], st)
    dec = sb("dec", [P, NTILE, 3, H], st)
    edec = sb("edec", [P, NTILE, 3, H], st)
    bdec = sb("bdec", [P, NTILE, H], st)
    gm = sb("gm", [64, H, NS], st)
    cds = sb("cds", [P, H, NS], st)
    oss = sb("oss", [P, 2, 4], st)

    (ld_w, ld_st, halo0, halo_s, raw_t, raw_s, tail_s, conv_s, silu_s, sq_s2, ss_t, ss_s, lnn_s, rs_s, nrm_s,
     mask0, mask_s) = (sem(x) for x in (
         "ld_w", "ld_st", "halo0", "halo_s", "raw_t", "raw_s", "tail_s", "conv_s", "qkv_silu_s", "qkv_sq_s", "ss_t",
         "ss_s", "lnn_s", "rs_s", "nrm_s", "mask0", "mask_s"))
    ab_t, ab_arg, ab_exp, ab_ln, g_s, dec_t, dec_s, edec_s = (sem(x) for x in (
        "ab_t", "ab_arg", "ab_exp", "ab_ln", "g_s", "dec_t", "dec_s", "edec_s"))
    (tok_t, ktok_s, vtok_s, src_s, rows_t, darg_s, dexp_s, n_s, masked, w_t, w_s, tx_t, tx_s, ks_t, kq_t, kq_s, r_s,
     u_t, u_s, o_t, s_t, S_s, oln_s, orr_s, o_s, turn_t, turn_s) = (sem(x) for x in (
         "tok_t", "ktok_s", "vtok_s", "src_s", "rows_t", "darg_s", "dexp_s", "n_s", "masked", "w_t", "w_s", "tx_t",
         "tx_s", "ks_t", "kq_t", "kq_s", "r_s", "u_t", "u_s", "o_t", "s_t", "S_s", "oln_s", "orr_s", "o_s", "turn_t",
         "turn_s"))
    z_t, z_s, ada2_t, ada_s2, um_s, su_t, scaled_s, so_s, st_out, S_out = (sem(x) for x in (
        "z_t", "z_s", "ada2_t", "ada_s2", "um_s", "su_t", "scaled_s", "so_s", "st_out", "S_out"))


    def chan(q):
        return (8 + q, q - 8, q)[q // 8]

    def dest(q):
        return (qkT[:, 1, q % 8], qkT[:, 0, q % 8], oT[:, q % 8])[q // 8]

    fills = [[] for _ in GDN_STEPS]
    units = [("z", m) for m in range(8)] + [("ada", m) for m in range(8)] + UNITS[:IN_MIXER]
    weight = {"ada": 6}
    total, at = sum(weight.get(kind, 4) for kind, _ in units), 0
    for u in units:
        fills[at * len(GDN_STEPS) // total].append(u)
        at += weight.get(u[0], 4)
    arow = sqb[0:NSEQ].rearrange("p a t -> p (a t)")[:, 0:HALF]
    arow_s, turned = sem("arow2_s"), sem("turned")

    def late(n_step):
        return [UNITS[UNITS.index(u) - 1] for u in fills[n_step] if u in UNITS[1:]] + (
            [UNITS[IN_MIXER - 1]] if n_step == len(GDN_STEPS) - 1 else [])

    hb, pext, _, ptails = short
    unit_t, act_s, dve_s, phalo0, phalo, pre_s, ptail = (
        sem(x) for x in ("unit_t", "br_act_s", "br_dve_s", "br_halo0", "br_halo", "br_pre_s", "br_ptail"))

    def seq_view(a):
        return a.rearrange("p (s t) -> p s t", s=NS)

    block = st.enter_context(nc.Block())

    @block.sync
    def _(sp):
        for i in range(8, S_GB):
            if i == S_GB - 1:
                sp.wait_ge(S_s, 4)
                sp.dma_start(t["rec_prompt"][0, 0].rearrange("h k v -> k h v"),
                             S[:].rearrange("p a n -> p (a n)").rearrange("p (h v) -> p h v", h=H)).then_inc(S_out, 16)
            load_slot(sp, i)
            if i == 10:
                for h in range(H):
                    sp.dma_start(states[:, h], t["state_gdn_rec"][0, :, h].rearrange("s k v -> k s v")).then_inc(ld_st, 16)
        for h in range(H):
            sp.wait_ge(so_s, h + 1)
            sp.dma_start(t["rec_sample"][0, :, h].rearrange("s k v -> k s v"), states[:, h]).then_inc(st_out, 16)
        sp.wait_ge(S_out, 16)

    @block.gpsimd
    def _(pool):
        nc.gpsimd.memset(ext[:, :, 0:KW - 1], 0.0).then_inc(halo0, 1)
        nc.gpsimd.memset(masks[:], 0.0).then_inc(mask0, 1)
        pool.wait_ge(mask0, 1)
        k = 0
        for lev in range(LEVELS):
            b = 1 << lev
            v = masks[:, lev].rearrange("p (m z r) -> p m z r", z=2, r=b)[:, :, 1, :]
            nc.gpsimd.memset(v, 1.0).then_inc(mask_s, 1)
            k += 1
            pool.wait_ge(mask_s, k)
            nc.gpsimd.affine_select(out=v, in_=v, compare_op=ALU.is_ge, fill=0.0, base=0,
                                    pattern=[[-2 * b, P // (2 * b)], [0, b]], channel_multiplier=1).then_inc(mask_s, 1)
            k += 1
            pool.wait_ge(mask_s, k)
            nc.gpsimd.affine_select(out=v, in_=v, compare_op=ALU.is_ge, fill=0.0, base=b - 1,
                                    pattern=[[2 * b, P // (2 * b)], [0, b]], channel_multiplier=-1).then_inc(mask_s, 1)
            k += 1
        pool.wait_ge(mask_s, k)
        for q in range(24):
            if q >= 2:
                pool.wait_ge(conv_s, q - 1)
            e = ext[:, q % 2, EXT:EW].rearrange("p (s j) -> p s j", s=NS)
            nc.gpsimd.tensor_copy(e[:, :, 0:KW - 1], gst[:, chan(q)].rearrange("p (s j) -> p s j", s=NS)).then_inc(halo_s, 1)
            pool.wait_ge(raw_s, q + 1)
            nc.gpsimd.tensor_copy(tails[:, chan(q), 0:3], ext[:, q % 2, EXT - 3:EXT])
            nc.gpsimd.tensor_copy(tails[:, chan(q), 3:TAILS].rearrange("p (s j) -> p s j", s=NS),
                                  e[:, :, SEXT - 3:SEXT]).then_inc(tail_s, 1)
        def keep(c):
            pool.wait_ge(pre_s, c + 1)
            nc.gpsimd.tensor_copy(ptails[:, c, 0:2], pext[:, c % 2, PEXT - 2:PEXT])
            nc.gpsimd.tensor_copy(seq_view(ptails[:, c, 2:PTAILS]),
                                  seq_view(pext[:, c % 2, PEXT:PW])[:, :, PSEXT - 2:PSEXT]).then_inc(ptail, 1)

        first_c = min(n for n, f in enumerate(fills) if ("c", 0) in f)
        for n_step, (tau, kind, lev) in enumerate(GDN_STEPS):
            if kind == "level":
                for gr, gi, heads, w in groups(tau):
                    n = TILE[tau][1]
                    pool.wait_ge(n_s, gi + 1)
                    if lev == 1:
                        pool.wait_ge(tx_s, level_no(tau, 0, gr) + 1)
                    if lev >= 2:
                        pool.wait_ge(w_t, level_no(tau, lev - 1, gr) + 1)
                    nc.gpsimd.tensor_tensor(
                        mb[0:n, gr, :].rearrange("p (h i) -> p h i", i=w),
                        nb[0:n, gr, :].rearrange("p (h i) -> p h i", i=w),
                        masks[0:n, lev, 0:w].unsqueeze(1).to_broadcast([n, 512 // w, w]), ALU.mult).then_inc(masked, 1)
            if n_step == first_c:
                pool.wait_ge(z_t, 8)
                nc.gpsimd.memset(pext[:, :, 0:SW - 1], 0.0).then_inc(phalo0, 1)
            if (tau, kind) == (2, "state"):
                pool.wait_ge(kq_t, 2)
                pool.wait_ge(edec_s, 2)
                for h in range(H):
                    nc.gpsimd.tensor_tensor(states[:, h], states[:, h],
                                            cds[:, h, :].unsqueeze(2).to_broadcast([P, NS, P]), ALU.mult).then_inc(scaled_s, 1)
            for what, c in fills[n_step]:
                if what == "c":
                    if c >= 1:
                        keep(c - 1)
                    if c >= 2:
                        pool.wait_ge(dve_s, c - 1)
                    nc.gpsimd.tensor_copy(seq_view(pext[:, c % 2, PEXT:PW])[:, :, 0:SW - 1],
                                          seq_view(sst[:, c])).then_inc(phalo, 1)
        keep(NC - 1)

    @block.scalar
    def _(act):
        def silu(q):
            act.wait_ge(conv_s, q + 1)
            a = acc[:, q % 2]
            nc.scalar.activation(dest(q)[:, 0:SEQ], a[:, 0:SEQ], ACT.Silu)
            nc.scalar.activation(dest(q)[:, SEQ:T].rearrange("p (s t) -> p s t", s=NS), sample_cols(a),
                                 ACT.Silu).then_inc(silu_s, 1)
            if q < 16:
                act.wait_ge(silu_s, q + 1)
                if q >= 2:
                    act.wait_ge(ss_t, q - 1)
                nc.scalar.activation(sqb[:, q % 2, :], dest(q), ACT.Square).then_inc(sq_s2, 1)

        for q in range(24):
            act.wait_ge(raw_t, q + 1)
            if q >= 2:
                act.wait_ge(conv_s, q - 1)
                act.wait_ge(tail_s, q - 1)
            nc.scalar.activation(ext[:, q % 2, KW - 1:EXT], ps[:, q % 2, 0:SEQ], ACT.Copy)
            nc.scalar.activation(ext[:, q % 2, EXT:EW].rearrange("p (s j) -> p s j", s=NS)[:, :, KW - 1:SEXT],
                                 ps[:, q % 2, SEQ:T].rearrange("p (s t) -> p s t", s=NS), ACT.Copy).then_inc(raw_s, 1)
            if q >= 1:
                silu(q - 1)
            if q == 18:
                act.wait_ge(ss_s, 16)
                for i in range(2):
                    nc.scalar.activation(rowsum[:, 8 * i:8 * i + 8], rowsum[:, 8 * i:8 * i + 8], ACT.Ln).then_inc(lnn_s, 1)
                for i in range(2):
                    act.wait_ge(lnn_s, i + 1)
                    nc.scalar.activation(rowsum[:, 8 * i:8 * i + 8], rowsum[:, 8 * i:8 * i + 8], ACT.Exp,
                                         scale=-0.5).then_inc(rs_s, 1)
                act.wait_ge(ab_arg, 1)
                nc.scalar.activation(earg[:], earg[:], ACT.Exp)
                nc.scalar.activation(par[:, 0, :], par[:, 0, :], ACT.Exp).then_inc(ab_exp, 1)
                act.wait_ge(ab_exp, 1)
                nc.scalar.activation(ab[:, :, 0:8], earg[:, :, 8:16], ACT.Ln, bias=1.0).then_inc(ab_ln, 1)
        silu(23)
        act.wait_ge(dec_s, 1)
        nc.scalar.activation(edec[:], dec[:], ACT.Exp).then_inc(edec_s, 1)
        nc.scalar.activation(cds[:], ps[:, 7, 128:192].rearrange("p (h s) -> p h s", h=H), ACT.Exp).then_inc(edec_s, 1)

        for n_step, (tau, kind, lev) in enumerate(GDN_STEPS):
            t0, n = TILE[tau]
            if kind == "tok":
                act.wait_ge(tok_t, tau + 1)
                for gr in range(2):
                    nc.scalar.activation(vtok[0:n, gr, :], ps[0:n, 4 + gr, :], ACT.Copy).then_inc(vtok_s, 1)
            if kind == "rows":
                for gr, gi, heads, w in groups(tau):
                    act.wait_ge(darg_s, gi + 1)
                    nc.scalar.activation(tb[0:n, gr, :], xb[0:n, gr, :], ACT.Exp).then_inc(dexp_s, 1)
            if kind == "level" and lev >= 1:
                for gr, gi, heads, w in groups(tau):
                    act.wait_ge(w_t, level_no(tau, lev, gr) + 1)
                    nc.scalar.activation(wb[0:n, gr, :], ps[0:n, 2 + gr, :], ACT.Copy).then_inc(w_s, 1)
            if (tau, kind) == (2, "state"):
                for gr in range(2):
                    act.wait_ge(kq_t, gr + 1)
                    nc.scalar.activation(wb[:, gr, :], ps[:, 2 + gr, :], ACT.Copy).then_inc(kq_s, 1)
            if kind == "value":
                for gr in range(2):
                    act.wait_ge(u_t, 2 * tau + gr + 1)
                    nc.scalar.activation(mb[0:n, gr, :], ps[0:n, u_bank(tau) + gr, :], ACT.Copy).then_inc(u_s, 1)
            if kind == "out":
                for gr in range(2):
                    i = 2 * tau + gr
                    act.wait_ge(oln_s, i + 1)
                    nc.scalar.activation(oss[0:n, gr, :], oss[0:n, gr, :], ACT.Ln).then_inc(orr_s, 1)
                    act.wait_ge(orr_s, 2 * i + 1)
                    nc.scalar.activation(oss[0:n, gr, :], oss[0:n, gr, :], ACT.Exp, scale=-0.5).then_inc(orr_s, 1)
            if kind == "turn":
                for gr in range(2):
                    act.wait_ge(turn_t, 2 * tau + gr + 1)
                    nc.scalar.activation(oT[:, 4 * gr:4 * gr + 4, t0:t0 + n],
                                         ps[:, 6 + gr, 0:4 * n].rearrange("p (h t) -> p h t", h=4), ACT.Copy).then_inc(turn_s, 1)
            for what, m in fills[n_step]:
                if what == "z":
                    act.wait_ge(z_t, m + 1)
                    nc.scalar.activation(zT[:, m], ps[:, 0, 0:T], ACT.Copy).then_inc(z_s, 1)
                if what == "ada":
                    act.wait_ge(ada2_t, m + 1)
                    if m == 0:
                        act.wait_ge(ss_t, 16)
                    else:
                        act.wait_ge(turned, m)
                    nc.scalar.activation(arow, ps[0:NSEQ, 1, :], ACT.Copy).then_inc(arow_s, 1)
            for what, c in late(n_step):
                if what == "h":
                    act.wait_ge(unit_t, c + 1)
                    nc.scalar.activation(hb[:, c, :], ps[:, (c + 1) % 2, 0:T], ACT.Copy).then_inc(act_s, 1)

    @block.tensor
    def _(pe):
        def sums(m):
            pe.wait_ge(sq_s2, m + 1)
            if m >= 2:
                pe.wait_ge(ss_s, m - 1)
            nc.tensor.matmul(ps[:, 2 + m % 2, 0:T], ones[:], sqb[:, m % 2, :], start=True, stop=True).then_inc(ss_t, 1)

        def chunk(i, j, out, rhs):
            for k in range(NC):
                last = nc.tensor.matmul(out, ring[:, place(i), k, P * j:P * j + P], rhs[:, k, :],
                                        start=k == 0, stop=k == NC - 1)
            return last

        pe.wait_ge(ld_w, 48)
        for tau, (t0, n) in enumerate(TILE):
            for k in range(NC):
                last = nc.tensor.matmul(ps[0:n, 6, 16 * tau:16 * tau + 16], hT[:, k, t0:t0 + n], wab[:, k, :],
                                        start=k == 0, stop=k == NC - 1)
        last.then_inc(ab_t, 1)
        for q in range(24):
            i, j = S_QKV + q // 4, q % 4
            if j == 0:
                wait_slot(pe, i)
            if q >= 2:
                pe.wait_ge(raw_s, q - 1)
            chunk(i, j, ps[:, q % 2, 0:T], hT).then_inc(raw_t, 1)
            if 3 <= q < 19:
                sums(q - 3)
            if q == 22:
                pe.wait_ge(g_s, 1)
                for tau, (t0, n) in enumerate(TILE):
                    o = ps[0:n, 7, 16 * tau:16 * tau + 16]
                    nc.tensor.matmul(o[:, 0:8], (scausal if tau == 2 else causal)[:], g[0:n, tau, :], start=True, stop=True)
                    nc.tensor.matmul(o[:, 8:16], (ssame if tau == 2 else ones)[:], g[0:n, tau, :], start=True, stop=True)
                nc.tensor.matmul(ps[:, 7, 128:192], ones[0:64, :], gm[:].rearrange("p h s -> p (h s)"),
                                 start=True, stop=True).then_inc(dec_t, 1)

        def tok(tau):
            t0, n = TILE[tau]
            if tau == 0:
                pe.wait_ge(nrm_s, 1)
                pe.wait_ge(silu_s, 24)
            else:
                pe.wait_ge(turn_s, 2 * tau)
                pe.wait_ge(S_s, 2 * tau)
            for src, bank in ((qkT[:, 1], 2), (oT, 4)):
                for h in range(H):
                    last = nc.tensor.transpose(ps[0:n, bank + h // 4, P * (h % 4):P * (h % 4) + P], src[:, h, t0:t0 + n],
                                               ident[:])
            last.then_inc(tok_t, 1)

        def rows(tau):
            t0, n = TILE[tau]
            for gr, gi, heads, w in groups(tau):
                pe.wait_ge(src_s, gi + 1)
                if gr == 0:
                    pe.wait_ge(ktok_s, tau + 1)
                    pe.wait_ge(vtok_s, 2 * tau + 2)
                    pe.wait_ge(nrm_s, 2)
                else:
                    pe.wait_ge(n_s, gi)
                nc.tensor.matmul(ps[0:n, 6, :], ones[0:n, 0:n], nb[0:n, gr, :], start=True, stop=True)
                nc.tensor.matmul(ps[0:n, 7, :], ones[0:n, 0:n], wb[0:n, gr, :], start=True, stop=True)
                for x, h in enumerate(heads):
                    nc.tensor.matmul(ps[0:n, 2 + 2 * gr, w * x:w * x + w], qkT[:, 1, h, t0:t0 + n],
                                     qkT[:, 1, h, t0:t0 + n], start=True, stop=True)
                for x, h in enumerate(heads):
                    last = nc.tensor.matmul(ps[0:n, 3 + 2 * gr, w * x:w * x + w], qkT[:, 1, h, t0:t0 + n],
                                            qkT[:, 0, h, t0:t0 + n], start=True, stop=True)
                last.then_inc(rows_t, 1)

        def level(tau, lev):
            n = TILE[tau][1]
            for gr, gi, heads, w in groups(tau):
                pe.wait_ge(masked, level_no(tau, lev, gr) + 1)
                if lev == 0:
                    pe.wait_ge(n_s, 2 * tau + len(groups(tau)))
                else:
                    pe.wait_ge(tx_s, level_no(tau, lev - 1, gr) + 1)
                for x, h in enumerate(heads):
                    rhs = ident[0:w, 0:w] if lev == 0 else head_block(tb, tau, h)
                    last = nc.tensor.matmul(ps[0:n, 2 + gr, w * x:w * x + w], head_block(mb, tau, h), rhs,
                                            start=True, stop=True)
                last.then_inc(w_t, 1)
            if lev == 0:
                return
            for gr, gi, heads, w in groups(tau):
                pe.wait_ge(w_s, wide_no(tau, lev, gr) + 1)
                if lev < levels(tau) - 1:
                    for x, h in enumerate(heads):
                        nc.tensor.matmul(ps[0:n, 4 + gr, w * x:w * x + w], head_block(xb, tau, h), head_block(wb, tau, h),
                                         start=True, stop=True)
                for x, h in enumerate(heads):
                    last = nc.tensor.matmul(ps[0:n, 6 + gr, w * x:w * x + w], head_block(wb, tau, h),
                                            head_block(xb, tau, h), start=True, stop=True)
                last.then_inc(tx_t, 1)

        def state(tau):
            t0, n = TILE[tau]
            pe.wait_ge(tx_s, level_no(tau, levels(tau) - 1, len(groups(tau)) - 1) + 1)
            if tau == 1:
                pe.wait_ge(S_s, 2)
                for gr in range(2):
                    for kq, bank in ((1, 2), (0, 4)):
                        for h in range(4 * gr, 4 * gr + 4):
                            last = nc.tensor.matmul(ps[:, bank + gr, P * (h % 4):P * (h % 4) + P], qkT[:, kq, h, t0:t0 + n],
                                                    head_values(S, 0, h), start=True, stop=True)
                    last.then_inc(ks_t, 1)
            if tau == 2:
                pe.wait_ge(ld_st, 16 * H)
                for h in range(H):
                    o = ps[:, 2 + h // 4, P * (h % 4):P * (h % 4) + P].rearrange("p (k t) -> p k t", k=2)
                    for s in range(NS):
                        last = nc.tensor.matmul(o[:, :, ST * s:ST * s + ST], states[:, h, s, :],
                                                qkT[:, :, h, SEQ + ST * s:SEQ + ST * s + ST], start=True, stop=True)
                    if h % 4 == 3:
                        last.then_inc(kq_t, 1)
                pe.wait_ge(kq_s, 2)
                for gr in range(2):
                    for kq, bank in ((1, 4), (0, 6)):
                        for x in range(4):
                            last = nc.tensor.transpose(ps[0:64, bank + gr, P * x:P * x + P],
                                                       wb[:, gr, P * x + 64 * kq:P * x + 64 * kq + 64], ident[:])
                    last.then_inc(ks_t, 1)

        def value(tau):
            n = TILE[tau][1]
            for gr in range(2):
                pe.wait_ge(r_s, 2 * tau + gr + 1)
                for h in range(4 * gr, 4 * gr + 4):
                    last = nc.tensor.matmul(head_values(ps[:, u_bank(tau):u_bank(tau) + 2], tau, h), head_block(xb, tau, h),
                                            head_values(nb, tau, h), start=True, stop=True)
                last.then_inc(u_t, 1)

        def out(tau):
            n = TILE[tau][1]
            for gr in range(2):
                pe.wait_ge(u_s, 2 * tau + gr + 1)
                for h in range(4 * gr, 4 * gr + 4):
                    last = nc.tensor.matmul(head_values(ps[:, o_bank(tau):o_bank(tau) + 2], tau, h), head_block(qb, tau, h),
                                            head_values(mb, tau, h), start=True, stop=True)
                last.then_inc(o_t, 1)
                if tau < 2:
                    for h in range(4 * gr, 4 * gr + 4):
                        last = nc.tensor.matmul(ps[:, 4 + gr, P * (h % 4):P * (h % 4) + P], head_values(ktok, tau, h),
                                                head_values(mb, tau, h), start=True, stop=True)
                    last.then_inc(s_t, 1)
            if tau == 2:
                for h in range(H):
                    pe.wait_ge(um_s, h + 1)
                    bank = 2 + 2 * (h % 2)
                    if h >= 2:
                        pe.wait_ge(so_s, h - 1)
                    elif h == 1:
                        pe.wait_ge(o_s, 6)
                    um = (xb, qb)[h % 2]
                    for x in range(2):
                        last = nc.tensor.matmul(ps[:, bank + x, :], head_values(ktok, tau, h), um[0:64, x, :],
                                                start=True, stop=True)
                    last.then_inc(su_t, 1)

        def turn(tau):
            n = TILE[tau][1]
            for gr in range(2):
                pe.wait_ge(o_s, 2 * tau + gr + 1)
                for h in range(4 * gr, 4 * gr + 4):
                    last = nc.tensor.transpose(ps[:, 6 + gr, n * (h % 4):n * (h % 4) + n], head_values(wb, tau, h),
                                               ident[0:n, 0:n])
                last.then_inc(turn_t, 1)

        def turn_ada(m):
            pe.wait_ge(arow_s, m + 1)
            if m == 0:
                pe.wait_ge(z_s, 8)
            for j in range(4):
                n = 4 * m + j
                last = nc.tensor.transpose(ps[:, 0, NSEQ * n:NSEQ * n + NSEQ], arow[:, P * j:P * j + P], ident[0:NSEQ, 0:NSEQ])
            last.then_inc(turned, 1)

        for n_step, (tau, kind, lev) in enumerate(GDN_STEPS):
            {"tok": tok, "rows": rows, "state": state, "value": value, "out": out, "turn": turn}.get(
                kind, lambda tau: level(tau, lev))(tau)
            for what, m in fills[n_step]:
                if what == "z":
                    i, j = S_Z + m // 4, m % 4
                    if j == 0:
                        wait_slot(pe, i)
                    if m >= 1:
                        pe.wait_ge(z_s, m)
                    else:
                        pe.wait_ge(raw_s, 24)
                    chunk(i, j, ps[:, 0, 0:T], hT).then_inc(z_t, 1)
                elif what in ("h", "c", "b"):
                    u = UNITS.index((what, m))
                    i, j = S_H + u // 4, u % 4
                    if j == 0:
                        wait_slot(pe, i)
                    if u == 0:
                        turn_ada(7)
                    elif u == 1:
                        pe.wait_ge(ada_s2, 1)
                    else:
                        mine, k = taken(u - 2)
                        pe.wait_ge(act_s if mine else dve_s, k)
                    chunk(i, j, ps[:, (u + 1) % 2, 0:T], hT).then_inc(unit_t, 1)
                else:
                    wait_slot(pe, S_ADA2 + m)
                    if m >= 1:
                        turn_ada(m - 1)
                    for k in range(NC):
                        last = nc.tensor.matmul(ps[0:NSEQ, 1, :], cT[:, k, :], ring[:, place(S_ADA2 + m), k, :],
                                                start=k == 0, stop=k == NC - 1)
                    last.then_inc(ada2_t, 1)

    @block.vector
    def _(dve):
        def link(ins):
            order.link(dve, ins)

        def wide(ap, n, w=P):
            return ap.rearrange("p (h i) -> p h i", i=w)

        def conv(q):
            dve.wait_ge(raw_s, q + 1)
            dve.wait_ge(halo_s, q + 1)
            if q >= 2:
                dve.wait_ge(silu_s, q - 1)
            a, e, c = acc[:, q % 2, :], ext[:, q % 2, :], chan(q)
            m = EW - KW + 1
            link(nc.vector.tensor_scalar(a, e[:, 0:m], convw[:, 0, c:c + 1], None, ALU.mult))
            for j in range(1, KW):
                ins = nc.vector.scalar_tensor_tensor(out=a, in0=e[:, j:j + m], scalar=convw[:, j, c:c + 1], in1=a,
                                                     op0=ALU.mult, op1=ALU.add)
                if j < KW - 1:
                    link(ins)
                else:
                    ins.then_inc(conv_s, 1)

        def sum_out(m):
            dve.wait_ge(ss_t, m + 1)
            s = 1.0 if m < 8 else float(P)
            nc.vector.tensor_scalar(rowsum[:, m], ps[:, 2 + m % 2, 0:T], s, s * 1e-6, ALU.mult, ALU.add).then_inc(ss_s, 1)

        dve.wait_ge(halo0, 1)
        link(nc.vector.memset(ab[:], 0.0))
        dve.wait_ge(ab_t, 1)
        nc.vector.tensor_copy(ab[:, 0:2, :], ps[:, 6, 0:32].rearrange("p (a b) -> p a b", b=16))
        link(nc.vector.tensor_copy(ab[0:64, 2, :], ps[0:64, 6, 32:48]))
        dve.wait_ge(ld_w, 48)
        link(nc.vector.tensor_tensor(ab[:, :, 8:16], ab[:, :, 8:16], par[:, 1:2, :].to_broadcast([P, NTILE, H]), ALU.add))
        nc.vector.tensor_scalar(earg[:, :, 0:8], ab[:, :, 0:8], -1.0, None, ALU.mult)
        nc.vector.tensor_scalar(pos[:], ab[:, :, 8:16], 0.0, None, ALU.max)
        link(nc.vector.scalar_tensor_tensor(out=earg[:, :, 8:16], in0=ab[:, :, 8:16], scalar=-1.0, in1=ab[:, :, 8:16],
                                            op0=ALU.mult, op1=ALU.max))
        nc.vector.tensor_scalar(earg[:, :, 8:16], earg[:, :, 8:16], -1.0, None, ALU.mult).then_inc(ab_arg, 1)
        for q in range(24):
            conv(q)
            if 3 <= q < 19:
                sum_out(q - 3)
            if q == 20:
                for i in range(2):
                    dve.wait_ge(rs_s, i + 1)
                    x = qkT[:, 1 - i].rearrange("p h t -> p (h t)")
                    r = rowsum[:, 8 * i:8 * i + 8].rearrange("p h t -> p (h t)")
                    nc.vector.tensor_tensor(x, x, r, ALU.mult).then_inc(nrm_s, 1)
                dve.wait_ge(ab_ln, 1)
                link(nc.vector.tensor_scalar(earg[:, :, 0:8], earg[:, :, 0:8], 1.0, None, ALU.add))
                nc.vector.reciprocal(beta[:], earg[:, :, 0:8])
                link(nc.vector.tensor_tensor(g[:], pos[:], ab[:, :, 0:8], ALU.add))
                link(nc.vector.scalar_tensor_tensor(out=g[:], in0=g[:], scalar=-1.0,
                                                    in1=par[:, 0:1, :].to_broadcast([P, NTILE, H]), op0=ALU.mult, op1=ALU.mult))
                nc.vector.tensor_tensor(gm[:], g[0:64, 2, :].unsqueeze(2).to_broadcast([64, H, NS]),
                                        sblock[:].unsqueeze(1).to_broadcast([64, H, NS]), ALU.mult).then_inc(g_s, 1)
        link(nc.vector.memset(dec[:], 0.0))
        dve.wait_ge(dec_t, 1)
        for tau, (t0, n) in enumerate(TILE):
            nc.vector.tensor_copy(dec[0:n, tau, 0, :], ps[0:n, 7, 16 * tau:16 * tau + 8])
            link(nc.vector.tensor_copy(dec[0:n, tau, 2, :], ps[0:n, 7, 16 * tau + 8:16 * tau + 16]))
        nc.vector.tensor_tensor(dec[:, :, 1, :], dec[:, :, 2, :], dec[:, :, 0, :], ALU.subtract).then_inc(dec_s, 1)
        dve.wait_ge(edec_s, 1)
        link(nc.vector.tensor_tensor(bdec[:], beta[:], edec[:, :, 0, :], ALU.mult))

        for n_step, (tau, kind, lev) in enumerate(GDN_STEPS):
            t0, n = TILE[tau]
            causes = scausal if tau == 2 else causal
            if kind == "tok":
                if tau:
                    dve.wait_ge(turn_t, 2 * tau)
                for gr, gi, heads, w in groups(tau):
                    k = len(heads)
                    h0 = heads[0]
                    nc.vector.tensor_tensor(wide(nb[0:n, gr, :], n, w), causes[0:n, 0:w].unsqueeze(1).to_broadcast([n, k, w]),
                                            g[0:n, tau, h0:h0 + k].unsqueeze(2).to_broadcast([n, k, w]), ALU.mult)
                    nc.vector.tensor_tensor(wide(wb[0:n, gr, :], n, w), ident[0:n, 0:w].unsqueeze(1).to_broadcast([n, k, w]),
                                            beta[0:n, tau, h0:h0 + k].unsqueeze(2).to_broadcast([n, k, w]),
                                            ALU.mult).then_inc(src_s, 1)
                dve.wait_ge(tok_t, tau + 1)
                for gr in range(2):
                    ins = nc.vector.tensor_tensor(wide(ktok[0:n, gr, :], n), wide(ps[0:n, 2 + gr, :], n),
                                                  edec[0:n, tau, 1, 4 * gr:4 * gr + 4].unsqueeze(2).to_broadcast([n, 4, P]),
                                                  ALU.mult)
                ins.then_inc(ktok_s, 1)
            if kind == "rows":
                for gr, gi, heads, w in groups(tau):
                    k = len(heads)
                    h0 = heads[0]
                    dve.wait_ge(rows_t, gi + 1)
                    link(nc.vector.tensor_tensor(wide(xb[0:n, gr, :], n, w), wide(ps[0:n, 6, :], n, w),
                                                 dec[0:n, tau, 0, h0:h0 + k].unsqueeze(2).to_broadcast([n, k, w]), ALU.subtract))
                    nc.vector.tensor_scalar(xb[0:n, gr, :], xb[0:n, gr, :], 0.0, None, ALU.min).then_inc(darg_s, 1)
                    dve.wait_ge(dexp_s, gi + 1)
                    link(nc.vector.tensor_tensor(wide(tb[0:n, gr, :], n, w), wide(tb[0:n, gr, :], n, w),
                                                 causes[0:n, 0:w].unsqueeze(1).to_broadcast([n, k, w]), ALU.mult))
                    nc.vector.tensor_tensor(qb[0:n, gr, :], ps[0:n, 3 + 2 * gr, :], tb[0:n, gr, :], ALU.mult)
                    link(nc.vector.tensor_tensor(nb[0:n, gr, :], ps[0:n, 2 + 2 * gr, :], tb[0:n, gr, :], ALU.mult))
                    nc.vector.tensor_tensor(nb[0:n, gr, :], nb[0:n, gr, :], ps[0:n, 7, :], ALU.mult).then_inc(n_s, 1)
            if kind == "level":
                for gr, gi, heads, w in groups(tau):
                    k = len(heads)
                    if lev == 0:
                        eye = ident[0:n, 0:w].unsqueeze(1).to_broadcast([n, k, w])
                        dve.wait_ge(masked, level_no(tau, 0, gr) + 1)
                        nc.vector.tensor_tensor(wide(xb[0:n, gr, :], n, w), eye, wide(mb[0:n, gr, :], n, w), ALU.subtract)
                        dve.wait_ge(w_t, level_no(tau, 0, gr) + 1)
                        nc.vector.tensor_tensor(wide(tb[0:n, gr, :], n, w), eye, wide(ps[0:n, 2 + gr, :], n, w),
                                                ALU.subtract).then_inc(tx_s, 1)
                    else:
                        dve.wait_ge(tx_t, wide_no(tau, lev, gr) + 1)
                        dve.wait_ge(tx_s, level_no(tau, lev - 1, gr) + 1)
                        if lev < levels(tau) - 1:
                            nc.vector.tensor_tensor(tb[0:n, gr, :], tb[0:n, gr, :], ps[0:n, 4 + gr, :], ALU.subtract)
                        nc.vector.tensor_tensor(xb[0:n, gr, :], xb[0:n, gr, :], ps[0:n, 6 + gr, :],
                                                ALU.subtract).then_inc(tx_s, 1)
            if kind == "state":
                kb, qbank = (2, 4) if tau == 1 else (4, 6)
                for gr in range(2):
                    bc = lambda a: a[0:n, 4 * gr:4 * gr + 4].unsqueeze(2).to_broadcast([n, 4, P])
                    if gr == 0:
                        dve.wait_ge(vtok_s, 2 * tau + 2)
                    ins = nc.vector.tensor_tensor(wide(nb[0:n, gr, :], n), wide(vtok[0:n, gr, :], n), bc(beta[:, tau, :]),
                                                  ALU.mult)
                    if tau == 0:
                        ins.then_inc(r_s, 1)
                        continue
                    link(ins)
                    dve.wait_ge(ks_t, 2 * (tau - 1) + (gr + 1 if tau == 1 else 2))
                    nc.vector.tensor_tensor(wide(tb[0:n, gr, :], n), wide(ps[0:n, qbank + gr, :], n), bc(edec[:, tau, 0, :]),
                                            ALU.mult)
                    link(nc.vector.tensor_tensor(wide(wb[0:n, gr, :], n), wide(ps[0:n, kb + gr, :], n), bc(bdec[:, tau, :]),
                                                 ALU.mult))
                    nc.vector.tensor_tensor(nb[0:n, gr, :], nb[0:n, gr, :], wb[0:n, gr, :], ALU.subtract).then_inc(r_s, 1)
            if kind == "out":
                for gr in range(2):
                    i = 2 * tau + gr
                    dve.wait_ge(o_t, i + 1)
                    if tau == 0:
                        link(nc.vector.tensor_copy(wb[0:n, gr, :], ps[0:n, o_bank(tau) + gr, :]))
                    else:
                        link(nc.vector.tensor_tensor(wb[0:n, gr, :], ps[0:n, o_bank(tau) + gr, :], tb[0:n, gr, :], ALU.add))
                    link(nc.vector.tensor_tensor(nb[0:n, gr, :], wb[0:n, gr, :], wb[0:n, gr, :], ALU.mult))
                    link(nc.vector.tensor_reduce(oss[0:n, gr, :], wide(nb[0:n, gr, :], n), AX.X, ALU.add))
                    nc.vector.tensor_scalar(oss[0:n, gr, :], oss[0:n, gr, :], 1.0 / P, EPS, ALU.mult, ALU.add).then_inc(oln_s, 1)
                    if tau == 1:
                        sv = wide(S[:, gr, :], P)
                        link(nc.vector.tensor_tensor(sv, sv, edec[:, tau, 2, 4 * gr:4 * gr + 4].unsqueeze(2).to_broadcast([P, 4, P]),
                                                     ALU.mult))
                    if tau < 2:
                        dve.wait_ge(s_t, i + 1)
                    if tau == 0:
                        nc.vector.tensor_copy(S[:, gr, :], ps[:, 4 + gr, :]).then_inc(S_s, 1)
                    if tau == 1:
                        nc.vector.tensor_tensor(S[:, gr, :], S[:, gr, :], ps[:, 4 + gr, :], ALU.add).then_inc(S_s, 1)
                for gr in range(2):
                    i = 2 * tau + gr
                    dve.wait_ge(orr_s, 2 * i + 2)
                    nc.vector.tensor_tensor(wide(wb[0:n, gr, :], n), wide(wb[0:n, gr, :], n),
                                            oss[0:n, gr, :].unsqueeze(2).to_broadcast([n, 4, P]), ALU.mult).then_inc(o_s, 1)
                if tau == 2:
                    def spread(h):
                        if h >= 2:
                            dve.wait_ge(su_t, h - 1)
                        um = (xb, qb)[h % 2][0:64].rearrange("p a n -> p (a n)").rearrange("p (s v) -> p s v", s=NS)
                        nc.vector.tensor_tensor(um, head_values(mb, 2, h).unsqueeze(1).to_broadcast([64, NS, P]),
                                                sblock[:].unsqueeze(2).to_broadcast([64, NS, P]), ALU.mult).then_inc(um_s, 1)
                    dve.wait_ge(u_s, 6)
                    spread(0)
                    spread(1)
                    for h in range(H):
                        dve.wait_ge(su_t, h + 1)
                        dve.wait_ge(scaled_s, h + 1)
                        for x in range(2):
                            sv = states[:, h, 4 * x:4 * x + 4, :].rearrange("p s v -> p (s v)")
                            ins = nc.vector.tensor_tensor(sv, sv, ps[:, 2 + 2 * (h % 2) + x, :], ALU.add)
                        ins.then_inc(so_s, 1)
                        if h + 2 < H:
                            spread(h + 2)
            if ("h", 0) in fills[n_step]:
                dve.wait_ge(turned, 8)
                nc.vector.tensor_tensor(adaT[:, 16:48, :], ps[:, 0, 0:32 * NSEQ].rearrange("p (c s) -> p c s", s=NSEQ),
                                        bada[:, 16:48].unsqueeze(2).to_broadcast([P, 32, NSEQ]), ALU.add).then_inc(ada_s2, 1)
            for what, m in late(n_step):
                o = ps[:, (m + 1) % 2, 0:T]
                if what == "c":
                    short_convolution(nc, dve, link, m, o, scw, short, unit_t, act_s, dve_s, phalo0, phalo, pre_s, ptail)
                if what == "b":
                    dve.wait_ge(unit_t, 2 * NC + m + 1)
                    if m == 0:
                        dve.wait_ge(dve_s, NC)
                    nc.vector.tensor_tensor(hb[:, m, :], hb[:, m, :], o, ALU.mult).then_inc(dve_s, 1)


def u_bank(tau):
    return 6 if tau < 2 else 2


def o_bank(tau):
    return 2 if tau < 2 else 4


def sample_cols(a):
    return a[:, EXT - KW + 1:EXT - KW + 1 + NS * SEXT].rearrange("p (s j) -> p s j", s=NS)[:, :, KW - 1:SEXT]


UNITS = [(kind, c) for kind in ("h", "c", "b", "gb", "wb", "ga", "wa", "wo") for c in range(NC)]
IN_MIXER = 3 * NC
BY_ACT = ("h", "gb", "ga")


def taken(n):
    mine = UNITS[n][0] in BY_ACT
    return mine, sum((kind in BY_ACT) == mine for kind, _ in UNITS[:n + 1])


def short_convolution(nc, dve, link, c, o, scw, short, unit_t, act_s, dve_s, halo0, halo, pre_s, ptail):
    hb, ext, acc, _ = short

    def seq_view(a):
        return a.rearrange("p (s t) -> p s t", s=NS)

    dve.wait_ge(unit_t, NC + c + 1)
    dve.wait_ge(act_s, c + 1)
    dve.wait_ge(halo, c + 1)
    if c == 0:
        dve.wait_ge(halo0, 1)
    if c >= 2:
        dve.wait_ge(ptail, c - 1)
    e, a = ext[:, c % 2, :], acc[:, c % 2, :]
    nc.vector.tensor_tensor(e[:, SW - 1:PEXT], o[:, 0:SEQ], hb[:, c, 0:SEQ], ALU.mult)
    nc.vector.tensor_tensor(seq_view(e[:, PEXT:PW])[:, :, SW - 1:PSEXT], seq_view(o[:, SEQ:T]),
                            seq_view(hb[:, c, SEQ:T]), ALU.mult).then_inc(pre_s, 1)
    dve.wait_ge(pre_s, c + 1)
    m = PW - SW + 1
    link(nc.vector.tensor_scalar(a[:, 0:m], e[:, 0:m], scw[:, 0, c:c + 1], None, ALU.mult))
    link(nc.vector.scalar_tensor_tensor(out=a[:, 0:m], in0=e[:, 1:m + 1], scalar=scw[:, 1, c:c + 1], in1=a[:, 0:m],
                                        op0=ALU.mult, op1=ALU.add))
    nc.vector.scalar_tensor_tensor(out=hb[:, c, 0:SEQ], in0=e[:, 2:SEQ + 2], scalar=scw[:, 2, c:c + 1],
                                   in1=a[:, 0:SEQ], op0=ALU.mult, op1=ALU.add)
    s0 = PEXT - SW + 1
    nc.vector.scalar_tensor_tensor(out=seq_view(hb[:, c, SEQ:T]), in0=seq_view(e[:, PEXT:PW])[:, :, 2:PSEXT],
                                   scalar=scw[:, 2, c:c + 1], in1=seq_view(a[:, s0:s0 + NS * PSEXT])[:, :, SW - 1:PSEXT],
                                   op0=ALU.mult, op1=ALU.add).then_inc(dve_s, 1)


def branches(nc, t, st, sb, sem, ring, ident, gnw, short, adaT, hT, oT, zT, tails, x2T, xrow, order, load_slot,
             wait_slot, load_piece):
    ps = st.enter_context(nc.psum_tensor("ps_br", [P, 8, 512], F32))
    hb, _, _, ptails = short
    gb = sb("gb", [P, NC, T], st)
    trow = sb("trow", [P, QKV], st)
    ga = trow[:, 0:NC * T].rearrange("p (c t) -> p c t", c=NC)
    gtmp = sb("gtmp", [P, 2, NS * ST], st)
    prow = sb("prow", [PTAILS, D], st)
    unit_t, act_s, dve_s, x_ld, x_t, x_s, tr_t, tr_s, pt_t, pt_s, z_silu, o_s, ptail, out_d = (
        sem("br_" + x) if x != "unit_t" else sem(x) for x in (
            "unit_t", "act_s", "dve_s", "x_ld", "x_t", "x_s", "tr_t", "tr_s", "pt_t", "pt_s", "z_silu", "o_s", "ptail",
            "out_d"))
    st_out = sem("st_out")
    G1 = adaT[:, 16:24, :]

    def wait_taken(eng, n):
        mine, k = taken(n)
        eng.wait_ge(act_s if mine else dve_s, k)

    def seq_view(a):
        return a.rearrange("p (s t) -> p s t", s=NS)

    block = st.enter_context(nc.Block())

    @block.sync
    def _(sp):
        for i in range(S_GB, NSLOT1):
            load_slot(sp, i)
            if i == 30:
                sp.wait_ge(tr_s, 6)
                sp.dma_start(t["conv_prompt"][0, 0], trow[0:3, :]).then_inc(out_d, 16)
                sp.dma_start(t["conv_sample"][0].rearrange("s j c -> (s j) c"), trow[3:TAILS, :]).then_inc(out_d, 16)
                sp.wait_ge(pt_s, 2)
                sp.dma_start(t["sc_prompt"][0, 0], prow[0:2, :]).then_inc(out_d, 16)
                sp.dma_start(t["sc_sample"][0].rearrange("s j c -> (s j) c"), prow[2:PTAILS, :]).then_inc(out_d, 16)
        for p in range(RAW):
            if p % 2 == 0:
                sp.wait_ge(unit_t, 4 * (NSLOT1 - (RING1 - 1) + p // 2 - S_H + 1))
            load_piece(sp, 0, p)
        sp.wait_ge(out_d, 64)
        sp.wait_ge(st_out, 16 * H)

    @block.scalar
    def _(act):
        for tau in range(2):
            act.dma_start(xrow[:, tau, :], t["x_prompt"][0, P * tau:P * tau + P, :]).then_inc(x_ld, 16)
        act.dma_start(xrow[0:64, 2, :], t["x_sample"].rearrange("s t d -> (s t) d")).then_inc(x_ld, 16)
        nc.scalar.activation(zT[:], zT[:], ACT.Silu).then_inc(z_silu, 1)
        def take(kinds):
            for n, (kind, c) in enumerate(UNITS):
                if n >= IN_MIXER and kind in kinds:
                    act.wait_ge(unit_t, n + 1)
                    nc.scalar.activation({"gb": gb, "ga": ga}[kind][:, c, :], ps[:, n % 2, 0:T], ACT.Sigmoid).then_inc(act_s, 1)

        take(("gb",))
        for c in range(NC):
            act.wait_ge(x_t, c + 1)
            nc.scalar.activation(x2T[:, c, :], ps[:, 2 + c % 4, 0:T], ACT.Copy).then_inc(x_s, 1)
        act.wait_ge(tr_t, 1)
        for i in range(6):
            nc.scalar.activation(trow[0:TAILS, HALF * i:HALF * i + HALF], ps[0:TAILS, 2 + i, :], ACT.Copy).then_inc(tr_s, 1)
        act.wait_ge(pt_t, 1)
        for i in range(2):
            nc.scalar.activation(prow[:, HALF * i:HALF * i + HALF], ps[0:PTAILS, 2 + i, :], ACT.Copy).then_inc(pt_s, 1)
        act.wait_ge(out_d, 64)
        take(("ga",))

    @block.tensor
    def _(pe):
        for n, (kind, c) in enumerate(UNITS):
            if n < IN_MIXER:
                continue
            if (kind, c) == ("wb", 0):
                pe.wait_ge(x_ld, 48)
                for k in range(NC):
                    if k >= 4:
                        pe.wait_ge(x_s, k - 3)
                    for tau, (t0, n_tok) in enumerate(TILE):
                        last = nc.tensor.transpose(ps[:, 2 + k % 4, t0:t0 + n_tok], xrow[0:n_tok, tau, P * k:P * k + P],
                                                   ident[0:n_tok, 0:n_tok])
                    last.then_inc(x_t, 1)
                pe.wait_ge(x_s, NC)
                for k in range(3 * NC):
                    last = nc.tensor.transpose(ps[0:TAILS, 2 + k // 4, P * (k % 4):P * (k % 4) + P], tails[:, k, :], ident[:])
                last.then_inc(tr_t, 1)
                pe.wait_ge(ptail, NC)
                pe.wait_ge(tr_s, 6)
                for k in range(NC):
                    last = nc.tensor.transpose(ps[0:PTAILS, 2 + k // 4, P * (k % 4):P * (k % 4) + P], ptails[:, k, :], ident[:])
                last.then_inc(pt_t, 1)
            i, j = S_H + n // 4, n % 4
            if j == 0:
                wait_slot(pe, i)
            if n >= 2:
                wait_taken(pe, n - 2)
            if (kind, c) in (("wb", 0), ("wo", 0)):
                wait_taken(pe, n - 1 if kind == "wo" else n - NC - 1)
            if (kind, c) == ("wa", 0):
                pe.wait_ge(o_s, 1)
            rhs = {"wb": hb, "wa": oT, "wo": ga}.get(kind, hT)
            for k in range(NC):
                last = nc.tensor.matmul(ps[:, n % 2, 0:T], ring[:, place(i), k, P * j:P * j + P], rhs[:, k, :],
                                        start=k == 0, stop=k == NC - 1)
            last.then_inc(unit_t, 1)

    @block.vector
    def _(dve):
        def link(ins):
            order.link(dve, ins)

        dve.wait_ge(z_silu, 1)
        nc.vector.scalar_tensor_tensor(out=oT[:].rearrange("p h t -> p (h t)"), in0=oT[:].rearrange("p h t -> p (h t)"),
                                       scalar=gnw, in1=zT[:].rearrange("p h t -> p (h t)"), op0=ALU.mult,
                                       op1=ALU.mult).then_inc(o_s, 1)
        for n, (kind, c) in enumerate(UNITS):
            if n < IN_MIXER or kind in BY_ACT:
                continue
            dve.wait_ge(unit_t, n + 1)
            o = ps[:, n % 2, 0:T]
            if kind == "wb":
                dve.wait_ge(act_s, NC + c + 1)
                nc.vector.tensor_tensor(gb[:, c, :], gb[:, c, :], o, ALU.mult).then_inc(dve_s, 1)
            if kind == "wa":
                dve.wait_ge(act_s, 2 * NC + c + 1)
                link(nc.vector.tensor_tensor(ga[:, c, :], ga[:, c, :], o, ALU.mult))
                nc.vector.tensor_tensor(ga[:, c, :], ga[:, c, :], gb[:, c, :], ALU.add).then_inc(dve_s, 1)
            if kind == "wo":
                nc.vector.scalar_tensor_tensor(out=x2T[:, c, 0:SEQ], in0=o[:, 0:SEQ], scalar=G1[:, c, 0:1],
                                               in1=x2T[:, c, 0:SEQ], op0=ALU.mult, op1=ALU.add)
                link(nc.vector.tensor_tensor(seq_view(gtmp[:, c % 2, :]), seq_view(o[:, SEQ:T]),
                                             G1[:, c, 1:NSEQ].unsqueeze(2).to_broadcast([P, NS, ST]), ALU.mult))
                nc.vector.tensor_tensor(x2T[:, c, SEQ:T], x2T[:, c, SEQ:T], gtmp[:, c % 2, :], ALU.add).then_inc(dve_s, 1)


def experts(nc, t, sb, sem, ring, ident, ones, causal, vecs, adaT, x2T, h2tok, order, norm, raw_full,
            load_piece):
    n2w, nfw = vecs[:, 8:16], vecs[:, 16:24]
    SH2, SC2, G2 = adaT[:, 24:32, :], adaT[:, 32:40, :], adaT[:, 40:48, :]
    yacc = sb("yacc", [P, NC, T])
    route = sb("route", [P, E + 1, 2, NTILE])
    iota = sb("iota", [P, CAP])
    brow = sb("brow", [P, 2, D])
    expert_row = sb("expert_row", [P, E])
    count = sb("count", [P, E + 1], dt=I32)
    PASSES = (T + CAP - 1) // CAP
    FAR = 1000.0

    def seq_view(a):
        return a.rearrange("p (s t) -> p s t", s=NS)

    with ExitStack() as st:
        ps = st.enter_context(nc.psum_tensor("ps_rt", [P, 8, 512], F32))
        h2T = sb("h2T", [P, NC, T], st)
        sq = sb("sq_r", [P, 2, T], st)
        rstd = sb("rstd_r", [P, T], st)
        gw = sb("gw_r", [P, NC, NSEQ], st)
        wr = sb("wr", [P, NC, E], st)
        br = sb("br", [P, E], st)
        strict = sb("strict", [P, P], st)
        L = sb("logits", [P, NTILE, E], st)
        m8 = sb("m8", [P, NTILE, 8], st)
        gt = sb("gt", [P, NTILE, E], st)
        eq = sb("eq", [P, NTILE, E], st)
        ceq = sb("ceq", [P, NTILE, E], st)
        need = sb("need", [P, NTILE], st)
        sel = sb("sel", [P, NTILE, E], st)
        wt = sb("wt", [P, NTILE, E], st)
        rank = sb("rank", [P, NTILE, E], st)
        zero = sb("zero32", [P, E], st)
        cmax = sb("cmax", [P, 1], st)
        whole = sb("whole", [P, 2, D], st)
        ld, h_s, hr_t, hr_s, lg_t, arg_s, exp_s, sel_s, rank_t, pk, rows_d, row_s, bias_s = (
            sem("rt_" + x) for x in ("ld", "h_s", "hr_t", "hr_s", "lg_t", "arg_s", "exp_s", "sel_s", "rank_t", "pk",
                                     "rows_d", "row_s", "bias_s"))
        sq_s, sum_t, mean_s, log_s, rs_s = norm
        block = st.enter_context(nc.Block())

        @block.gpsimd
        def _(pool):
            nc.gpsimd.iota(iota[:], pattern=[[1, CAP]], base=0, channel_multiplier=0,
                           allow_small_or_imprecise_dtypes=True).then_inc(pk, 1)
            nc.gpsimd.tensor_tensor(strict[:], causal[:], ident[:], ALU.subtract).then_inc(pk, 1)
            nc.gpsimd.memset(yacc[:], 0.0).then_inc(pk, 1)
            nc.gpsimd.memset(route[:], FAR).then_inc(pk, 1)
            nc.gpsimd.memset(expert_row[:], 0.0).then_inc(row_s, 1)
            for q in range(P // E):
                pool.wait_ge(row_s, q + 1)
                nc.gpsimd.affine_select(out=expert_row[:], in_=expert_row[:], compare_op=ALU.not_equal, fill=1.0,
                                        base=-E * q, pattern=[[-1, E]], channel_multiplier=1).then_inc(row_s, 1)

        @block.scalar
        def _(act):
            act.dma_start(wr[:], t["w_router"][0].rearrange("(c p) e -> p c e", p=P)).then_inc(ld, 16)
            act.dma_start(br[:], t["b_router"].to_broadcast([P, E])).then_inc(ld, 16)
            for q, (name, m) in enumerate((("b_gate", 0), ("b_gate", 0), ("b_up", 0), ("b_up", 0), ("b_down", 1), ("b_down", 1))):
                act.dma_start(whole[E * (q % 4):E * (q % 4) + E, m, :], t[name][0]).then_inc(rows_d, 16)
            for c in range(NC):
                if c >= 2:
                    act.wait_ge(sum_t, 1 * NC + c - 1)
                nc.scalar.activation(sq[:, c % 2, :], x2T[:, c, :], ACT.Square).then_inc(sq_s, 1)
            act.wait_ge(mean_s, 2)
            nc.scalar.activation(rstd[:], rstd[:], ACT.Ln).then_inc(log_s, 1)
            act.wait_ge(log_s, 2)
            nc.scalar.activation(rstd[:], rstd[:], ACT.Exp, scale=-0.5).then_inc(rs_s, 1)
            act.wait_ge(rows_d, 96)
            nc.scalar.activation(brow[:, 0, :].bitcast(F32R), whole[:, 0, :], ACT.Copy)
            nc.scalar.activation(brow[0:2 * E, 1, :].bitcast(F32R), whole[0:2 * E, 1, :], ACT.Copy).then_inc(bias_s, 1)
            act.wait_ge(arg_s, 1)
            nc.scalar.activation(wt[:], wt[:], ACT.Exp).then_inc(exp_s, 1)
            for tau, (t0, n) in enumerate(TILE):
                act.wait_ge(hr_t, tau + 1)
                nc.scalar.activation(h2tok[0:n, tau, :].rearrange("p (a b) -> p a b", a=2),
                                     ps[0:n, 2 * tau:2 * tau + 2, :], ACT.Copy).then_inc(hr_s, 1)

        @block.tensor
        def _(pe):
            for c in range(NC):
                pe.wait_ge(sq_s, 1 * NC + c + 1)
                nc.tensor.matmul(ps[:, 7, 0:T], ones[:], sq[:, c % 2, :], start=c == 0, stop=c == NC - 1).then_inc(sum_t, 1)
            pe.wait_ge(h_s, 1)
            pe.wait_ge(ld, 32)
            for tau, (t0, n) in enumerate(TILE):
                for k in range(NC):
                    last = nc.tensor.matmul(ps[0:n, 6, E * tau:E * tau + E], h2T[:, k, t0:t0 + n], wr[:, k, :],
                                            start=k == 0, stop=k == NC - 1)
            last.then_inc(lg_t, 1)
            def to_rows(tau):
                t0, n = TILE[tau]
                for k in range(NC):
                    last = nc.tensor.transpose(ps[0:n, 2 * tau + k // 4, P * (k % 4):P * (k % 4) + P], h2T[:, k, t0:t0 + n],
                                               ident[:])
                last.then_inc(hr_t, 1)

            to_rows(0)
            pe.wait_ge(pk, 4)
            pe.wait_ge(sel_s, 1)
            for tau, (t0, n) in enumerate(TILE):
                o = ps[0:n, 7, E * tau:E * tau + E]
                for u in range(tau):
                    nc.tensor.matmul(o, ones[:, 0:n], sel[:, u, :], start=u == 0, stop=False)
                nc.tensor.matmul(o, strict[0:n, 0:n], sel[0:n, tau, :], start=tau == 0, stop=True)
            for tau, (t0, n) in enumerate(TILE):
                last = nc.tensor.matmul(ps[:, 7, 3 * E:4 * E], ones[0:n, :], sel[0:n, tau, :], start=tau == 0, stop=tau == 2)
            last.then_inc(rank_t, 1)
            to_rows(1)
            to_rows(2)

        @block.vector
        def _(dve):
            def link(ins):
                order.link(dve, ins)

            def over_e(a):
                return a.unsqueeze(2).to_broadcast([P, NTILE, E])

            link(nc.vector.tensor_scalar(gw[:], SC2, 1.0, None, ALU.add))
            link(nc.vector.tensor_tensor(gw[:], gw[:], n2w.unsqueeze(2).to_broadcast([P, NC, NSEQ]), ALU.mult))
            link(nc.vector.memset(L[:], 0.0))
            link(nc.vector.memset(zero[:], 0.0))
            link(nc.vector.memset(rank[:], 0.0))
            dve.wait_ge(sum_t, 2 * NC)
            nc.vector.tensor_scalar(rstd[:], ps[:, 7, 0:T], 1.0 / D, EPS, ALU.mult, ALU.add).then_inc(mean_s, 1)
            dve.wait_ge(rs_s, 2)
            link(nc.vector.tensor_tensor(h2T[:], x2T[:], rstd[:].unsqueeze(1).to_broadcast([P, NC, T]), ALU.mult))
            samples = h2T[:, :, SEQ:T].rearrange("p c (s t) -> p c s t", s=NS)
            link(nc.vector.tensor_tensor(samples, samples, gw[:, :, 1:NSEQ].unsqueeze(3).to_broadcast([P, NC, NS, ST]), ALU.mult))
            nc.vector.tensor_tensor(samples, samples, SH2[:, :, 1:NSEQ].unsqueeze(3).to_broadcast([P, NC, NS, ST]), ALU.add)
            for c in range(NC):
                ins = nc.vector.tensor_scalar(h2T[:, c, 0:SEQ], h2T[:, c, 0:SEQ], gw[:, c, 0:1], SH2[:, c, 0:1], ALU.mult, ALU.add)
            ins.then_inc(h_s, 1)
            dve.wait_ge(bias_s, 1)
            for r0, m in ((E, 0), (3 * E, 0), (E, 1)):
                rows = slice(r0, r0 + E)
                nc.vector.tensor_tensor(brow[rows, m, :].bitcast(F32R), whole[rows, m, :], brow[rows, m, :], ALU.subtract)
            dve.wait_ge(lg_t, 1)
            dve.wait_ge(ld, 32)
            for tau, (t0, n) in enumerate(TILE):
                ins = nc.vector.tensor_tensor(L[0:n, tau, :], ps[0:n, 6, E * tau:E * tau + E], br[0:n, :], ALU.add)
            link(ins)
            for tau in range(NTILE):
                ins = nc.vector.max(m8[:, tau, :], L[:, tau, :])
            link(ins)
            nc.vector.tensor_tensor(wt[:], L[:], over_e(m8[:, :, 0]), ALU.subtract).then_inc(arg_s, 1)
            nc.vector.tensor_tensor(gt[:], L[:], over_e(m8[:, :, TOPK - 1]), ALU.is_gt)
            link(nc.vector.tensor_tensor(eq[:], L[:], over_e(m8[:, :, TOPK - 1]), ALU.is_equal))
            nc.vector.tensor_reduce(need[:], gt[:], AX.X, ALU.add)
            for tau in range(NTILE):
                ins = nc.vector.tensor_tensor_scan(ceq[:, tau, :], eq[:, tau, :], zero[:], 0.0, ALU.add, ALU.add)
            link(ins)
            link(nc.vector.tensor_scalar(need[:], need[:], -1.0, float(TOPK), ALU.mult, ALU.add))
            link(nc.vector.tensor_tensor(ceq[:], ceq[:], over_e(need[:]), ALU.is_le))
            link(nc.vector.tensor_tensor(eq[:], eq[:], ceq[:], ALU.mult))
            nc.vector.tensor_tensor(sel[:], gt[:], eq[:], ALU.add).then_inc(sel_s, 1)
            dve.wait_ge(sel_s, 1)
            dve.wait_ge(exp_s, 1)
            link(nc.vector.tensor_tensor(wt[:], wt[:], sel[:], ALU.mult))
            link(nc.vector.tensor_reduce(need[:], wt[:], AX.X, ALU.add))
            link(nc.vector.reciprocal(need[:], need[:]))
            dve.wait_ge(pk, 4)
            for tau in range(NTILE):
                nc.vector.tensor_scalar(route[:, 0:E, 1, tau], wt[:, tau, :], need[:, tau:tau + 1], None, ALU.mult)
            dve.wait_ge(rank_t, 1)
            for tau, (t0, n) in enumerate(TILE):
                ins = nc.vector.tensor_scalar(rank[0:n, tau, :], ps[0:n, 7, E * tau:E * tau + E], -FAR, None, ALU.add)
            link(ins)
            link(nc.vector.tensor_tensor(rank[:], rank[:], sel[:], ALU.mult))
            for tau in range(NTILE):
                nc.vector.tensor_scalar(route[:, 0:E, 0, tau], rank[:, tau, :], FAR, None, ALU.add)
            nc.vector.tensor_copy(count[:, 0:E], ps[:, 7, 3 * E:4 * E])
            link(nc.vector.tensor_reduce(cmax[:], ps[:, 7, 3 * E:4 * E], AX.X, ALU.max))
            link(nc.vector.tensor_copy(count[:, E:E + 1], cmax[:]))

    with ExitStack() as st:
        ps = st.enter_context(nc.psum_tensor("ps_moe", [P, 8, 512], F32))
        high = sb("high", [P, SPLIT, QUART, HALF], st)
        low = sb("low", [P, SPLIT, QUART, HALF], st)
        xh = sb("xh", [P, NC, CAP], st)
        xl = sb("xl", [P, NC, CAP], st)
        hh = sb("hh", [P, NC, CAP], st)
        hl = sb("hl", [P, NC, CAP], st)
        raw = sb("raw_gu", [P, D], st)
        gate, sig, hid, yrow = (ring[:, RING1 - 1, 2 * n:2 * n + 2, :].rearrange("p a n -> p (a n)") for n in range(4))
        fold = sb("fold", [P, P], st)
        pair = sb("pair", [P, CAP // 2], st)
        slots = sb("slots", [P, CAP], st)
        pick = sb("pick", [P, NTILE, CAP], st)
        wpick = sb("wpick", [P, NTILE, CAP], st)
        put = sb("put", [P, T], st)
        chosen = sb("chosen", [P, P], st)
        cur = sb("cur", [P, 2, NTILE], st)
        nxt = sb("nxt", [P, NTILE], st)
        (pick_s, wpick_s, gath_t, xh_s, x_s, high_s, low_s, piece_t, gate_s, sig_s, hid_s, raw_s, fold_t, hh_s, hl_s, yrow_s,
         put_t, put_s, comb_t, comb_s, vector_step, chosen_s, clip_s) = (sem("ex_" + x) for x in (
             "pick_s", "wpick_s", "gath_t", "xh_s", "x_s", "high_s", "low_s", "piece_t", "gate_s", "sig_s", "hid_s",
             "raw_s", "fold_t", "hh_s", "hl_s", "yrow_s", "put_t", "put_s", "comb_t", "comb_s", "vector_step", "chosen_s", "clip_s"))


        def r(a):
            return a.bitcast(F32R)

        def run_pass(eng, b, body):
            body(b * E, 0, b, True)
            with eng.Fori(1, E) as e:
                body(b * E + e, e, b, False)

        def over_passes(eng, body, prologue, epilogue):
            prologue(0)
            run_pass(eng, 0, body)
            epilogue(0)
            most = eng.value_load(count[0:1, E:E + 1], min_val=0, max_val=T)
            for b in range(1, PASSES):
                with eng.If(most > CAP * b):
                    prologue(b)
                    run_pass(eng, b, body)
                    epilogue(b)

        block = st.enter_context(nc.Block())

        @block.sync
        def _(sp):
            def body(i, e, b, first):
                for p in range(RAW if first and b == 0 else 0, PIECES):
                    sp.wait_ge(low_s, PIECES * i + p - RAW + 1)
                    load_piece(sp, e, p)

            over_passes(sp, body, lambda b: None, lambda b: None)

        @block.scalar
        def _(act):
            def body(i, e, b, first):
                start = first and b == 0

                def round_piece(p):
                    act.wait_ge(raw_full[p % RAW], 16 * (PIECES // RAW * i + p // RAW + 1))
                    if not start or p >= SPLIT:
                        act.wait_ge(piece_t, PIECES * i + p + 1 - SPLIT)
                    nc.scalar.activation(r(high[:, p % SPLIT]), raw_piece(ring, p), ACT.Copy).then_inc(high_s, 1)

                if start:
                    for p in range(3):
                        round_piece(p)
                act.wait_ge(gath_t, i + b + 1)
                if not start:
                    act.wait_ge(piece_t, PIECES * (i - 1) + 8)
                nc.scalar.activation(r(xh[:]).rearrange("p (a c) n -> p a (c n)", a=2), ps[:, 0:2, :], ACT.Copy).then_inc(xh_s, 1)

                def rows_out(m, a):
                    act.wait_ge(piece_t, PIECES * i + 4 * m + 2 * a + 2)
                    if m or not start:
                        act.wait_ge(fold_t, 4 * i + 2 * m + a - 1)
                    nc.scalar.activation(raw[:, HALF * a:HALF * a + HALF], ps[:, 2 * m + a, :], ACT.Copy).then_inc(raw_s, 1)

                if not start:
                    for p in range(3):
                        round_piece(p)
                if not first:
                    take_rows(i - 1)
                for p in range(3, 6):
                    round_piece(p)
                rows_out(0, 0)
                for p in range(6, 8):
                    round_piece(p)
                rows_out(0, 1)
                for p in range(8, 10):
                    round_piece(p)
                rows_out(1, 0)
                for a in range(2):
                    act.wait_ge(gate_s, 2 * i + a + 1)
                    half = slice(HALF * a, HALF * a + HALF)
                    nc.scalar.activation(sig[:, half], gate[:, half], ACT.Sigmoid, scale=ALPHA).then_inc(sig_s, 1)
                for p in range(10, 12):
                    round_piece(p)
                rows_out(1, 1)
                for a in range(2):
                    act.wait_ge(hid_s, 2 * i + a + 1)
                    nc.scalar.activation(r(hh[:, 4 * a:4 * a + 4, :]).rearrange("p c n -> p (c n)"),
                                         hid[:, HALF * a:HALF * a + HALF], ACT.Copy).then_inc(hh_s, 1)

            def take_rows(i):
                act.wait_ge(piece_t, PIECES * i + PIECES)
                nc.scalar.activation(yrow.rearrange("p (a n) -> p a n", a=2), ps[:, 4:6, :], ACT.Copy).then_inc(yrow_s, 1)
                act.wait_ge(put_t, i + 1)
                nc.scalar.activation(put[:], ps[:, 2, 0:T], ACT.Copy).then_inc(put_s, 1)

            over_passes(act, body, lambda b: None, lambda b: take_rows(b * E + E - 1))

        @block.tensor
        def _(pe):
            def gather(i):
                pe.wait_ge(pick_s, i + 1)
                for c in range(NC):
                    for tau, (t0, n) in enumerate(TILE):
                        last = nc.tensor.matmul(ps[:, c // 4, CAP * (c % 4):CAP * (c % 4) + CAP],
                                                h2tok[0:n, tau, P * c:P * c + P], pick[0:n, tau, :],
                                                start=tau == 0, stop=tau == NTILE - 1)
                last.then_inc(gath_t, 1)

            def half(i, j, bank, high_x, low_x, wide):
                m, a = j // 2, j % 2
                rows = slice(64, 128) if m == 1 else slice(0, 64)
                for q in range(2):
                    pe.wait_ge(low_s, PIECES * i + 2 * j + q + 1)
                    hb, lb = high[:, (2 * j + q) % SPLIT], low[:, (2 * j + q) % SPLIT]
                    for k in range(QUART):
                        c = QUART * q + k
                        nc.tensor.matmul(ps[:, bank, :], r(high_x[:, c, :]), r(hb[:, k, :]), start=c == 0, stop=False)
                        if wide:
                            nc.tensor.matmul(ps[:, bank, :], r(low_x[:, c, :]), r(hb[:, k, :]), start=False, stop=False)
                        last = nc.tensor.matmul(ps[:, bank, :], r(high_x[:, c, :]), r(lb[:, k, :]), start=False, stop=False)
                    if q == 1:
                        if j == 0:
                            pe.wait_ge(chosen_s, i + 1)
                        last = nc.tensor.matmul(ps[:, bank, :], r(chosen[rows, :]),
                                                r(brow[rows, m // 2, HALF * a:HALF * a + HALF]), start=False, stop=True)
                    last.then_inc(piece_t, 1)

            def halves(n_tok, b, *args):
                with pe.If(n_tok > CAP * b + CAP // 2):
                    half(*args, True)
                with pe.Else():
                    half(*args, False)

            def fold_half(i, m, a):
                pe.wait_ge(raw_s, 4 * i + 2 * m + a + 1)
                for c in range(4):
                    last = nc.tensor.matmul(ps[:, 2 * m + a, P * c:P * c + P],
                                            raw[:, HALF * a + P * c:HALF * a + P * c + P], fold[:], start=True, stop=True)
                last.then_inc(fold_t, 1)

            def scatter_matrix(i):
                pe.wait_ge(wpick_s, i + 1)
                for tau, (t0, n) in enumerate(TILE):
                    last = nc.tensor.transpose(ps[:, 2, t0:t0 + n], wpick[0:n, tau, :], ident[0:n, 0:n])
                last.then_inc(put_t, 1)

            def combine(i, a):
                pe.wait_ge(yrow_s, i + 1)
                pe.wait_ge(put_s, i + 1)
                for c in range(4 * a, 4 * a + 4):
                    if c >= 4:
                        pe.wait_ge(comb_s, NC * i + c - 3)
                    nc.tensor.matmul(ps[:, 4 + c % 4, 0:T], yrow[:, P * c:P * c + P], put[:], start=True,
                                     stop=True).then_inc(comb_t, 1)

            def body(i, e, b, first):
                start = first and b == 0
                n_tok = pe.value_load(count[0:1, bass.ds(e, 1)], min_val=0, max_val=T)
                pe.wait_ge(x_s, i + 1)
                if not first:
                    scatter_matrix(i - 1)
                halves(n_tok, b, i, 0, 0, xh, xl)
                halves(n_tok, b, i, 1, 1, xh, xl)
                if not first:
                    pe.wait_ge(put_s, i)
                halves(n_tok, b, i, 2, 2, xh, xl)
                fold_half(i, 0, 0)
                fold_half(i, 0, 1)
                if not first:
                    combine(i - 1, 0)
                fold_half(i, 1, 0)
                halves(n_tok, b, i, 3, 3, xh, xl)
                if not first:
                    combine(i - 1, 1)
                fold_half(i, 1, 1)
                pe.wait_ge(gate_s, 2 * i + 2)
                gather(i + b + 1)
                if not first:
                    pe.wait_ge(comb_s, NC * i)
                pe.wait_ge(hl_s, 2 * i + 2)
                halves(n_tok, b, i, 4, 4, hh, hl)
                halves(n_tok, b, i, 5, 5, hh, hl)

            def prologue(b):
                gather(b * (E + 1))

            def epilogue(b):
                scatter_matrix(b * E + E - 1)
                combine(b * E + E - 1, 0)
                combine(b * E + E - 1, 1)

            over_passes(pe, body, prologue, epilogue)

        @block.vector
        def _(dve):
            def picks(i, e, b, link_no):
                if not isinstance(i, int) or i > 0:
                    dve.wait_ge(gath_t, i)
                nc.vector.tensor_scalar(nxt[:], route[:, e, 0, :], float(-CAP * b), None, ALU.add).then_inc(vector_step, 1)
                dve.wait_ge(vector_step, link_no)
                for tau in range(NTILE):
                    ins = nc.vector.tensor_scalar(pick[:, tau, :], iota[:], nxt[:, tau:tau + 1], None, ALU.is_equal)
                ins.then_inc(pick_s, 1)

            def add_up(i, a):
                for c in range(4 * a, 4 * a + 4):
                    dve.wait_ge(comb_t, NC * i + c + 1)
                    nc.vector.tensor_tensor(yacc[:, c, :], yacc[:, c, :], ps[:, 4 + c % 4, 0:T], ALU.add).then_inc(comb_s, 1)

            def body(i, e, b, first):
                n_tok = dve.value_load(count[0:1, bass.ds(e, 1)], min_val=0, max_val=T)
                with dve.If(n_tok > CAP * b + CAP // 2):
                    steps(i, e, b, first, True)
                with dve.Else():
                    steps(i, e, b, first, False)

            def steps(i, e, b, first, wide):
                start = first and b == 0
                chain = b + 1 + LINKS * i
                mid = CAP // 2
                w = CAP if wide else mid
                row = expert_row[:, bass.ds(e, 1)]

                banks = ps[:].rearrange("p a n -> p (a n)")

                def half(buffer, a):
                    return buffer[:, HALF * a:HALF * a + HALF].rearrange("p (c n) -> p c n", n=CAP)[:, :, 0:w]

                def left(p):
                    dve.wait_ge(high_s, PIECES * i + p + 1)
                    nc.vector.tensor_tensor(r(low[:, p % SPLIT]), raw_piece(ring, p), high[:, p % SPLIT], ALU.subtract).then_inc(low_s, 1)

                def split(high_part, low_part, src, semaphore):
                    dst = low_part if wide else high_part[:, :, mid:CAP]
                    nc.vector.tensor_tensor(r(dst), src, high_part[:, :, 0:w], ALU.subtract).then_inc(semaphore, 1)

                if start:
                    for p in range(3):
                        left(p)
                dve.wait_ge(xh_s, i + 1)
                split(xh[:], xl[:], ps[:, 0:2, :].rearrange("p a (c n) -> p (a c) n", n=CAP)[:, :, 0:w], x_s)
                if not start:
                    for p in range(3):
                        left(p)
                    dve.wait_ge(piece_t, PIECES * i)
                if wide:
                    nc.vector.tensor_copy(fold[:], ident[:])
                    nc.vector.tensor_scalar(r(chosen[:]), ones[:], row, None, ALU.mult).then_inc(chosen_s, 1)
                else:
                    nc.vector.tensor_copy(fold[:, 0:mid], pair[:])
                    nc.vector.tensor_scalar(r(chosen[:, 0:mid]), ones[:, 0:mid], row, None, ALU.mult)
                    nc.vector.tensor_scalar(r(chosen[:, mid:P]), ones[:, mid:P], 0.0, None, ALU.mult).then_inc(chosen_s, 1)
                for p in range(3, 8):
                    left(p)
                picks(i + b + 1, e + 1, b, chain + 1)
                left(8)
                for a in range(2):
                    dve.wait_ge(fold_t, 4 * i + a + 1)
                    nc.vector.tensor_scalar(half(gate, a), half(banks, a), LIMIT, None, ALU.min).then_inc(gate_s, 1)
                for a in range(2):
                    dve.wait_ge(sig_s, 2 * i + a + 1)
                    nc.vector.tensor_tensor(half(gate, a), half(gate, a), half(sig, a), ALU.mult).then_inc(vector_step, 1)
                    dve.wait_ge(fold_t, 4 * i + 2 + a + 1)
                    nc.vector.tensor_scalar(half(hid, a), half(banks, 2 + a), LIMIT, -LIMIT, ALU.min, ALU.max).then_inc(clip_s, 1)
                    dve.wait_ge(vector_step, chain + 2 + a)
                    dve.wait_ge(clip_s, 2 * i + a + 1)
                    nc.vector.scalar_tensor_tensor(out=half(hid, a), in0=half(hid, a), scalar=1.0, in1=half(gate, a),
                                                   op0=ALU.add, op1=ALU.mult).then_inc(hid_s, 1)
                    if not first:
                        add_up(i - 1, a)
                    if a == 0:
                        left(9)
                if not start:
                    dve.wait_ge(put_t, i)
                nc.vector.tensor_copy(slots[:, mid:CAP], iota[:, mid:CAP] if wide else iota[:, 0:mid])
                nc.vector.tensor_scalar(cur[:, 1, :], route[:, e, 1, :], 1.0, None, ALU.mult)
                nc.vector.tensor_scalar(cur[:, 0, :], route[:, e, 0, :], float(-CAP * b), None, ALU.add).then_inc(vector_step, 1)
                for a in range(2):
                    dve.wait_ge(hh_s, 2 * i + a + 1)
                    split(hh[:, 4 * a:4 * a + 4, :], hl[:, 4 * a:4 * a + 4, :], half(hid, a), hl_s)
                dve.wait_ge(vector_step, chain + 4)
                for p in range(10, 12):
                    left(p)
                for tau in range(NTILE):
                    ins = nc.vector.tensor_scalar(wpick[:, tau, :], slots[:], cur[:, 0, tau:tau + 1], cur[:, 1, tau:tau + 1],
                                                  ALU.is_equal, ALU.mult)
                ins.then_inc(wpick_s, 1)

            def last_sums(b):
                for a in range(2):
                    add_up(b * E + E - 1, a)

            nc.vector.tensor_copy(pair[0:CAP // 2, :], ident[0:CAP // 2, 0:CAP // 2])
            order.link(dve, nc.vector.tensor_copy(pair[CAP // 2:CAP, :], ident[CAP // 2:CAP, CAP // 2:CAP]))
            order.link(dve, nc.vector.tensor_copy(fold[:], ident[:]))
            nc.vector.tensor_copy(slots[:], iota[:])
            over_passes(dve, body, lambda b: picks(b * (E + 1), 0, b, b + LINKS * b * E + 1), last_sums)

    with ExitStack() as st:
        ps = st.enter_context(nc.psum_tensor("ps_fin", [P, 8, 512], F32))
        sq = sb("sq_f", [P, 2, T], st)
        rstd = sb("rstd_f", [P, T], st)
        yrows = sb("yrows", [P, NTILE, D], st)
        x_s, y_s, yt_t, yo_s, out_d = (sem("fn_" + x) for x in ("x_s", "y_s", "yt_t", "yo_s", "out_d"))
        sq_s, sum_t, mean_s, log_s, rs_s = norm
        block = st.enter_context(nc.Block())

        @block.vector
        def _(dve):
            samples = yacc[:, :, SEQ:T].rearrange("p c (s t) -> p c s t", s=NS)
            order.link(dve, nc.vector.tensor_tensor(samples, samples, G2[:, :, 1:NSEQ].unsqueeze(3).to_broadcast([P, NC, NS, ST]),
                                                    ALU.mult))
            nc.vector.tensor_tensor(x2T[:, :, SEQ:T], x2T[:, :, SEQ:T], yacc[:, :, SEQ:T], ALU.add)
            for c in range(NC):
                nc.vector.scalar_tensor_tensor(out=x2T[:, c, 0:SEQ], in0=yacc[:, c, 0:SEQ], scalar=G2[:, c, 0:1],
                                               in1=x2T[:, c, 0:SEQ], op0=ALU.mult, op1=ALU.add).then_inc(x_s, 1)
            dve.wait_ge(sum_t, 3 * NC)
            nc.vector.tensor_scalar(rstd[:], ps[:, 7, 0:T], 1.0 / D, EPS, ALU.mult, ALU.add).then_inc(mean_s, 1)
            dve.wait_ge(rs_s, 3)
            for c in range(NC):
                nc.vector.scalar_tensor_tensor(out=x2T[:, c, :], in0=x2T[:, c, :], scalar=nfw[:, c:c + 1], in1=rstd[:],
                                               op0=ALU.mult, op1=ALU.mult).then_inc(y_s, 1)

        @block.scalar
        def _(act):
            for c in range(NC):
                act.wait_ge(x_s, c + 1)
                if c >= 2:
                    act.wait_ge(sum_t, 2 * NC + c - 1)
                nc.scalar.activation(sq[:, c % 2, :], x2T[:, c, :], ACT.Square).then_inc(sq_s, 1)
            act.wait_ge(mean_s, 3)
            nc.scalar.activation(rstd[:], rstd[:], ACT.Ln).then_inc(log_s, 1)
            act.wait_ge(log_s, 3)
            nc.scalar.activation(rstd[:], rstd[:], ACT.Exp, scale=-0.5).then_inc(rs_s, 1)
            for tau, (t0, n) in enumerate(TILE):
                act.wait_ge(yt_t, tau + 1)
                nc.scalar.activation(yrows[0:n, tau, :].rearrange("p (a b) -> p a b", a=2), ps[0:n, 2 * tau:2 * tau + 2, :],
                                     ACT.Copy).then_inc(yo_s, 1)

        @block.tensor
        def _(pe):
            for c in range(NC):
                pe.wait_ge(sq_s, 2 * NC + c + 1)
                nc.tensor.matmul(ps[:, 7, 0:T], ones[:], sq[:, c % 2, :], start=c == 0, stop=c == NC - 1).then_inc(sum_t, 1)
            for tau, (t0, n) in enumerate(TILE):
                for k in range(NC):
                    if tau == 0:
                        pe.wait_ge(y_s, k + 1)
                    last = nc.tensor.transpose(ps[0:n, 2 * tau + k // 4, P * (k % 4):P * (k % 4) + P], x2T[:, k, t0:t0 + n],
                                               ident[:])
                last.then_inc(yt_t, 1)

        @block.sync
        def _(sp):
            for tau in range(2):
                sp.wait_ge(yo_s, tau + 1)
                sp.dma_start(t["y_prompt"][0, P * tau:P * tau + P, :], yrows[:, tau, :]).then_inc(out_d, 16)
            sp.wait_ge(yo_s, 3)
            sp.dma_start(t["y_sample"].rearrange("s t d -> (s t) d"), yrows[0:64, 2, :]).then_inc(out_d, 16)
            sp.wait_ge(out_d, 48)


def raw_piece(ring, p):
    s = p % RAW
    return ring[:, s // 2, QUART * (s % 2):QUART * (s % 2) + QUART, :]


INS = ["x_prompt", "x_sample", "c_prompt", "c_sample", "state_gdn_conv", "state_gdn_rec", "state_sc_conv", "w_ada",
       "b_ada", "norm1_w", "w_in", "gdn_conv_w", "gdn_a_log", "gdn_dt_bias", "gdn_norm_w", "w_branch_a", "sc_conv_w",
       "w_branch_b", "w_out", "norm2_w", "w_router", "b_router", "w_gate", "b_gate", "w_up", "b_up", "w_down",
       "b_down", "final_norm_w"]
OUTS = [("y_prompt", (1, SEQ, D)), ("y_sample", (NS, ST, D)), ("conv_prompt", (1, 1, 3, QKV)),
        ("rec_prompt", (1, 1, H, P, P)), ("sc_prompt", (1, 1, 2, D)), ("conv_sample", (1, NS, 3, QKV)),
        ("rec_sample", (1, NS, H, P, P)), ("sc_sample", (1, NS, 2, D))]


def kernel(**inputs):
    import numpy as np
    import concourse.bacc as bacc
    from concourse.bass_utils import run_bass_kernel_spmd

    nc = bacc.Bacc("TRN2", target_bir_lowering=False, num_devices=1)
    arrays, t = {}, {}
    for name in INS:
        arrays["in_" + name] = np.ascontiguousarray(inputs[name])
        t[name] = nc.dram_tensor("in_" + name, arrays["in_" + name].shape, F32, kind="ExternalInput").ap()
    for name, shape in OUTS:
        t[name] = nc.dram_tensor("out_" + name, shape, F32, kind="ExternalOutput").ap()
    build(nc, t)
    r = run_bass_kernel_spmd(nc, [arrays], core_ids=[0])
    return tuple(r.results[0]["out_" + name] for name, _ in OUTS)
```
